# Optimizing a Trainium2 kernel written in Bass

```python
import jax, jax.numpy as jnp
from jax import lax
import numpy as np

D_MODEL = 1024
BATCH = 1
SEQ = 512
DEPTH = 1

CHUNK = 64
EPS = 1e-6
ROPE_THETA = 10000.0
N_BRANCH = 3
D_BRANCH = 1024
MLSTM_HEADS = 4
MLSTM_HD = 256
D_MLSTM = MLSTM_HEADS * MLSTM_HD
CONV_W = 4
MLSTM_F_BIAS = 3.0
DSA_HEADS = 8
DSA_HD = 128
D_DSA = DSA_HEADS * DSA_HD
IDX_HEADS = 8
IDX_HD = 64
DSA_TOPK = 256
Q_BLOCK = 128
N_MEM = 256
MEM_HEADS = 4
MEM_HD = 256
D_MEM = MEM_HEADS * MEM_HD
SPLITS = (2 * D_MLSTM, D_MLSTM, 2 * MLSTM_HEADS, D_MLSTM, D_MLSTM,
          D_DSA, D_DSA, D_DSA, D_DSA, IDX_HEADS * IDX_HD, IDX_HD, IDX_HEADS,
          D_MEM, D_MEM, N_BRANCH * D_MODEL)
D_IN = (2 * D_MLSTM + D_MLSTM + 2 * MLSTM_HEADS + D_MLSTM + D_MLSTM
        + 4 * D_DSA + IDX_HEADS * IDX_HD + IDX_HD + IDX_HEADS
        + 2 * D_MEM + N_BRANCH * D_MODEL)

kernel_name = 'hybrid_mlstm_dsa_memxattn_block'

def rms_norm(x, g):
    x32 = x.astype(jnp.float32)
    y = x32 * lax.rsqrt(jnp.mean(x32 * x32, axis=-1, keepdims=True) + EPS)
    return (y * g.astype(jnp.float32)).astype(x.dtype)

def rotary(x, positions):
    d = x.shape[-1]
    half = d // 2
    inv_freq = jnp.power(ROPE_THETA, -jnp.arange(half, dtype=jnp.float32) / half)
    ang = positions.astype(jnp.float32)[..., None] * inv_freq
    cos = jnp.cos(ang)[:, :, None, :]
    sin = jnp.sin(ang)[:, :, None, :]
    x32 = x.astype(jnp.float32)
    x1, x2 = x32[..., :half], x32[..., half:]
    return jnp.concatenate([x1 * cos - x2 * sin, x2 * cos + x1 * sin], axis=-1).astype(x.dtype)

def causal_conv(u, w, b):
    c = u.shape[-1]
    out = lax.conv_general_dilated(u, w[:, None, :].astype(u.dtype), window_strides=(1,),
                                   padding=[(CONV_W - 1, 0)],
                                   dimension_numbers=('NWC', 'WIO', 'NWC'),
                                   feature_group_count=c)
    return out + b.astype(u.dtype)

def mlstm_scan(q, k, v, i_pre, log_f):
    B, S, H, dh = q.shape
    nc = S // CHUNK
    to_c4 = lambda a: a.reshape(B, nc, CHUNK, H, dh).transpose(1, 0, 3, 2, 4)
    to_c3 = lambda a: a.reshape(B, nc, CHUNK, H).transpose(1, 0, 3, 2)
    tril = jnp.tril(jnp.ones((CHUNK, CHUNK), dtype=bool))

    def step(carry, xs):
        C, n, m = carry
        qc, kc, vc, ic, fc = xs
        b = jnp.cumsum(fc, axis=-1)
        d_log = b[..., :, None] - b[..., None, :] + ic[..., None, :]
        d_log = jnp.where(tril, d_log, -jnp.inf)
        inter = b + m[..., None]
        m_t = jnp.maximum(inter, jnp.max(d_log, axis=-1))
        w_intra = jnp.exp(d_log - m_t[..., None])
        w_inter = jnp.exp(inter - m_t)
        a = jnp.einsum('bhtd,bhsd->bhts', qc, kc) * w_intra
        num = (w_inter[..., None] * jnp.einsum('bhtd,bhde->bhte', qc, C)
               + jnp.einsum('bhts,bhse->bhte', a, vc))
        den = w_inter * jnp.einsum('bhtd,bhd->bht', qc, n) + jnp.sum(a, axis=-1)
        h = num / jnp.maximum(jnp.abs(den), jnp.exp(-m_t))[..., None]
        b_last = b[..., -1]
        g = b_last[..., None] - b + ic
        m_new = jnp.maximum(b_last + m, jnp.max(g, axis=-1))
        decay = jnp.exp(b_last + m - m_new)
        wk = jnp.exp(g - m_new[..., None])
        C = decay[..., None, None] * C + jnp.einsum('bhs,bhsd,bhse->bhde', wk, kc, vc)
        n = decay[..., None] * n + jnp.einsum('bhs,bhsd->bhd', wk, kc)
        return (C, n, m_new), h

    init = (jnp.zeros((B, H, dh, dh), jnp.float32), jnp.zeros((B, H, dh), jnp.float32),
            jnp.zeros((B, H), jnp.float32))
    _, hs = lax.scan(step, init, (to_c4(q), to_c4(k), to_c4(v), to_c3(i_pre), to_c3(log_f)))
    return hs.transpose(1, 0, 3, 2, 4).reshape(B, S, H, dh)

def dsa_attention(q, k, v, qi, ki, wi):
    B, S, H, dh = q.shape
    top_k = min(DSA_TOPK, S // 4)
    nb = S // Q_BLOCK
    blocks = lambda a: a.reshape((B, nb, Q_BLOCK) + a.shape[2:]).swapaxes(0, 1)
    starts = jnp.arange(nb, dtype=jnp.int32) * Q_BLOCK
    key_pos = jnp.arange(S, dtype=jnp.int32)
    gather = jax.vmap(lambda kb, ib: kb[ib])

    def one_block(args):
        qb, qib, wib, t0 = args
        t = t0 + jnp.arange(Q_BLOCK, dtype=jnp.int32)
        visible_end = (t // CHUNK + 1) * CHUNK
        logits = jnp.einsum('bqhd,bsd->bqhs', qib, ki).astype(jnp.float32) * (IDX_HD ** -0.5)
        score = jnp.einsum('bqhs,bqh->bqs', jax.nn.relu(logits), wib.astype(jnp.float32))
        admissible = key_pos[None, :] < visible_end[:, None]
        score = jnp.where(admissible[None], score, -jnp.inf)
        _, idx = lax.top_k(score, top_k)
        valid = idx < visible_end[None, :, None]
        k_sel = gather(k, idx)
        v_sel = gather(v, idx)
        s = jnp.einsum('bqhd,bqkhd->bhqk', qb, k_sel).astype(jnp.float32) * (dh ** -0.5)
        s = jnp.where(valid[:, None], s, -jnp.inf)
        p = jax.nn.softmax(s, axis=-1)
        return jnp.einsum('bhqk,bqkhd->bqhd', p.astype(v.dtype), v_sel)

    out = lax.map(one_block, (blocks(q), blocks(qi), blocks(wi), starts))
    return out.swapaxes(0, 1).reshape(B, S, H, dh)

def memory_attention(q, k, v):
    s = jnp.einsum('bshd,bmhd->bhsm', q, k).astype(jnp.float32) * (q.shape[-1] ** -0.5)
    p = jax.nn.softmax(s, axis=-1)
    return jnp.einsum('bhsm,bmhd->bshd', p.astype(v.dtype), v)

def setup_inputs(seed: int = 0) -> dict:
    key = jax.random.key(seed)
    ks = jax.random.split(key, 18)
    f32 = jnp.float32
    nrm = lambda k, shape, scale: jax.random.normal(k, shape, f32) * scale
    gain = lambda k, shape: 1.0 + 0.02 * jax.random.normal(k, shape, f32)
    x = jax.random.normal(ks[0], (BATCH, SEQ, D_MODEL), f32)
    mem = jax.random.normal(ks[1], (BATCH, N_MEM, D_MODEL), f32)
    offsets = jax.random.randint(ks[2], (BATCH, 1), 0, 1024, dtype=jnp.int32)
    positions = offsets + jnp.arange(SEQ, dtype=jnp.int32)[None, :]
    gate_off = jnp.array([0.0, MLSTM_F_BIAS], f32)[None, :, None]
    return {
        'x': x,
        'mem': mem,
        'positions': positions,
        'norm_g': gain(ks[3], (DEPTH, D_MODEL)),
        'mem_norm_g': gain(ks[4], (DEPTH, D_MODEL)),
        'w_in': nrm(ks[5], (DEPTH, D_MODEL, D_IN), D_MODEL ** -0.5),
        'conv_w': nrm(ks[6], (DEPTH, CONV_W, 2 * D_MLSTM), CONV_W ** -0.5),
        'conv_b': nrm(ks[7], (DEPTH, 2 * D_MLSTM), 0.01),
        'mlstm_gate_b': gate_off + nrm(ks[8], (DEPTH, 2, MLSTM_HEADS), 0.1),
        'mlstm_norm_g': gain(ks[9], (DEPTH, MLSTM_HEADS, MLSTM_HD)),
        'dsa_q_norm_g': gain(ks[10], (DEPTH, DSA_HD)),
        'dsa_k_norm_g': gain(ks[11], (DEPTH, DSA_HD)),
        'mem_q_norm_g': gain(ks[12], (DEPTH, MEM_HD)),
        'mem_k_norm_g': gain(ks[13], (DEPTH, MEM_HD)),
        'w_mem_kv': nrm(ks[14], (DEPTH, D_MODEL, 2 * D_MEM), D_MODEL ** -0.5),
        'w_branch': nrm(ks[15], (DEPTH, N_BRANCH, D_BRANCH, D_MODEL), D_BRANCH ** -0.5),
        'w_out': nrm(ks[16], (DEPTH, D_MODEL, D_MODEL), D_MODEL ** -0.5),
    }

def reference(x, mem, positions, norm_g, mem_norm_g, w_in, conv_w, conv_b, mlstm_gate_b,
              mlstm_norm_g, dsa_q_norm_g, dsa_k_norm_g, mem_q_norm_g, mem_k_norm_g,
              w_mem_kv, w_branch, w_out):
    B, S, _ = x.shape
    dt = x.dtype
    cuts = np.cumsum(np.array(SPLITS))[:-1].tolist()
    for l in range(DEPTH):
        h = rms_norm(x, norm_g[l])
        proj = h @ w_in[l]
        (qk_a, v_a, if_a, o_a, z_a, q_b, k_b, v_b, z_b, qi, ki, wi,
         q_m, z_m, gate) = jnp.split(proj, cuts, axis=-1)

        qk_a = jax.nn.silu(causal_conv(qk_a, conv_w[l], conv_b[l])).astype(jnp.float32)
        qa = qk_a[..., :D_MLSTM].reshape(B, S, MLSTM_HEADS, MLSTM_HD)
        ka = qk_a[..., D_MLSTM:].reshape(B, S, MLSTM_HEADS, MLSTM_HD) * (MLSTM_HD ** -0.5)
        va = v_a.astype(jnp.float32).reshape(B, S, MLSTM_HEADS, MLSTM_HD)
        if_a = if_a.astype(jnp.float32)
        i_pre = if_a[..., :MLSTM_HEADS] + mlstm_gate_b[l, 0].astype(jnp.float32)
        log_f = jax.nn.log_sigmoid(if_a[..., MLSTM_HEADS:] + mlstm_gate_b[l, 1].astype(jnp.float32))
        ha = mlstm_scan(qa, ka, va, i_pre, log_f)
        ha = rms_norm(ha, mlstm_norm_g[l]).reshape(B, S, D_MLSTM).astype(dt)
        y_a = ha * jax.nn.sigmoid(o_a) * jax.nn.silu(z_a)

        qb = rotary(rms_norm(q_b.reshape(B, S, DSA_HEADS, DSA_HD), dsa_q_norm_g[l]), positions)
        kb = rotary(rms_norm(k_b.reshape(B, S, DSA_HEADS, DSA_HD), dsa_k_norm_g[l]), positions)
        vb = v_b.reshape(B, S, DSA_HEADS, DSA_HD)
        qib = rotary(qi.reshape(B, S, IDX_HEADS, IDX_HD), positions)
        kib = rotary(ki.reshape(B, S, 1, IDX_HD), positions)[:, :, 0, :]
        wib = wi * (IDX_HEADS ** -0.5)
        y_b = dsa_attention(qb, kb, vb, qib, kib, wib).reshape(B, S, D_DSA) * jax.nn.silu(z_b)

        mem_h = rms_norm(mem, mem_norm_g[l])
        kv_m = mem_h @ w_mem_kv[l]
        km = rms_norm(kv_m[..., :D_MEM].reshape(B, -1, MEM_HEADS, MEM_HD), mem_k_norm_g[l])
        vm = kv_m[..., D_MEM:].reshape(B, -1, MEM_HEADS, MEM_HD)
        qm = rms_norm(q_m.reshape(B, S, MEM_HEADS, MEM_HD), mem_q_norm_g[l])
        y_m = memory_attention(qm, km, vm).reshape(B, S, D_MEM) * jax.nn.silu(z_m)

        g = jax.nn.sigmoid(gate.astype(jnp.float32)).astype(dt).reshape(B, S, N_BRANCH, D_MODEL)
        merged = (g[:, :, 0] * (y_a @ w_branch[l, 0])
                  + g[:, :, 1] * (y_b @ w_branch[l, 1])
                  + g[:, :, 2] * (y_m @ w_branch[l, 2]))
        x = x + merged @ w_out[l]
    return x


_drawn_inputs = setup_inputs


def setup_inputs(seed=0):
    import zlib

    import numpy as np

    out = dict(_drawn_inputs(seed))
    spreads = {}
    factors = {'norm_g': 6.448,
     'mem_norm_g': 8.0,
     'conv_b': 8.0,
     'mlstm_norm_g': 8.0,
     'dsa_q_norm_g': 8.0,
     'dsa_k_norm_g': 8.0,
     'mem_q_norm_g': 8.0,
     'mem_k_norm_g': 8.0}
    for name, (base, spread) in spreads.items():
        noise = np.random.default_rng([zlib.crc32(name.encode()), seed]).standard_normal(out[name].shape)
        drawn = base * np.exp(spread * noise) if base else spread * noise
        out[name] = __import__('jax').numpy.asarray(drawn.astype(out[name].dtype))
    for name, factor in factors.items():
        out[name] = (out[name] * factor).astype(out[name].dtype)
    return out
```

```python
from contextlib import ExitStack

import numpy as np

import concourse.bass as bass
from concourse import mybir

F32 = mybir.dt.float32
F32R = mybir.dt.float32r
I32 = mybir.dt.int32
ALU = mybir.AluOpType
ACT = mybir.ActivationFunctionType
AX = mybir.AxisListType.X

P = 128
S = 512
D = 1024
TT = S // P
KT = D // P
KH = KT // 2
MEM = 256
MT = MEM // P
CONV = 4
A_HEADS, A_HD = 4, 256
B_HEADS, B_HD = 8, 128
I_HEADS, I_HD = 8, 64
M_HEADS, M_HD = 4, 256
TOPK = 128
EPS = 1e-6
ROPE_THETA = 10000.0

C_QA = 0
C_KA = C_QA + D
C_VA = C_KA + D
C_IF = C_VA + D
C_OA = C_IF + 2 * A_HEADS
C_ZA = C_OA + D
C_QB = C_ZA + D
C_ZB = C_QB + 3 * D
C_QI = C_ZB + D
C_KI = C_QI + I_HEADS * I_HD
C_QM = C_KI + I_HD + I_HEADS
C_ZM = C_QM + D
C_GATE = C_ZM + D

NEG = -1.0e30
TAKEN = -3.0e38
LOWEST = -3.0e38
INV_2PI = float(np.float32(1.0 / (2.0 * np.pi)))
ROUNDER = 1.5 * 2.0 ** 23
TWO_PI_HI = 6.28125
TWO_PI_MID = float(np.float32(np.floor((2 * np.pi - TWO_PI_HI) * 2 ** 20) / 2 ** 20))
TWO_PI_LO = float(np.float32(2 * np.pi - TWO_PI_HI - TWO_PI_MID))
PI_IN = 3.1415925


def off(t):
    return P * t * (t + 1) // 2


def st_off(s):
    return sum(S - P * r for r in range(s))


class Panels:

    def __init__(self):
        self.panel, self.loads, self.uses = 0, 0, [0, 0, 0, 0]

    def take(self, panels, loads, banks):
        start = (self.panel, self.loads, tuple(self.uses))
        self.panel += panels
        self.loads += loads
        self.uses = [u + b for u, b in zip(self.uses, banks)]
        return start


_plan = Panels()
IDX1 = _plan.take(1, 1, (0, 1, 1, 1))
IDX2 = _plan.take(1, 2, (1, 1, 1, 1))
KV = _plan.take(4, 4, (2, 2, 2, 2))
MS = _plan.take(M_HEADS, 2 * M_HEADS, (M_HEADS,) * 4)
BS = _plan.take(2 * B_HEADS, 6 * B_HEADS, (2 * B_HEADS, 2 * B_HEADS, 2 * B_HEADS, B_HEADS))
AS = _plan.take(3 * A_HEADS, 5 * A_HEADS, (3 * A_HEADS,) * 4)
GB = _plan.take(4, 8, (4,) * 4)
GA = _plan.take(4, 8, (4,) * 4)
OUT = _plan.take(2, 2, (2,) * 4)


class Steps:

    def __init__(self, eng, sem):
        self.eng, self.sem, self.n, self.turn, self.base, self.per = eng, sem, 0, None, 0, 0

    def value(self):
        if self.turn is None:
            return self.n
        return self.turn * self.per + (self.base + self.n)

    def then(self, instruction):
        instruction.then_inc(self.sem, 1)
        self.n += 1
        self.eng.wait_ge(self.sem, self.value())

    def enter(self, turn, first, per):
        self.turn, self.per, self.base, self.entered = turn, per, self.n - first * per, self.n
        self.n = 0

    def leave(self, turns):
        assert self.n == self.per, (self.n, self.per)
        self.n = self.entered + turns * self.per
        self.turn = None


def hybrid_block(nc, x, mem, positions, norm_g, mem_norm_g, w_in, conv_w, conv_b, mlstm_gate_b,
                 mlstm_norm_g, dsa_q_norm_g, dsa_k_norm_g, mem_q_norm_g, mem_k_norm_g,
                 w_mem_kv, w_branch, w_out, inv_freq, out):
    ctx = ExitStack()
    with ctx:
        def sb(name, shape, dt=F32):
            return ctx.enter_context(nc.sbuf_tensor(name, shape, dt))

        def sem(name):
            return ctx.enter_context(nc.semaphore(name))

        hT_hi = sb("hT_hi", [P, KT, S], F32R)
        hT_lo = sb("hT_lo", [P, KT, S], F32R)
        w_raw = sb("w_raw", [P, 2, KH, S])
        w_hi = sb("w_hi", [P, 2, KH, S], F32R)
        w_lo = sb("w_lo", [P, 2, KH, S], F32R)
        y_hi = sb("y_hi", [P, KT, S], F32R)
        y_lo = sb("y_lo", [P, KT, S], F32R)
        yF = sb("yF", [P, KT * S])
        merged = sb("merged", [P, KT * S])
        ident = sb("ident", [P, P])
        causal = sb("causal", [P, P])
        pick = sb("pick", [A_HEADS, A_HEADS, P])
        ones = sb("ones", [P, 1])
        minus_half = sb("minus_half", [P, 8])
        cols = sb("cols", [P, 92])
        gqk = sb("gqk", [P, 2])
        negmask = sb("negmask", [P, off(TT)])
        score = sb("score", [P, off(TT)])
        tabs = sb("tabs", [P, 2, TT, 2 * P])
        sig = sb("sig", [P, 2, S])
        arena = sb("arena", [P, 9216])
        maxrow = sig[0:A_HEADS, 1, :]
        small = sb("small", [P, 192])

        x_in = yF[:, :].rearrange("p (t n) -> p t n", t=TT)
        mem_in = merged[:, 0:MT * D].rearrange("p (t n) -> p t n", t=MT)
        g_row = arena[:, 0:D]
        memg_row = arena[:, D:2 * D]
        x_sc = arena[:, 2 * D:4 * D].rearrange("p (b n) -> p b n", b=2)
        junk = arena[:, 4 * D:5 * D]
        vec_rows = arena[0:92, 5 * D:5 * D + P]
        gain_rows = arena[:, 5 * D + P:5 * D + 3 * P]
        memT_hi = y_hi
        memT_lo = y_lo
        Y0 = 0
        qiT = yF[:, 0:4 * 384].rearrange("p (h n) -> p h n", h=4)
        kiT = yF[:, 1536:2048]
        relu = yF[:, 2048:3072].rearrange("p (b n) -> p b n", b=2)
        cos32 = yF[:, 3072:3328].rearrange("p (t n) -> p t n", t=TT)
        sin32 = yF[:, 3328:3584].rearrange("p (t n) -> p t n", t=TT)
        ki_rot = yF[:, 3584:4096].rearrange("p (t n) -> p t n", t=TT)
        ang = arena[:, 6 * D:6 * D + 256]
        turns = arena[:, 6 * D + 256:6 * D + 512]
        cosd = arena[:, 6 * D + 512:6 * D + 768].rearrange("p (t n) -> p t n", t=TT)
        sind = arena[:, 6 * D + 768:7 * D].rearrange("p (t n) -> p t n", t=TT)
        invf = arena[:, 7 * D:7 * D + 64]
        pos_i = small[:, 0:4].bitcast(I32)
        pos_f = small[:, 4:8]
        qi_rot = arena[:, 4 * D:4 * D + 1536].rearrange("p (t n) -> p t n", t=3)
        qi_b = arena[:, 8 * D:8 * D + 512]
        km_raw = merged[:, 2048:4096]
        km_sq = arena[:, 4096:6144]
        rows = merged[0:A_HEADS, 0:2048].rearrange("p (r n) -> p r n", r=4)
        kmT = arena[:, 0:2048].rearrange("p (h n) -> p h n", h=M_HEADS)
        vm = arena[:, 2048:4096].rearrange("p (m n) -> p m n", m=MT)
        m_qT = arena[:, 4096:5120].rearrange("p (e n) -> p e n", e=2)
        m_sq = arena[:, 5120:6144].rearrange("p (e n) -> p e n", e=2)
        m_p = m_sq[:, :, :].rearrange("p e n -> p (e n)").rearrange("p (t n) -> p t n", t=TT)
        m_pT = arena[:, 6144:7168].rearrange("p (t n) -> p t n", t=TT)
        m_on = arena[:, 7168:8192].rearrange("p (t n) -> p t n", t=TT)
        m_zs = arena[:, 8192:9216].rearrange("p (e n) -> p e n", e=2)
        b_raw = arena[:, 0:1536].rearrange("p (t n) -> p t n", t=TT)
        b_rc = arena[:, 4096:5120]
        b_rs = arena[:, 2048:3072]
        b_qT = arena[:, 3072:3584]
        b_kT = arena[:, 3584:4096]
        b_pT = arena[:, 5120:6400]
        b_on = arena[:, 6400:6912].rearrange("p (t n) -> p t n", t=TT)
        b_zs = arena[:, 8192:8704]
        b_sq = arena[:, 7168:8192]
        a_qT = tabs[:, 0, :, :].rearrange("p t n -> p (t n)").rearrange("p (e n) -> p e n", e=2)
        a_kT = tabs[:, 1, :, :].rearrange("p t n -> p (t n)").rearrange("p (e n) -> p e n", e=2)
        a_conv = negmask[:, 0:1024].rearrange("p (b n) -> p b n", b=2)
        a_v = arena[:, 0:TT * (A_HD + 1)].rearrange("p (t n) -> p t n", t=TT)
        a_w = arena[:, 1028:2308]
        a_at = arena[:, 2308:3588]
        a_md = arena[:, 3588:4100].rearrange("p (t n) -> p t n", t=TT)
        a_hn = arena[:, 4100:5124].rearrange("p (t n) -> p t n", t=TT)
        a_o = arena[:, 5124:6148].rearrange("p (e n) -> p e n", e=2)
        a_oz = arena[:, 6148:7172].rearrange("p (e n) -> p e n", e=2)
        a_junk = arena[:, 7172:7428]
        xss, xrs = small[:, 8:14], small[:, 14:20]
        kss, krs = small[:, 20:28], small[:, 28:36]
        wi8 = small[:, 36:68].rearrange("p (t n) -> p t n", t=TT)
        ifr = small[:, 68:100].rearrange("p (t n) -> p t n", t=TT)
        top8 = small[:, 100:108]
        gcols = small[:, 108:140].rearrange("p (k h t) -> p k h t", k=2, h=A_HEADS)
        m_var, m_rs, m_ps, m_ns = (small[:, 140 + 4 * j:144 + 4 * j] for j in range(4))
        mx, nb, rsum, rinv = (small[:, 156 + 4 * j:160 + 4 * j] for j in range(4))
        b_var, b_rstd = small[:, 172:180], small[:, 180:188]
        gate_b = small[0:A_HEADS, 188:190]
        small2 = sb("small2", [P, 52])
        hcw = small2[:, 0:20].rearrange("p (j b) -> p j b", j=5)
        hcol = small2[:, 20:28].rearrange("p (k t) -> p k t", k=2)
        hg = small2[:, 28:30]
        a_den, a_ri, a_ss, a_s = (small2[:, 30 + 4 * j:34 + 4 * j] for j in range(4))
        scratch = small2[0:1, 48:52]

        banks = [ctx.enter_context(nc.psum_tensor(f"proj{b}", [P, S], F32)) for b in range(4)]
        att = [ctx.enter_context(nc.psum_tensor(f"att{b}", [P, S], F32)) for b in range(4)]

        x_landed = [sem(f"x_landed{t}") for t in range(TT)]
        mem_landed = sem("mem_landed")
        g_landed = sem("g_landed")
        small_landed, vec_landed = sem("small_landed"), sem("vec_landed")
        w_landed = [sem("w_landed0"), sem("w_landed1")]
        w_hi_done, w_lo_done, w_used = sem("w_hi_done"), sem("w_lo_done"), sem("w_used")
        proj_done = [sem(f"proj_done{b}") for b in range(4)]
        bank_empty = [sem(f"bank_empty{b}") for b in range(4)]
        dve_step, act_step, pool_step = sem("dve_step"), sem("act_step"), sem("pool_step")
        consts = sem("consts")
        x_ssq, x_var, x_rstd, x_scaled = sem("x_ssq"), sem("x_var"), sem("x_rstd"), sem("x_scaled")
        x_turned, xT_hi, xT_lo = sem("x_turned"), sem("xT_hi"), sem("xT_lo")
        vec_turned, vec_copied = sem("vec_turned"), sem("vec_copied")
        ang_ready, sincos = sem("ang_ready"), sem("sincos")
        qi_rotated, gates_copied = sem("qi_rotated"), sem("gates_copied")
        gates_turned, gates_read = sem("gates_turned"), sem("gates_read")
        gate_abs, gate_ln, gate_rows, gate_cols = sem("gate_abs"), sem("gate_ln"), sem("gate_rows"), sem("gate_cols")
        gate_back, em_done = sem("gate_back"), sem("em_done")
        idx_turned, idx_copied, ki_copied = sem("idx_turned"), sem("idx_copied"), sem("ki_copied")
        logits, relued, summed = sem("logits"), sem("relued"), sem("summed")
        km_squared, km_var, km_rstd, km_normed = (sem("km_squared"), sem("km_var"),
                                                             sem("km_rstd"), sem("km_normed"))
        km_turned, km_ready = sem("km_turned"), sem("km_ready")
        m_ssq, m_varred, m_rstd = sem("m_ssq"), sem("m_varred"), sem("m_rstd")
        m_scores, m_bias, m_exp = sem("m_scores"), sem("m_bias"), sem("m_exp")
        m_pturned, m_pcopied, m_out, m_scaled, m_oturned, m_y = (sem("m_pturned"), sem("m_pcopied"), sem("m_out"),
                                                                 sem("m_scaled"), sem("m_oturned"), sem("m_y"))
        b_squared, b_varred, b_rstded, b_rotated = (sem("b_squared"), sem("b_varred"),
                                                             sem("b_rstded"), sem("b_rotated"))
        b_turned, b_qcopied, b_kcopied, b_scores = sem("b_turned"), sem("b_qcopied"), sem("b_kcopied"), sem("b_scores")
        b_masked, b_bias, b_exp, b_pturned, b_pcopied = (sem("b_masked"), sem("b_bias"), sem("b_exp"),
                                                         sem("b_pturned"), sem("b_pcopied"))
        b_out, b_scaled, b_oturned, b_y = sem("b_out"), sem("b_scaled"), sem("b_oturned"), sem("b_y")
        a_qk, a_spread, a_md_done, a_wdone = (sem("a_qk"), sem("a_spread"),
                                                       sem("a_md_done"), sem("a_wdone"))
        a_st, a_atd, a_params = sem("a_st"), sem("a_atd"), sem("a_params")
        a_num, a_rinv, a_ssq, a_var, a_rstd = sem("a_num"), sem("a_rinv"), sem("a_ssq"), sem("a_var"), sem("a_rstd")
        a_scale, a_hnd, a_turned, a_y, a_ozd = (sem("a_scale"), sem("a_hnd"), sem("a_turned"), sem("a_y"),
                                                sem("a_ozd"))
        g_merged = sem("g_merged")
        ys_hi, ys_lo = sem("ys_hi"), sem("ys_lo")
        x_again, out_sent = sem("x_again"), sem("out_sent")

        block = ctx.enter_context(nc.Block())

        def w_cols(w, k0, c0, n):
            return w[k0 * P:(k0 + KH) * P, bass.ds(c0, n)].rearrange("(k p) n -> p k n", p=P)

        wi, wkv, wo = w_in[0], w_mem_kv[0], w_out[0]
        wb = [w_branch[0, j] for j in range(3)]

        def turns_of(eng, steps, n, per, body):
            body(0, True, False)
            with eng.Fori(1, n - 1) as i:
                if steps is not None:
                    steps.enter(i, 1, per)
                body(i, False, False)
                if steps is not None:
                    steps.leave(n - 2)
            body(n - 1, False, True)

        @block.sync
        def _(sp):
            for t in range(TT):
                sp.dma_start(x_in[:, t], x[0, t * P:(t + 1) * P, :]).then_inc(x_landed[t], 16)

            def load(p, parts):
                for kh in range(2):
                    if not (isinstance(p, int) and p == 0):
                        sp.wait_ge(w_lo_done, p * 2 + (kh - 1))
                    at = 0
                    for w, c0, n in parts:
                        sp.dma_start(w_raw[:, kh, :, at:at + n], w_cols(w, kh * KH, c0, n)).then_inc(w_landed[kh], 16)
                        at += n

            load(IDX1[0], [(wi, C_QI, 512)])
            load(IDX2[0], [(wi, C_KI, I_HD + I_HEADS), (wi, C_IF, 2 * A_HEADS)])
            with sp.Fori(0, 4) as i:
                load(i + KV[0], [(wkv, i * 512, 512)])
            with sp.Fori(0, M_HEADS) as h:
                load(h + MS[0], [(wi, h * M_HD + C_QM, M_HD), (wi, h * M_HD + C_ZM, M_HD)])
            with sp.Fori(0, B_HEADS) as h:
                load(h * 2 + BS[0], [(wi, h * P + (C_QB + c * D), P) for c in range(3)])
                load(h * 2 + (BS[0] + 1), [(wi, h * P + C_ZB, P), (wi, h * P + (C_GATE + 2 * D), P), (wb[2], h * P, P)])
            with sp.Fori(0, A_HEADS) as h:
                load(h * 3 + AS[0], [(wi, h * A_HD + C_QA, A_HD), (wi, h * A_HD + C_KA, A_HD)])
                load(h * 3 + (AS[0] + 1), [(wi, h * A_HD + C_VA, A_HD)])
                load(h * 3 + (AS[0] + 2), [(wi, h * A_HD + C_OA, A_HD), (wi, h * A_HD + C_ZA, A_HD)])
            with sp.Fori(0, 4) as j:
                load(j + GB[0], [(wi, j * 256 + (C_GATE + D), 256), (wb[1], j * 256, 256)])
            with sp.Fori(0, 4) as j:
                load(j + GA[0], [(wi, j * 256 + C_GATE, 256), (wb[0], j * 256, 256)])
            sp.wait_ge(ys_lo, 3 * KT)
            for t in range(TT):
                sp.dma_start(x_in[:, t], x[0, t * P:(t + 1) * P, :]).then_inc(x_again, 16)
            with sp.Fori(0, 2) as c:
                load(c + OUT[0], [(wo, c * 512, 512)])
            for c in range(2):
                for t in range(TT):
                    sp.wait_ge(bank_empty[t], OUT[2][t] + c + 1)
                    sp.dma_start(out[0, t * P:(t + 1) * P, c * 512:(c + 1) * 512],
                                 x_in[:, t, c * 512:(c + 1) * 512]).then_inc(out_sent, 16)
            sp.wait_ge(out_sent, 16 * 2 * TT)

        @block.tensor
        def _(pe):
            mm, turn = nc.tensor.matmul, nc.tensor.transpose

            def products(ps, lhs, rhs, k0, first, last):
                for k in range(KH):
                    for j, (a, b) in enumerate(((0, 0), (0, 1), (1, 0))):
                        ins = mm(ps, lhs[a](k, k0), rhs[b](k, k0), start=(first and k == 0 and j == 0),
                                 stop=(last and k == KH - 1 and j == 2))
                return ins

            def panel(p, blocks, hooks=None):
                hooks = hooks or {}
                slot = 0
                for kh in range(2):
                    pe.wait_ge(w_lo_done, p * 2 + (kh + 1))
                    for n, (b, used, lhs, rhs, width, before) in enumerate(blocks):
                        for hook in hooks.get(slot, ()):
                            hook()
                        slot += 1
                        if kh == 0 and not (isinstance(used, int) and used == 0):
                            pe.wait_ge(bank_empty[b], used)
                        if kh == 0 and before is not None:
                            pe.wait_ge(*before)
                        ins = products(banks[b][:, 0:width], lhs(kh), rhs(kh), kh * KH, kh == 0, kh == 1)
                        if kh == 1:
                            ins.then_inc(proj_done[b], 1)
                        elif n == len(blocks) - 1:
                            ins.then_inc(w_used, 1)

            def w_as_lhs(c0):
                return lambda kh: [lambda k, k0, w=w: w[:, kh, k, c0:c0 + P] for w in (w_hi, w_lo)]

            def w_as_rhs(n):
                return lambda kh: [lambda k, k0, w=w: w[:, kh, k, 0:n] for w in (w_hi, w_lo)]

            def tokens(pair, t):
                return lambda kh: [lambda k, k0, w=w: w[:, k0 + k, t * P:(t + 1) * P] for w in pair]

            def all_tokens(pair):
                return lambda kh: [lambda k, k0, w=w: w[:, k0 + k, :] for w in pair]

            hT, yT = (hT_hi, hT_lo), (y_hi, y_lo)

            pe.wait_ge(consts, 4)
            pe.wait_ge(vec_landed, 16 * 5)
            turn(att[0][:, 0:92], vec_rows, ident[0:92, 0:92]).then_inc(vec_turned, 1)
            for t in range(TT + MT):
                pe.wait_ge(x_scaled, t + 1)
                for half in range(2):
                    n = 2 * t + half
                    if n == 0:
                        pe.wait_ge(vec_copied, 1)
                    if n >= 4:
                        pe.wait_ge(xT_lo, n - 3)
                    for k in range(4):
                        ins = turn(att[n % 4][:, k * P:(k + 1) * P],
                                   x_sc[:, t % 2, (half * 4 + k) * P:(half * 4 + k + 1) * P], ident[:, :])
                    ins.then_inc(x_turned, 1)

            pe.wait_ge(xT_lo, 2 * TT)
            panel(IDX1[0], [(t, 0, tokens(hT, t), w_as_rhs(512), 512, None) for t in range(1, TT)])
            panel(IDX2[0], [(t, IDX2[2][t], tokens(hT, t), w_as_rhs(80), 80, None) for t in range(TT)])

            def gates_to_rows():
                pe.wait_ge(gates_copied, TT)
                pe.wait_ge(xT_lo, 2 * (TT + MT))
                for kind in range(2):
                    for t in range(TT):
                        ins = turn(att[kind][0:A_HEADS, t * P:(t + 1) * P],
                                   ifr[:, t, kind * A_HEADS:(kind + 1) * A_HEADS], ident[:, :])
                ins.then_inc(gates_turned, 1)

            def idx_transposes():
                pe.wait_ge(qi_rotated, 3)
                pe.wait_ge(bank_empty[3], IDX2[2][3] + 1)
                pe.wait_ge(gates_read, 1)
                for t in range(3):
                    for j in range(4):
                        ins = turn(att[t][:, j * P:(j + 1) * P], qi_rot[:, t, j * P:(j + 1) * P], ident[:, :])
                    ins.then_inc(idx_turned, 1)
                for t in range(TT):
                    ins = turn(att[3][:, t * P:(t + 1) * P], ki_rot[:, t, :], ident[:, :])
                ins.then_inc(idx_turned, 1)

            def logit(u):
                t, h = u // 8 + 1, u % 8
                if u == 0:
                    pe.wait_ge(idx_copied, 3)
                    pe.wait_ge(ki_copied, 1)
                if u >= 4:
                    pe.wait_ge(relued, u - 3)
                lo = I_HD * (h % 2)
                mm(att[u % 4][:, 0:(t + 1) * P], qiT[lo:lo + I_HD, h // 2, (t - 1) * P:t * P],
                   kiT[lo:lo + I_HD, 0:(t + 1) * P], start=True, stop=True).then_inc(logits, 1)

            def kv_hooks(i):
                if i == 0:
                    return {0: [gates_to_rows], 2: [idx_transposes]}
                return {s: [lambda u=(i - 1) * 8 + 2 * s + e: logit(u) for e in range(2)] for s in range(4)}

            memT = (memT_hi, memT_lo)
            pe.wait_ge(xT_lo, 2 * (TT + MT))
            for i in range(4):
                panel(KV[0] + i, [(2 * (i % 2) + m, KV[2][2 * (i % 2) + m] + i // 2, tokens(memT, m),
                                   w_as_rhs(512), 512, None) for m in range(MT)], kv_hooks(i))

            def gates_to_columns():
                pe.wait_ge(gate_rows, 1)
                pe.wait_ge(summed, 24)
                for kind in range(2):
                    for t in range(TT):
                        c = (kind * TT + t) * A_HEADS
                        ins = turn(att[0][:, c:c + A_HEADS], rows[:, kind, t * P:(t + 1) * P],
                                   ident[0:A_HEADS, 0:A_HEADS])
                ins.then_inc(gate_back, 1)

            def km_transposes():
                pe.wait_ge(km_normed, 1)
                pe.wait_ge(gate_cols, 1)
                for h in range(M_HEADS):
                    for e in range(2):
                        for m in range(MT):
                            ins = turn(att[h][:, (e * MT + m) * P:(e * MT + m + 1) * P],
                                       km_raw[:, m * D + h * M_HD + e * P:m * D + h * M_HD + (e + 1) * P],
                                       ident[:, :])
                    ins.then_inc(km_turned, 1)

            def m_norm_scores(h):
                pe.wait_ge(bank_empty[1], h + (MS[2][1] + 1))
                if isinstance(h, int) and h == 0:
                    pe.wait_ge(km_ready, M_HEADS)
                    pe.wait_ge(bank_empty[3], KV[2][3] + 2)
                else:
                    pe.wait_ge(m_y, h * 2)
                for t in range(TT):
                    for e in range(2):
                        ins = mm(att[0][:, t:t + 1], m_sq[:, e, t * P:(t + 1) * P], ones[:, :],
                                 start=(e == 0), stop=(e == 1))
                ins.then_inc(m_ssq, 1)
                kh_ = kmT.rearrange("p h n -> p (h n)")
                for t in range(TT):
                    for e in range(2):
                        ins = mm(att[1 + t // 2][:, (t % 2) * MEM:(t % 2 + 1) * MEM], m_qT[:, e, t * P:(t + 1) * P],
                                 kh_[:, bass.ds(h * 512 + e * MEM, MEM)], start=(e == 0), stop=(e == 1))
                    if t % 2:
                        ins.then_inc(m_scores, 1)

            def m_turn_p(h):
                for g in range(2):
                    pe.wait_ge(m_exp, h * 4 + (2 * g + 2))
                    for t in (2 * g, 2 * g + 1):
                        for m in range(MT):
                            c = ((t % 2) * MT + m) * P
                            ins = turn(att[3 - 3 * g][:, c:c + P], m_p[:, t, m * P:(m + 1) * P], ident[:, :])
                    ins.then_inc(m_pturned, 1)

            def m_values(h):
                vflat = vm.rearrange("p m n -> p (m n)")
                for g in range(2):
                    pe.wait_ge(m_pcopied, h * 2 + (g + 1))
                    for t in (2 * g, 2 * g + 1):
                        for m in range(MT):
                            ins = mm(att[1 + g][:, (t % 2) * M_HD:(t % 2 + 1) * M_HD],
                                     m_pT[:, t, m * P:(m + 1) * P], vflat[:, bass.ds(h * M_HD + m * D, M_HD)],
                                     start=(m == 0), stop=(m == MT - 1))
                    ins.then_inc(m_out, 1)

            def m_turn_out(h):
                pe.wait_ge(m_scaled, h * 2 + 2)
                for e in range(2):
                    for t in range(TT):
                        ins = turn(att[3 - 3 * e][:, t * P:(t + 1) * P], m_on[:, t, e * P:(e + 1) * P], ident[:, :])
                    ins.then_inc(m_oturned, 1)

            def m_hooks(h, first):
                if first:
                    return {0: [gates_to_columns], 3: [km_transposes]}
                g = h - 1
                return {1: [lambda: m_norm_scores(g)], 4: [lambda: m_turn_p(g)],
                        5: [lambda: m_values(g)], 7: [lambda: m_turn_out(g)]}

            def m_body(h, first, last):
                panel(h + MS[0], [(b, h + MS[2][b], w_as_lhs(b * P), all_tokens(hT), S, None) for b in range(4)],
                      m_hooks(h, first))

            turns_of(pe, None, M_HEADS, 0, m_body)

            def b_turn_qk(h):
                pe.wait_ge(b_rotated, h + 1)
                if not (isinstance(h, int) and h == 0):
                    pe.wait_ge(b_pcopied, h * 4)
                else:
                    pe.wait_ge(m_y, 2 * M_HEADS)
                for c in range(2):
                    for t in range(TT):
                        ins = turn(att[c][:, t * P:(t + 1) * P],
                                   b_rc[:, (2 * t + c) * P:(2 * t + c + 1) * P], ident[:, :])
                    ins.then_inc(b_turned, 1)

            def b_score(h):
                if not (isinstance(h, int) and h == 0):
                    pe.wait_ge(b_y, h)
                pe.wait_ge(b_qcopied, h + 1)
                pe.wait_ge(b_kcopied, h + 1)
                for t in range(TT):
                    mm(att[(t + 2) % 4][:, 0:(t + 1) * P], b_qT[:, t * P:(t + 1) * P], b_kT[:, 0:(t + 1) * P],
                       start=True, stop=True).then_inc(b_scores, 1)

            def b_turn_p(h):
                for t in range(TT):
                    pe.wait_ge(b_exp, h * 4 + (t + 1))
                    for s in range(t + 1):
                        ins = turn(att[(t + 2) % 4][:, s * P:(s + 1) * P],
                                   score[:, off(t) + s * P:off(t) + (s + 1) * P], ident[:, :])
                    ins.then_inc(b_pturned, 1)

            def b_values(h):
                pe.wait_ge(b_pcopied, h * 4 + 4)
                for t in range(TT):
                    for s in range(t + 1):
                        ins = mm(att[2][:, t * P:(t + 1) * P], b_pT[:, off(t) + s * P:off(t) + (s + 1) * P],
                                 b_raw[:, s, 2 * P:3 * P], start=(s == 0), stop=(s == t))
                ins.then_inc(b_out, 1)

            def b_turn_out(h):
                pe.wait_ge(b_scaled, h + 1)
                for t in range(TT):
                    ins = turn(att[3][:, t * P:(t + 1) * P], b_on[:, t, :], ident[:, :])
                ins.then_inc(b_oturned, 1)

            def b_body(h, first, last):
                g = h - 1
                if first:
                    g = M_HEADS - 1
                    hooks_t = {1: [lambda: m_norm_scores(g)], 4: [lambda: m_turn_p(g)],
                               5: [lambda: m_values(g)], 7: [lambda: m_turn_out(g)]}
                    hooks_f = {}
                else:
                    hooks_t = {1: [lambda: b_score(g)], 5: [lambda: b_turn_p(g)], 7: [lambda: b_values(g)]}
                    hooks_f = {0: [lambda: b_turn_out(g)]}
                hooks_f[5] = [lambda: b_turn_qk(h)]
                step = (2, 2, 2, 1)
                panel(h * 2 + BS[0], [(t, h * step[t] + BS[2][t], tokens(hT, t), w_as_rhs(384), 384, None)
                                      for t in range(TT)], hooks_t)
                panel(h * 2 + (BS[0] + 1),
                      [(b, h * 2 + (BS[2][b] + 1), w_as_lhs(b * P), all_tokens(yT if b == 2 else hT), S,
                        (ys_lo, KT) if b == 2 and first else None) for b in range(3)], hooks_f)

            turns_of(pe, None, B_HEADS, 0, b_body)

            def a_spread_max(h):
                if isinstance(h, int) and h == 0:
                    pe.wait_ge(b_y, B_HEADS)
                else:
                    pe.wait_ge(a_y, h * 2)
                mm(att[0][:, :], pick[:, 0, :], maxrow, start=True, stop=True).then_inc(a_spread, 1)

            def a_scores(h):
                pe.wait_ge(a_qk, h * 4 + 4)
                for s in range(TT):
                    bank, c = ((1, 0), (2, 0), (3, 0), (3, 2 * P))[s]
                    n = S - s * P
                    for e in range(2):
                        ins = mm(att[bank][:, c:c + n], a_kT[:, e, s * P:(s + 1) * P], a_qT[:, e, s * P:S],
                                 start=(e == 0), stop=(e == 1))
                    ins.then_inc(a_st, 1)

            def a_numerators(h):
                pe.wait_ge(a_atd, h * 4 + 4)
                pe.wait_ge(bank_empty[3], h * 3 + (AS[2][3] + 2))
                for t in range(TT):
                    for s in range(t + 1):
                        c = st_off(s) + (t - s) * P
                        ins = mm(att[t][:, 0:A_HD + 1], a_at[:, c:c + P], a_v[:, s, :], start=(s == 0), stop=(s == t))
                    ins.then_inc(a_num, 1)

            def a_turn_h(h):
                pe.wait_ge(a_hnd, h * 4 + 4)
                for e in range(2):
                    for t in range(TT):
                        ins = turn(att[e][:, t * P:(t + 1) * P], a_hn[:, t, e * P:(e + 1) * P], ident[:, :])
                    ins.then_inc(a_turned, 1)

            def a_body(h, first, last):
                g = h - 1
                if first:
                    g = B_HEADS - 1
                    qk_hooks = {1: [lambda: b_score(g)], 3: [lambda: b_turn_p(g)], 5: [lambda: b_values(g)],
                                7: [lambda: b_turn_out(g)]}
                else:
                    qk_hooks = {1: [lambda: a_numerators(g)], 5: [lambda: a_turn_h(g)]}
                u = lambda b, j: h * 3 + (AS[2][b] + j)
                panel(h * 3 + AS[0], [(b, u(b, 0), w_as_lhs(b * P), all_tokens(hT), S, None) for b in range(4)],
                      qk_hooks)
                panel(h * 3 + (AS[0] + 1), [(t, u(t, 1), tokens(hT, t), w_as_rhs(A_HD), A_HD, None)
                                            for t in range(TT)], {2: [lambda: a_spread_max_of(h)]})
                panel(h * 3 + (AS[0] + 2), [(b, u(b, 2), w_as_lhs(b * P), all_tokens(hT), S, None)
                                            for b in range(4)], {1: [lambda: a_scores(h)]})

            def a_spread_max_of(h):
                pe.wait_ge(a_params, h + 1)
                a_spread_max(h)

            turns_of(pe, None, A_HEADS, 0, a_body)

            def gated(sec, j, n, before, hooks=None):
                panel(j + sec[0], [(b, j + sec[2][b], w_as_lhs(b * P), all_tokens(hT if b < 2 else yT), S,
                                    before if b == 2 else None) for b in range(4)], hooks)

            g = A_HEADS - 1
            gated(GB, 0, 0, (ys_lo, 2 * KT), {1: [lambda: a_numerators(g)], 5: [lambda: a_turn_h(g)]})
            with pe.Fori(1, 4) as j:
                gated(GB, j, 0, None)
            gated(GA, 0, 0, (ys_lo, 3 * KT))
            with pe.Fori(1, 4) as j:
                gated(GA, j, 0, None)
            for c in range(2):
                panel(OUT[0] + c, [(t, OUT[2][t] + c, tokens(yT, t), w_as_rhs(512), 512,
                                    (ys_lo, 4 * KT) if c == 0 and t == 0 else None) for t in range(TT)])

        @block.scalar
        def _(act):
            A_ = nc.scalar.activation
            steps = Steps(act, act_step)

            def split_hi(p, kh, loads, n, before=None):
                act.wait_ge(w_landed[kh], loads * 16)
                if kh == 1 and before is not None:
                    act.wait_ge(proj_done[before[0]], before[1])
                elif kh == 0 and not (isinstance(p, int) and p == 0):
                    act.wait_ge(w_used, p)
                A_(w_hi[:, kh, :, 0:n], w_raw[:, kh, :, 0:n], ACT.Copy).then_inc(w_hi_done, 1)

            def split_y(src, times):
                for k in range(KT):
                    A_(y_hi[:, k, :], src[:, k * S:(k + 1) * S], ACT.Copy).then_inc(ys_hi, 1)

            with nc.allow_non_contiguous_dma(reason="a few columns of vectors"):
                act.dma_start(g_row, norm_g.partition_broadcast(P)).then_inc(g_landed, 16)
                act.dma_start(pos_i, positions[0].rearrange("(t p) -> p t", p=P)).then_inc(small_landed, 16)
                act.dma_start(vec_rows[0:64, :], conv_w[0].rearrange("j (b n) -> (j b) n", n=P)).then_inc(vec_landed, 16)
                act.dma_start(vec_rows[64:80, :], conv_b[0].rearrange("(b n) -> b n", n=P)).then_inc(vec_landed, 16)
                act.dma_start(vec_rows[80:88, :], mlstm_norm_g[0].rearrange("h (b n) -> (h b) n", n=P)).then_inc(vec_landed, 16)
                act.dma_start(vec_rows[88:90, :], mem_q_norm_g[0].rearrange("(b n) -> b n", n=P)).then_inc(vec_landed, 16)
                act.dma_start(vec_rows[90:92, :], mem_k_norm_g[0].rearrange("(b n) -> b n", n=P)).then_inc(vec_landed, 16)
                act.dma_start(gain_rows[:, 0:P], dsa_q_norm_g.partition_broadcast(P)).then_inc(small_landed, 16)
                act.dma_start(gain_rows[:, P:2 * P], dsa_k_norm_g.partition_broadcast(P)).then_inc(small_landed, 16)
                act.dma_start(invf, inv_freq.partition_broadcast(P)).then_inc(small_landed, 16)
                act.dma_start(gate_b, mlstm_gate_b[0].rearrange("k h -> h k")).then_inc(small_landed, 16)
                act.dma_start(memg_row, mem_norm_g.partition_broadcast(P)).then_inc(small_landed, 16)
                act.dma_start(mem_in, mem[0].rearrange("(t p) n -> p t n", p=P)).then_inc(mem_landed, 16)

            for t in range(TT + MT):
                if t < TT:
                    act.wait_ge(x_landed[t], 16)
                elif t == TT:
                    act.wait_ge(mem_landed, 16)
                if t:
                    act.wait_ge(x_ssq, t)
                src = x_in[:, t] if t < TT else mem_in[:, t - TT]
                A_(junk, src, ACT.Square, accum_out=xss[:, t:t + 1]).then_inc(x_ssq, 1)
            split_hi(0, 0, 1, 512)
            for n in range(2 * (TT + MT)):
                act.wait_ge(x_turned, n + 1)
                t, half = n // 2, n % 2
                dst = hT_hi if t < TT else memT_hi
                c = t if t < TT else t - TT
                A_(dst[:, half * 4:half * 4 + 4, c * P:(c + 1) * P],
                   att[n % 4][:, :].rearrange("p (k n) -> p k n", k=4), ACT.Copy).then_inc(xT_hi, 1)
                if n == 5:
                    act.wait_ge(ang_ready, 1)
                    A_(sind.rearrange("p t n -> p (t n)"), ang, ACT.Sin).then_inc(sincos, 1)
                    A_(cosd.rearrange("p t n -> p (t n)"), turns, ACT.Sin).then_inc(sincos, 1)

            split_hi(0, 1, 1, 512)
            split_hi(1, 0, 3, 80)
            split_hi(1, 1, 3, 80, (3, 1))
            split_hi(2, 0, KV[1] + 1, 512)
            for t in range(TT):
                act.wait_ge(proj_done[t], IDX2[2][t] + 1)
                A_(wi8[:, t], banks[t][:, I_HD:I_HD + I_HEADS], ACT.Copy, scale=float(np.float32(I_HEADS ** -0.5)))
                ins = A_(ifr[:, t], banks[t][:, I_HD + I_HEADS:I_HD + 2 * I_HEADS], ACT.Copy)
                ins.then_inc(gates_copied, 1)

            def idx_copies():
                for t in range(3):
                    act.wait_ge(idx_turned, t + 1)
                    A_(qiT[:, :, t * P:(t + 1) * P], att[t][:, :].rearrange("p (j n) -> p j n", j=4),
                       ACT.Copy).then_inc(idx_copied, 1)

            def relus(i):
                for u in range(8 * i, 8 * i + 8):
                    t = u // 8 + 1
                    act.wait_ge(logits, u + 1)
                    if u >= 2:
                        act.wait_ge(summed, u - 1)
                    A_(relu[:, u % 2, 0:(t + 1) * P], att[u % 4][:, 0:(t + 1) * P], ACT.Relu,
                       scale=I_HD ** -0.5).then_inc(relued, 1)

            for i in range(4):
                p = KV[0] + i
                last = 3 if i == 0 else 2 * ((i - 1) % 2) + 1
                split_hi(p, 1, KV[1] + i + 1, 512, (last, KV[2][last] + (i + 1) // 2))
                if i == 1:
                    act.wait_ge(gate_abs, 1)
                    steps.then(A_(rows[:, 3], rows[:, 2], ACT.Exp, scale=-1.0))
                    A_(rows[:, 3], rows[:, 3], ACT.Ln, bias=1.0).then_inc(gate_ln, 1)
                if i == 0:
                    idx_copies()
                else:
                    relus(i - 1)
                split_hi(p + 1, 0, KV[1] + i + 2 if i < 3 else MS[1] + 2, 512)
                for m in range(MT):
                    b = 2 * (i % 2) + m
                    act.wait_ge(proj_done[b], KV[2][b] + i // 2 + 1)
                    if i < 2:
                        if i == 0 and m == 0:
                            act.wait_ge(x_scaled, TT + MT)
                        A_(km_raw[:, m * D + i * 512:m * D + (i + 1) * 512], banks[b][:, :], ACT.Copy)\
                            .then_inc(bank_empty[b], 1)
                    else:
                        A_(vm[:, m, (i - 2) * 512:(i - 1) * 512], banks[b][:, :], ACT.Copy)\
                            .then_inc(bank_empty[b], 1)

            def m_exps(h):
                for t in range(TT):
                    if t == 0:
                        act.wait_ge(m_bias, h + 1)
                    A_(m_p[:, t, :], att[1 + t // 2][:, (t % 2) * MEM:(t % 2 + 1) * MEM], ACT.Exp,
                       bias=nb[:, t:t + 1], scale=m_ps[:, t:t + 1], accum_out=rsum[:, t:t + 1]).then_inc(m_exp, 1)

            def m_evac(h, first):
                for e in range(2):
                    act.wait_ge(proj_done[e], h + (MS[2][e] + 1))
                    if first and e == 0:
                        act.wait_ge(vec_copied, 2)
                        act.wait_ge(km_var, 1)
                    A_(m_qT[:, e, :], banks[e][:, :], ACT.Copy, scale=gqk[:, e:e + 1])
                    ins = A_(m_sq[:, e, :], banks[e][:, :], ACT.Square)
                    ins.then_inc(bank_empty[e], 1)
                for e in range(2):
                    b = 2 + e
                    act.wait_ge(proj_done[b], h + (MS[2][b] + 1))
                    if not first and e == 0:
                        act.wait_ge(m_y, h * 2)
                    A_(m_zs[:, e, :], banks[b][:, :], ACT.Silu).then_inc(bank_empty[b], 1)


            def m_body(h, first, last):
                p = h + MS[0]
                split_hi(p, 1, h * 2 + (MS[1] + 2), 512, (3, h + MS[2][3]))
                if first:
                    act.wait_ge(gate_cols, 1)
                    A_(gcols[:, 1].rearrange("p h t -> p (h t)"), gcols[:, 1].rearrange("p h t -> p (h t)"), ACT.Exp,
                       scale=-1.0).then_inc(em_done, 1)
                    for g in range(M_HEADS):
                        act.wait_ge(km_turned, g + 1)
                        A_(kmT[:, g, :], att[g][:, :], ACT.Copy).then_inc(km_ready, 1)
                else:
                    m_exps(h - 1)
                if last:
                    split_hi(p + 1, 0, BS[1] + 3, 384)
                else:
                    split_hi(p + 1, 0, h * 2 + (MS[1] + 4), 512)
                m_evac(h, first)

            turns_of(act, steps, M_HEADS, 0, m_body)

            def b_exps(h):
                for t in range(TT):
                    if t == 0:
                        act.wait_ge(b_bias, h + 1)
                    s_t = score[:, off(t):off(t + 1)]
                    A_(s_t, s_t, ACT.Exp, bias=nb[:, t:t + 1], scale=m_ps[:, t:t + 1],
                       accum_out=rsum[:, t:t + 1]).then_inc(b_exp, 1)

            def b_raw_copies(h, first):
                for t in range(TT):
                    act.wait_ge(proj_done[t], h * (2, 2, 2, 1)[t] + (BS[2][t] + 1))
                    if t == 0:
                        if first:
                            act.wait_ge(m_out, 2 * M_HEADS)
                        else:
                            act.wait_ge(b_out, h)
                    A_(b_raw[:, t, :], banks[t][:, 0:384], ACT.Copy).then_inc(bank_empty[t], 1)

            def b_body(h, first, last):
                p = h * 2 + BS[0]
                split_hi(p, 1, h * 6 + (BS[1] + 3), 384, (3, BS[2][3]) if first else (2, h * 2 + BS[2][2]))
                if first:
                    m_exps(M_HEADS - 1)
                else:
                    b_exps(h - 1)
                split_hi(p + 1, 0, h * 6 + (BS[1] + 6), 384)
                b_raw_copies(h, first)
                split_hi(p + 1, 1, h * 6 + (BS[1] + 6), 384, (3, h + (BS[2][3] + 1)))
                if first:
                    act.wait_ge(m_y, 2 * M_HEADS)
                    act.wait_ge(xT_lo, 2 * (TT + MT))
                    split_y(yF, 1)
                if last:
                    split_hi(p + 2, 0, AS[1] + 2, 512)
                else:
                    split_hi(p + 2, 0, h * 6 + (BS[1] + 9), 384)
                act.wait_ge(proj_done[0], h * 2 + (BS[2][0] + 2))
                if not first:
                    act.wait_ge(b_y, h)
                A_(b_zs, banks[0][:, :], ACT.Silu).then_inc(bank_empty[0], 1)
                act.wait_ge(proj_done[1], h * 2 + (BS[2][1] + 2))
                if not first:
                    act.wait_ge(bank_empty[2], h * 2 + BS[2][2])
                A_(sig[:, 0], banks[1][:, :], ACT.Sigmoid).then_inc(bank_empty[1], 1)
                act.wait_ge(b_turned, h * 2 + 1)
                A_(b_qT, att[0][:, :], ACT.Copy).then_inc(b_qcopied, 1)

            turns_of(act, steps, B_HEADS, 0, b_body)

            def a_norm(h):
                act.wait_ge(a_rinv, h + 1)
                for t in range(TT):
                    ins = A_(a_hn[:, t, :], att[t][:, 0:A_HD], ACT.Square, scale=a_ri[:, t:t + 1],
                             accum_out=a_ss[:, t:t + 1])
                ins.then_inc(a_ssq, 1)
                act.wait_ge(a_scale, h + 1)
                for t in range(TT):
                    A_(a_hn[:, t, :], att[t][:, 0:A_HD], ACT.Copy, scale=a_s[:, t:t + 1]).then_inc(a_hnd, 1)

            def a_weights(h):
                act.wait_ge(a_md_done, h + 1)
                for s in range(TT):
                    ins = A_(a_w[:, st_off(s):st_off(s) + P], a_md[:, s, :], ACT.Exp, bias=hcol[:, 0, s:s + 1])
                    if s < TT - 1:
                        A_(a_w[:, st_off(s) + P:st_off(s + 1)], att[0][:, (s + 1) * P:S], ACT.Exp,
                           bias=hcol[:, 0, s:s + 1])
                ins.then_inc(a_wdone, 1)

            def a_body(h, first, last):
                p = h * 3 + AS[0]
                loads = h * 5 + AS[1]
                split_hi(p, 1, loads + 2, 512, (2, AS[2][2]) if first else (3, h * 3 + AS[2][3]))
                if first:
                    b_exps(B_HEADS - 1)
                else:
                    a_norm(h - 1)
                split_hi(p + 1, 0, loads + 3, A_HD)
                for b in range(4):
                    act.wait_ge(bank_empty[b], h * 3 + (AS[2][b] + 1))
                    dst = (a_qT if b < 2 else a_kT)[:, b % 2, :]
                    A_(dst, a_conv[:, b % 2, :], ACT.Silu).then_inc(a_qk, 1)
                split_hi(p + 1, 1, loads + 3, A_HD, (3, h * 3 + (AS[2][3] + 1)))
                if first:
                    act.wait_ge(b_y, B_HEADS)
                    split_y(yF, 2)
                split_hi(p + 2, 0, loads + 5, 512)
                a_weights(h)
                for t in range(TT):
                    act.wait_ge(proj_done[t], h * 3 + (AS[2][t] + 2))
                    A_(a_v[:, t, 0:A_HD], banks[t][:, 0:A_HD], ACT.Copy).then_inc(bank_empty[t], 1)
                split_hi(p + 2, 1, loads + 5, 512, (3, h * 3 + (AS[2][3] + 2)))
                split_hi(p + 3, 0, loads + 7, 512)
                for e in range(2):
                    act.wait_ge(proj_done[e], h * 3 + (AS[2][e] + 3))
                    A_(a_o[:, e, :], banks[e][:, :], ACT.Sigmoid).then_inc(bank_empty[e], 1)
                for e in range(2):
                    act.wait_ge(proj_done[2 + e], h * 3 + (AS[2][2 + e] + 3))
                    A_(a_oz[:, e, :], banks[2 + e][:, :], ACT.Silu).then_inc(bank_empty[2 + e], 1)

            turns_of(act, steps, A_HEADS, 0, a_body)

            def gates(sec, j, n):
                for b in range(2):
                    act.wait_ge(proj_done[b], j + (sec[2][b] + 1))
                    if not (isinstance(n, int) and n == 0):
                        act.wait_ge(g_merged, n * 2 + (b - 1))
                    A_(sig[:, b], banks[b][:, :], ACT.Sigmoid).then_inc(bank_empty[b], 1)

            def gb_body(sec, j, n, next_loads):
                p = j + sec[0]
                split_hi(p, 1, j * 2 + (sec[1] + 2), 512, (3, j + sec[2][3]))
                if n is None:
                    a_norm(A_HEADS - 1)
                    n = 0
                    act.wait_ge(bank_empty[2], AS[2][2])
                split_hi(p + 1, 0, next_loads, 512)
                gates(sec, j, n)

            gb_body(GB, 0, None, GB[1] + 4)
            with act.Fori(1, 4) as j:
                gb_body(GB, j, j, j * 2 + (GB[1] + 4))
            act.wait_ge(a_y, 2 * A_HEADS)
            act.wait_ge(proj_done[3], GA[2][3])
            split_y(yF, 3)
            with act.Fori(0, 3) as j:
                gb_body(GA, j, j + 4, j * 2 + (GA[1] + 4))
            gb_body(GA, 3, 7, OUT[1] + 1)
            act.wait_ge(g_merged, 16)
            act.wait_ge(proj_done[3], OUT[2][3])
            split_y(merged, 4)
            split_hi(OUT[0], 1, OUT[1] + 1, 512, (3, OUT[2][3]))
            split_hi(OUT[0] + 1, 0, OUT[1] + 2, 512)
            split_hi(OUT[0] + 1, 1, OUT[1] + 2, 512, (3, OUT[2][3] + 1))

        @block.vector
        def _(dve):
            V = nc.vector
            steps = Steps(dve, dve_step)
            then = steps.then

            def split_lo(p, kh, n):
                dve.wait_ge(w_hi_done, p * 2 + (kh + 1))
                V.tensor_tensor(w_lo[:, kh, :, 0:n], w_raw[:, kh, :, 0:n], w_hi[:, kh, :, 0:n].bitcast(F32),
                                ALU.subtract).then_inc(w_lo_done, 1)

            def split_y(src, times):
                for k in range(KT):
                    dve.wait_ge(ys_hi, (times - 1) * KT + k + 1)
                    V.tensor_tensor(y_lo[:, k, :], src[:, k * S:(k + 1) * S], y_hi[:, k, :].bitcast(F32),
                                    ALU.subtract).then_inc(ys_lo, 1)

            V.memset(ones[:, :], 1.0)
            V.memset(minus_half[:, :], -0.5).then_inc(consts, 1)
            dve.wait_ge(small_landed, 16 * 6)
            then(V.tensor_copy(pos_f, pos_i))
            for t in range(TT):
                ins = V.tensor_scalar(ang[:, t * 64:(t + 1) * 64], invf, pos_f[:, t:t + 1], None, ALU.mult)
            then(ins)
            then(V.tensor_scalar(turns, ang, INV_2PI, ROUNDER, ALU.mult, ALU.add))
            then(V.tensor_scalar(turns, turns, -ROUNDER, None, ALU.add))
            for part in (TWO_PI_HI, TWO_PI_MID, TWO_PI_LO):
                then(V.scalar_tensor_tensor(ang, turns, -part, ang, ALU.mult, ALU.add))
            then(V.tensor_scalar(turns, ang, float(np.pi / 2), float(-2 * np.pi), ALU.is_gt, ALU.mult))
            then(V.scalar_tensor_tensor(turns, ang, float(np.pi / 2), turns, ALU.add, ALU.add))
            then(V.tensor_scalar(turns, turns, PI_IN, -PI_IN, ALU.min, ALU.max))
            V.tensor_scalar(ang, ang, PI_IN, -PI_IN, ALU.min, ALU.max).then_inc(ang_ready, 1)

            def x_variance(t):
                dve.wait_ge(x_ssq, t + 1)
                V.tensor_scalar(xss[:, t:t + 1], xss[:, t:t + 1], 1.0 / D, EPS, ALU.mult, ALU.add).then_inc(x_var, 1)

            def x_scale(t):
                dve.wait_ge(x_rstd, t + 1)
                if t == 0:
                    dve.wait_ge(g_landed, 16)
                if t == TT:
                    dve.wait_ge(small_landed, 16 * 6)
                if t >= 2:
                    dve.wait_ge(x_turned, 2 * (t - 1))
                src = x_in[:, t] if t < TT else mem_in[:, t - TT]
                V.scalar_tensor_tensor(x_sc[:, t % 2, :], src, xrs[:, t:t + 1], g_row if t < TT else memg_row,
                                       ALU.mult, ALU.mult).then_inc(x_scaled, 1)

            def x_low(n):
                dve.wait_ge(xT_hi, n + 1)
                t, half = n // 2, n % 2
                hi, lo = (hT_hi, hT_lo) if t < TT else (memT_hi, memT_lo)
                c = t if t < TT else t - TT
                at = (slice(None), slice(half * 4, half * 4 + 4), slice(c * P, (c + 1) * P))
                V.tensor_tensor(lo[at], att[n % 4][:, :].rearrange("p (k n) -> p k n", k=4),
                                hi[at].bitcast(F32), ALU.subtract).then_inc(xT_lo, 1)

            x_variance(0)
            dve.wait_ge(vec_turned, 1)
            V.tensor_copy(cols[:, :], att[0][:, 0:92]).then_inc(vec_copied, 1)
            dve.wait_ge(vec_copied, 1)
            V.tensor_tensor(gqk[:, :], cols[:, 88:90], cols[:, 90:92], ALU.mult).then_inc(vec_copied, 1)
            x_variance(1)
            x_scale(0)
            for t in range(1, TT + MT):
                if t + 1 < TT + MT:
                    x_variance(t + 1)
                x_scale(t)
                x_low(2 * t - 2)
                x_low(2 * t - 1)
                if t == 1:
                    split_lo(0, 0, 512)
            x_low(2 * (TT + MT) - 2)
            x_low(2 * (TT + MT) - 1)

            dve.wait_ge(sincos, 2)
            for tab, src, src32 in ((0, cosd, cos32), (1, sind, sin32)):
                for half in range(2):
                    V.tensor_copy(src32[:, :, half * 32:(half + 1) * 32],
                                  src.rearrange("p t (i two) -> p t i two", two=2)[:, :, :, 0])
                for c in range(2):
                    for half in range(2):
                        g = gain_rows[:, c * P + half * 64:c * P + half * 64 + 64]
                        ins = V.tensor_tensor(tabs[:, tab, :, c * P + half * 64:c * P + half * 64 + 64], src,
                                              g.unsqueeze(1).to_broadcast([P, TT, 64]), ALU.mult)
            then(ins)

            def rotate(dst, a, b, src, cos, sin, heads):
                cb = cos.unsqueeze(1).to_broadcast([P, heads, I_HD])
                sb_ = sin.unsqueeze(1).to_broadcast([P, heads, I_HD])
                s3 = src.rearrange("p (h d) -> p h d", h=heads)
                V.tensor_tensor(a.rearrange("p (h d) -> p h d", h=heads), s3, cb, ALU.mult)
                return V.tensor_tensor(b.rearrange("p (h d) -> p h d", h=heads), s3, sb_, ALU.mult)

            def join(a, b, heads, half):
                a4 = a.rearrange("p (h two d) -> p h two d", h=heads, two=2)
                b4 = b.rearrange("p (h two d) -> p h two d", h=heads, two=2)
                V.tensor_tensor(a4[:, :, 0], a4[:, :, 0], b4[:, :, 1], ALU.subtract)
                return V.tensor_tensor(a4[:, :, 1], a4[:, :, 1], b4[:, :, 0], ALU.add)

            split_lo(0, 1, 512)
            split_lo(1, 0, 80)
            for t in range(1, TT):
                dve.wait_ge(proj_done[t], 1)
                if t > 1:
                    dve.wait_ge(qi_rotated, t - 1)
                a = qi_rot[:, t - 1, :]
                ins = rotate(None, a, qi_b, banks[t][:, :], cos32[:, t], sin32[:, t], I_HEADS)
                ins.then_inc(bank_empty[t], 1)
                dve.wait_ge(bank_empty[t], 1)
                join(a, qi_b, I_HEADS, 32).then_inc(qi_rotated, 1)
                if t == 1:
                    split_lo(1, 1, 80)
            split_lo(2, 0, 512)
            dve.wait_ge(qi_rotated, 3)
            for t in range(TT):
                dve.wait_ge(proj_done[t], IDX2[2][t] + 1)
                dve.wait_ge(gates_copied, t + 1)
                a, b = ki_rot[:, t, 0:I_HD], qi_b[:, 0:I_HD]
                then(rotate(None, a, b, banks[t][:, 0:I_HD], cos32[:, t], sin32[:, t], 1))
                then(join(a, b, 1, 32))
                V.tensor_copy(ki_rot[:, t, I_HD:2 * I_HD], a).then_inc(bank_empty[t], 1)

            def gate_in():
                dve.wait_ge(gates_turned, 1)
                then(V.tensor_scalar(rows[:, 0], att[0][0:A_HEADS, :], gate_b[:, 0:1], None, ALU.add))
                V.tensor_scalar(rows[:, 1], att[1][0:A_HEADS, :], gate_b[:, 1:2], None, ALU.add).then_inc(gates_read, 1)
                dve.wait_ge(gates_read, 1)
                V.scalar_tensor_tensor(rows[:, 2], rows[:, 1], -1.0, rows[:, 1], ALU.mult, ALU.max).then_inc(gate_abs, 1)

            def gate_scans():
                dve.wait_ge(gate_ln, 1)
                then(V.scalar_tensor_tensor(rows[:, 1], rows[:, 1], 0.0, rows[:, 3], ALU.min, ALU.subtract))
                then(V.memset(rows[:, 2], 1.0))
                then(V.tensor_tensor_scan(rows[:, 3], rows[:, 2], rows[:, 1], 0.0, ALU.mult, ALU.add))
                then(V.tensor_tensor(rows[:, 0], rows[:, 0], rows[:, 3], ALU.subtract))
                then(V.tensor_tensor_scan(maxrow, rows[:, 0], rows[:, 0], 0.0, ALU.max, ALU.max))
                V.tensor_tensor(rows[:, 1], rows[:, 3], maxrow, ALU.add).then_inc(gate_rows, 1)

            def sums(i):
                for u in range(8 * i, 8 * i + 8):
                    t, h = u // 8 + 1, u % 8
                    acc = score[:, off(t):off(t + 1)]
                    dve.wait_ge(relued, u + 1)
                    r = relu[:, u % 2, 0:(t + 1) * P]
                    if h == 0:
                        V.tensor_scalar(acc, r, wi8[:, t, 0:1], None, ALU.mult).then_inc(summed, 1)
                    else:
                        V.scalar_tensor_tensor(acc, r, wi8[:, t, h:h + 1], acc, ALU.mult, ALU.add).then_inc(summed, 1)
                    dve.wait_ge(summed, u + 1)
                then(V.memset(score[0:64, off(t) + t * P + 64:off(t + 1)], NEG))

            for i in range(4):
                p = KV[0] + i
                split_lo(p, 1, 512)
                if i == 0:
                    gate_in()
                    dve.wait_ge(idx_turned, 4)
                    V.tensor_copy(kiT, att[3][:, :]).then_inc(ki_copied, 1)
                else:
                    sums(i - 1)
                split_lo(p + 1, 0, 512)
                if i == 1:
                    gate_scans()
                if i == 2:
                    dve.wait_ge(km_squared, 1)
                    then(V.tensor_reduce(kss, km_sq.rearrange("p (g n) -> p g n", n=M_HD), AX, ALU.add))
                    V.tensor_scalar(kss, kss, 1.0 / M_HD, EPS, ALU.mult, ALU.add).then_inc(km_var, 1)

            def held(cell=0):
                if steps.turn is not None:
                    V.memset(scratch[:, cell:cell + 1], 0.0)

            def top_round(t):
                row = score[:, off(t):off(t + 1)]
                held()
                then(V.max(top8, row))
                held()
                then(V.match_replace(row, top8, row, TAKEN))

            def make_mask(t):
                V.tensor_scalar(negmask[:, off(t):off(t + 1)], score[:, off(t):off(t + 1)], 0.5 * TAKEN, NEG,
                                ALU.is_gt, ALU.mult)

            def m_norms(h):
                dve.wait_ge(m_ssq, h + 1)
                V.tensor_scalar(m_var, att[0][:, 0:TT], 1.0 / M_HD, EPS, ALU.mult, ALU.add).then_inc(m_varred, 1)
                dve.wait_ge(m_scores, h * 2 + 1)
                V.reduce_max(mx[:, 0:2], att[1][:, :].rearrange("p (t n) -> p t n", t=2), AX)
                dve.wait_ge(m_scores, h * 2 + 2)
                V.reduce_max(mx[:, 2:4], att[2][:, :].rearrange("p (t n) -> p t n", t=2), AX)
                dve.wait_ge(m_rstd, h + 1)
                V.tensor_scalar(m_ps, m_rs, M_HD ** -0.5, None, ALU.mult)
                then(V.tensor_scalar(m_ns, m_rs, -(M_HD ** -0.5), None, ALU.mult))
                V.tensor_tensor(nb, mx, m_ns, ALU.mult).then_inc(m_bias, 1)

            def m_rest(h):
                for g in range(2):
                    dve.wait_ge(m_pturned, h * 2 + (g + 1))
                    V.tensor_copy(m_pT[:, 2 * g:2 * g + 2, :].rearrange("p t n -> p (t n)"), att[3 - 3 * g][:, :])\
                        .then_inc(m_pcopied, 1)
                dve.wait_ge(m_exp, h * 4 + 4)
                then(V.reciprocal(rinv, rsum))
                for g in range(2):
                    dve.wait_ge(m_out, h * 2 + (g + 1))
                    V.tensor_tensor(m_on[:, 2 * g:2 * g + 2, :], att[1 + g][:, :].rearrange("p (t n) -> p t n", t=2),
                                    rinv[:, 2 * g:2 * g + 2].unsqueeze(2).to_broadcast([P, 2, M_HD]),
                                    ALU.mult).then_inc(m_scaled, 1)
                dve.wait_ge(bank_empty[3], h + (MS[2][3] + 1))
                for e in range(2):
                    dve.wait_ge(m_oturned, h * 2 + (e + 1))
                    V.tensor_tensor(yF[:, bass.ds(h * (2 * S) + e * S, S)], att[3 - 3 * e][:, :], m_zs[:, e, :],
                                    ALU.mult).then_inc(m_y, 1)

            def m_body(h, first, last):
                p = h + MS[0]
                split_lo(p, 1, 512)
                if first:
                    dve.wait_ge(gate_back, 1)
                    V.tensor_copy(gcols, att[0][:, 0:2 * TT * A_HEADS]
                                  .rearrange("p (k t h) -> p k h t", k=2, t=TT)).then_inc(gate_cols, 1)
                    dve.wait_ge(km_rstd, 1)
                    km3 = km_raw.rearrange("p (g n) -> p g n", n=M_HD)
                    V.tensor_tensor(km3, km3, krs.unsqueeze(2).to_broadcast([P, MT * M_HEADS, M_HD]),
                                    ALU.mult).then_inc(km_normed, 1)
                else:
                    m_norms(h - 1)
                tile = 1 if first else 2 if last else 3
                rounds = 16 if first or last else 8
                for r in range(rounds // 2):
                    top_round(tile)
                split_lo(p + 1, 0, 384 if last else 512)
                if not first:
                    m_rest(h - 1)
                for r in range(rounds // 2):
                    top_round(tile)

            turns_of(dve, steps, M_HEADS, M_PER, m_body)
            then(V.memset(negmask[:, 0:P], 0.0))
            for t in range(1, TT):
                make_mask(t)
            then(V.memset(negmask[0:64, 64:P], NEG))

            def b_maxes(h):
                for t in range(TT):
                    dve.wait_ge(b_scores, h * 4 + (t + 1))
                    held(t)
                    V.tensor_tensor_reduce(out=score[:, off(t):off(t + 1)], in0=att[(t + 2) % 4][:, 0:(t + 1) * P],
                                           in1=negmask[:, off(t):off(t + 1)], scale=1.0, scalar=LOWEST,
                                           op0=ALU.add, op1=ALU.max, accum_out=mx[:, t:t + 1]).then_inc(b_masked, 1)
                dve.wait_ge(b_masked, h * 4 + 4)
                V.tensor_tensor(nb, mx, m_ns, ALU.mult).then_inc(b_bias, 1)

            def b_probs(h):
                for t in range(TT):
                    dve.wait_ge(b_pturned, h * 4 + (t + 1))
                    V.tensor_copy(b_pT[:, off(t):off(t + 1)], att[(t + 2) % 4][:, 0:(t + 1) * P]).then_inc(b_pcopied, 1)
                dve.wait_ge(b_exp, h * 4 + 4)
                then(V.reciprocal(rinv, rsum))

            def b_outs(h):
                dve.wait_ge(b_out, h + 1)
                V.tensor_tensor(b_on, att[2][:, :].rearrange("p (t n) -> p t n", t=TT),
                                rinv.unsqueeze(2).to_broadcast([P, TT, P]), ALU.mult).then_inc(b_scaled, 1)

            def b_finish(h):
                dve.wait_ge(b_oturned, h + 1)
                dve.wait_ge(bank_empty[0], h * 2 + (BS[2][0] + 2))
                V.tensor_tensor(yF[:, bass.ds(h * S, S)], att[3][:, :], b_zs, ALU.mult).then_inc(b_y, 1)

            def b_rotary(h):
                dve.wait_ge(b_squared, h + 1)
                then(V.tensor_reduce(b_var, b_sq.rearrange("p (g n) -> p g n", n=P), AX, ALU.add))
                V.tensor_scalar(b_var, b_var, 1.0 / B_HD, EPS, ALU.mult, ALU.add).then_inc(b_varred, 1)
                for tab, dst in ((0, b_rc), (1, b_rs)):
                    ins = V.tensor_tensor(dst.rearrange("p (t n) -> p t n", t=TT), b_raw[:, :, 0:2 * P],
                                          tabs[:, tab], ALU.mult)
                then(ins)
                then(join(b_rc, b_rs, 2 * TT, 64))
                dve.wait_ge(b_rstded, h + 1)
                r2 = b_rstd.rearrange("p (t c) -> p t c", c=2)
                keys = b_rc.rearrange("p (t c n) -> p t c n", t=TT, c=2)[:, :, 1]
                V.tensor_tensor(keys, keys, r2[:, :, 1:2].to_broadcast([P, TT, P]), ALU.mult).then_inc(b_rotated, 1)
                V.tensor_scalar(m_ps, r2[:, :, 0], B_HD ** -0.5, None, ALU.mult)
                then(V.tensor_scalar(m_ns, r2[:, :, 0], -(B_HD ** -0.5), None, ALU.mult))

            def b_body(h, first, last):
                p = h * 2 + BS[0]
                split_lo(p, 1, 384)
                if first:
                    m_norms(M_HEADS - 1)
                else:
                    b_maxes(h - 1)
                split_lo(p + 1, 0, 384)
                if first:
                    m_rest(M_HEADS - 1)
                else:
                    b_probs(h - 1)
                    b_outs(h - 1)
                split_lo(p + 1, 1, 384)
                if first:
                    split_y(yF, 1)
                else:
                    b_finish(h - 1)
                split_lo(p + 2, 0, 512 if last else 384)
                b_rotary(h)
                dve.wait_ge(b_turned, h * 2 + 2)
                V.tensor_copy(b_kT, att[1][:, :]).then_inc(b_kcopied, 1)
                dve.wait_ge(bank_empty[1], h * 2 + (BS[2][1] + 2))
                dve.wait_ge(proj_done[2], h * 2 + (BS[2][2] + 2))
                V.tensor_tensor(merged[:, bass.ds(h * S, S)], banks[2][:, :], sig[:, 0], ALU.mult)\
                    .then_inc(bank_empty[2], 1)

            turns_of(dve, steps, B_HEADS, B_PER, b_body)

            def a_conv_all(h):
                for b in range(4):
                    dve.wait_ge(proj_done[b], h * 3 + (AS[2][b] + 1))
                    if b >= 2:
                        dve.wait_ge(a_qk, h * 4 + (b - 1))
                    u, acc = banks[b], a_conv[:, b % 2, :]
                    then(V.tensor_scalar(acc, u[:, :], hcw[:, 3, b:b + 1], hcw[:, 4, b:b + 1], ALU.mult, ALU.add))
                    for lag in range(1, CONV):
                        ins = V.scalar_tensor_tensor(acc[:, lag:], u[:, 0:S - lag],
                                                     hcw[:, CONV - 1 - lag, b:b + 1], acc[:, lag:],
                                                     ALU.mult, ALU.add)
                        if lag < CONV - 1:
                            then(ins)
                    ins.then_inc(bank_empty[b], 1)

            def a_load_params(h, first):
                if not first:
                    dve.wait_ge(a_y, h * 2)
                cw = cols[:, 0:80].rearrange("p (j c e) -> p j c e", j=5, c=2)
                V.tensor_copy(hcw.rearrange("p j (c e) -> p j c e", c=2), cw[:, :, :, bass.ds(h * 2, 2)])
                V.tensor_copy(hcol, gcols.rearrange("p k h t -> p k (h t)")[:, :, bass.ds(h * TT, TT)])
                V.tensor_copy(pick[:, 0, :], pick.rearrange("p h n -> p (h n)")[:, bass.ds(h * P, P)])
                V.tensor_copy(hg, cols[:, bass.ds(h * 2 + 80, 2)]).then_inc(a_params, 1)
                dve.wait_ge(a_params, h + 1)

            def a_denominators(h):
                dve.wait_ge(a_num, h * 4 + 4)
                for t in range(TT):
                    ins = V.tensor_scalar(a_den[:, t:t + 1], att[t][:, A_HD:A_HD + 1], -1.0, hcol[:, 1, t:t + 1],
                                          ALU.mult, ALU.max)
                then(ins)
                for t in range(TT):
                    ins = V.tensor_tensor(a_den[:, t:t + 1], att[t][:, A_HD:A_HD + 1], a_den[:, t:t + 1], ALU.max)
                then(ins)
                V.reciprocal(a_ri, a_den).then_inc(a_rinv, 1)
                dve.wait_ge(a_ssq, h + 1)
                V.tensor_scalar(a_ss, a_ss, 1.0 / A_HD, EPS, ALU.mult, ALU.add).then_inc(a_var, 1)
                dve.wait_ge(a_rstd, h + 1)
                V.tensor_tensor(a_s, a_ri, a_den, ALU.mult).then_inc(a_scale, 1)

            def a_finish(h):
                dve.wait_ge(a_ozd, h + 1)
                for e in range(2):
                    dve.wait_ge(a_turned, h * 2 + (e + 1))
                    V.scalar_tensor_tensor(yF[:, bass.ds(h * (2 * S) + e * S, S)], att[e][:, :], hg[:, e:e + 1],
                                           a_oz[:, e, :], ALU.mult, ALU.mult).then_inc(a_y, 1)

            def a_body(h, first, last):
                p = h * 3 + AS[0]
                split_lo(p, 1, 512)
                if first:
                    b_maxes(B_HEADS - 1)
                    split_lo(p + 1, 0, A_HD)
                    b_probs(B_HEADS - 1)
                    b_outs(B_HEADS - 1)
                    b_finish(B_HEADS - 1)
                    dve.wait_ge(em_done, 1)
                else:
                    a_denominators(h - 1)
                    split_lo(p + 1, 0, A_HD)
                    a_finish(h - 1)
                a_load_params(h, first)
                a_conv_all(h)
                split_lo(p + 1, 1, A_HD)
                if first:
                    split_y(yF, 2)
                    V.memset(a_v[:, :, A_HD:A_HD + 1], 1.0)
                split_lo(p + 2, 0, 512)
                dve.wait_ge(a_spread, h + 1)
                V.tensor_tensor(a_md, att[0][:, :].rearrange("p (t n) -> p t n", t=TT),
                                causal[:, :].unsqueeze(1).to_broadcast([P, TT, P]), ALU.add).then_inc(a_md_done, 1)
                split_lo(p + 2, 1, 512)
                split_lo(p + 3, 0, 512)
                dve.wait_ge(a_wdone, h + 1)
                for s in range(TT):
                    dve.wait_ge(a_st, h * 4 + (s + 1))
                    bank, c = ((1, 0), (2, 0), (3, 0), (3, 2 * P))[s]
                    n = S - s * P
                    V.scalar_tensor_tensor(a_at[:, st_off(s):st_off(s) + n], att[bank][:, c:c + n], A_HD ** -0.5,
                                           a_w[:, st_off(s):st_off(s) + n], ALU.mult, ALU.mult).then_inc(a_atd, 1)

            turns_of(dve, steps, A_HEADS, A_PER, a_body)

            def gb_merge(sec, j, n):
                for b in range(2):
                    dve.wait_ge(bank_empty[b], j + (sec[2][b] + 1))
                    dve.wait_ge(proj_done[2 + b], j + (sec[2][2 + b] + 1))
                    V.tensor_tensor(sig[:, b], banks[2 + b][:, :], sig[:, b], ALU.mult).then_inc(bank_empty[2 + b], 1)
                    dve.wait_ge(bank_empty[2 + b], j + (sec[2][2 + b] + 1))
                    m = merged[:, bass.ds(j * (2 * S) + b * S, S)]
                    V.tensor_tensor(m, m, sig[:, b], ALU.add).then_inc(g_merged, 1)

            split_lo(GB[0], 1, 512)
            a_denominators(A_HEADS - 1)
            split_lo(GB[0] + 1, 0, 512)
            a_finish(A_HEADS - 1)
            gb_merge(GB, 0, 0)
            with dve.Fori(1, 4) as j:
                split_lo(j + GB[0], 1, 512)
                split_lo(j + (GB[0] + 1), 0, 512)
                gb_merge(GB, j, j)
            split_y(yF, 3)
            with dve.Fori(0, 4) as j:
                split_lo(j + GA[0], 1, 512)
                split_lo(j + (GA[0] + 1), 0, 512)
                gb_merge(GA, j, j + 4)
            split_y(merged, 4)
            split_lo(OUT[0], 1, 512)
            split_lo(OUT[0] + 1, 0, 512)
            dve.wait_ge(x_again, 16 * TT)
            for c in range(2):
                for t in range(TT):
                    dve.wait_ge(proj_done[t], OUT[2][t] + c + 1)
                    o = x_in[:, t, c * 512:(c + 1) * 512]
                    V.tensor_tensor(o, banks[t][:, :], o, ALU.add).then_inc(bank_empty[t], 1)
                if c == 0:
                    split_lo(OUT[0] + 1, 1, 512)

        @block.gpsimd
        def _(pool):
            G = nc.gpsimd
            steps = Steps(pool, pool_step)
            G.memset(ident[:, :], 0.0)
            G.memset(causal[:, :], 0.0)
            steps.then(G.memset(pick[:, :, :], 0.0))
            G.affine_select(out=ident[:, :], in_=ident[:, :], compare_op=ALU.not_equal, fill=1.0, base=0,
                            pattern=[[-1, P]], channel_multiplier=1).then_inc(consts, 1)
            G.affine_select(out=causal[:, :], in_=causal[:, :], compare_op=ALU.is_ge, fill=NEG, base=0,
                            pattern=[[1, P]], channel_multiplier=-1).then_inc(consts, 1)
            G.affine_select(out=pick[:, :, :], in_=pick[:, :, :], compare_op=ALU.not_equal, fill=-1.0, base=0,
                            pattern=[[-1, A_HEADS], [0, P]], channel_multiplier=1).then_inc(consts, 1)
            pool.wait_ge(consts, 4)
            for t in range(TT + MT):
                pool.wait_ge(x_var, t + 1)
                G.tensor_tensor(xrs[:, t:t + 1], xss[:, t:t + 1], minus_half[:, 0:1], ALU.pow).then_inc(x_rstd, 1)
            for b in range(4):
                pool.wait_ge(bank_empty[b], KV[2][b] + 1)
            pool.wait_ge(idx_turned, 4)
            G.tensor_tensor(km_sq, km_raw, km_raw, ALU.mult).then_inc(km_squared, 1)
            pool.wait_ge(km_var, 1)
            G.tensor_tensor(krs, kss, minus_half[:, 0:8], ALU.pow).then_inc(km_rstd, 1)
            with pool.Fori(0, M_HEADS) as h:
                pool.wait_ge(m_varred, h + 1)
                G.tensor_tensor(m_rs, m_var, minus_half[:, 0:TT], ALU.pow).then_inc(m_rstd, 1)
            with pool.Fori(0, B_HEADS) as h:
                pool.wait_ge(bank_empty[3], h + (BS[2][3] + 1))
                qk = b_raw[:, :, 0:2 * P]
                G.tensor_tensor(b_sq.rearrange("p (t n) -> p t n", t=TT), qk, qk, ALU.mult).then_inc(b_squared, 1)
                pool.wait_ge(b_varred, h + 1)
                G.tensor_tensor(b_rstd, b_var, minus_half[:, 0:8], ALU.pow).then_inc(b_rstded, 1)

            def a_powers(h):
                pool.wait_ge(a_var, h + 1)
                G.tensor_tensor(a_den, a_ss, minus_half[:, 0:TT], ALU.pow).then_inc(a_rstd, 1)

            def a_gate(h):
                pool.wait_ge(bank_empty[3], h * 3 + (AS[2][3] + 3))
                G.tensor_tensor(a_oz, a_o, a_oz, ALU.mult).then_inc(a_ozd, 1)

            a_gate(0)
            with pool.Fori(1, A_HEADS) as h:
                a_powers(h - 1)
                a_gate(h)
            a_powers(A_HEADS - 1)


M_PER, B_PER, A_PER = 18, 5, 14

_INS = ['x', 'mem', 'positions', 'norm_g', 'mem_norm_g', 'w_in', 'conv_w', 'conv_b', 'mlstm_gate_b',
        'mlstm_norm_g', 'dsa_q_norm_g', 'dsa_k_norm_g', 'mem_q_norm_g', 'mem_k_norm_g', 'w_mem_kv',
        'w_branch', 'w_out']


def kernel(**inputs):
    import concourse.bacc as bacc
    from concourse.bass_utils import run_bass_kernel_spmd as run

    nc = bacc.Bacc("TRN2", target_bir_lowering=False, num_devices=1)
    arrays, args = {}, []
    for name in _INS:
        arrays[name] = np.ascontiguousarray(inputs[name])
    half = B_HD // 2
    arrays['inv_freq'] = (ROPE_THETA ** (-np.arange(half) / half)).astype(np.float32)[None, :]
    for name, a in arrays.items():
        args.append(nc.dram_tensor(name + "_in", a.shape, mybir.dt.from_np(a.dtype), kind="ExternalInput").ap())
    out = nc.dram_tensor("out", (1, S, D), F32, kind="ExternalOutput").ap()
    hybrid_block(nc, *args, out)
    r = run(nc, [{name + "_in": a for name, a in arrays.items()}], core_ids=[0])
    return r.results[0]["out"]
```

```python
from contextlib import ExitStack

import numpy as np

import concourse.bass as bass
from concourse import mybir

F32 = mybir.dt.float32
F32R = mybir.dt.float32r
I32 = mybir.dt.int32
ALU = mybir.AluOpType
ACT = mybir.ActivationFunctionType
AX = mybir.AxisListType.X

P = 128
S = 512
D = 1024
TT = S // P
KT = D // P
KH = KT // 2
MEM = 256
MT = MEM // P
CONV = 4
FIRST_TILES = (1, 2, 3, 0)
A_HEADS, A_HD = 4, 256
B_HEADS, B_HD = 8, 128
I_HEADS, I_HD = 8, 64
M_HEADS, M_HD = 4, 256
TOPK = 128
EPS = 1e-6
ROPE_THETA = 10000.0

C_QA = 0
C_KA = C_QA + D
C_VA = C_KA + D
C_IF = C_VA + D
C_OA = C_IF + 2 * A_HEADS
C_ZA = C_OA + D
C_QB = C_ZA + D
C_ZB = C_QB + 3 * D
C_QI = C_ZB + D
C_KI = C_QI + I_HEADS * I_HD
C_QM = C_KI + I_HD + I_HEADS
C_ZM = C_QM + D
C_GATE = C_ZM + D

NEG = -1.0e30
TAKEN = -3.0e38
LOWEST = -3.0e38
INV_2PI = float(np.float32(1.0 / (2.0 * np.pi)))
ROUNDER = 1.5 * 2.0 ** 23
TWO_PI_HI = 6.28125
TWO_PI_MID = float(np.float32(np.floor((2 * np.pi - TWO_PI_HI) * 2 ** 20) / 2 ** 20))
TWO_PI_LO = float(np.float32(2 * np.pi - TWO_PI_HI - TWO_PI_MID))
PI_IN = 3.1415925


def off(t):
    return P * t * (t + 1) // 2


def st_off(s):
    return sum(S - P * r for r in range(s))


class Panels:

    def __init__(self):
        self.panel, self.loads, self.uses = 0, 0, [0, 0, 0, 0]

    def take(self, panels, loads, banks):
        start = (self.panel, self.loads, tuple(self.uses))
        self.panel += panels
        self.loads += loads
        self.uses = [u + b for u, b in zip(self.uses, banks)]
        return start


_plan = Panels()
IDX1 = _plan.take(1, 1, (0, 1, 1, 1))
IDX2 = _plan.take(1, 2, (1, 1, 1, 1))
KV = _plan.take(4, 4, (2, 2, 2, 2))
MS = _plan.take(M_HEADS, 2 * M_HEADS, (M_HEADS,) * 4)
BS = _plan.take(2 * B_HEADS, 6 * B_HEADS, (2 * B_HEADS, 2 * B_HEADS, 2 * B_HEADS, B_HEADS))
AS = _plan.take(3 * A_HEADS, 5 * A_HEADS, (3 * A_HEADS,) * 4)
GB = _plan.take(4, 8, (4,) * 4)
GA = _plan.take(4, 8, (4,) * 4)
OUT = _plan.take(2, 2, (2,) * 4)


class Steps:

    def __init__(self, eng, sem):
        self.eng, self.sem, self.n, self.turn, self.base, self.per = eng, sem, 0, None, 0, 0

    def value(self):
        if self.turn is None:
            return self.n
        return self.turn * self.per + (self.base + self.n)

    def then(self, instruction):
        instruction.then_inc(self.sem, 1)
        self.n += 1
        self.eng.wait_ge(self.sem, self.value())

    def enter(self, turn, first, per):
        self.turn, self.per, self.base, self.entered = turn, per, self.n - first * per, self.n
        self.n = 0

    def leave(self, turns):
        assert self.n == self.per, (self.n, self.per)
        self.n = self.entered + turns * self.per
        self.turn = None


def hybrid_block(nc, x, mem, positions, norm_g, mem_norm_g, w_in, conv_w, conv_b, mlstm_gate_b,
                 mlstm_norm_g, dsa_q_norm_g, dsa_k_norm_g, mem_q_norm_g, mem_k_norm_g,
                 w_mem_kv, w_branch, w_out, inv_freq, out):
    ctx = ExitStack()
    with ctx:
        def sb(name, shape, dt=F32):
            return ctx.enter_context(nc.sbuf_tensor(name, shape, dt))

        def sem(name):
            return ctx.enter_context(nc.semaphore(name))

        hT_hi = sb("hT_hi", [P, KT, S], F32R)
        hT_lo = sb("hT_lo", [P, KT, S], F32R)
        w_raw = sb("w_raw", [P, 2, KH, S])
        w_hi = sb("w_hi", [P, 2, KH, S], F32R)
        w_lo = sb("w_lo", [P, 2, KH, S], F32R)
        y_hi = sb("y_hi", [P, KT, S], F32R)
        y_lo = sb("y_lo", [P, KT, S], F32R)
        yF = sb("yF", [P, KT * S])
        merged = sb("merged", [P, KT * S])
        ident = sb("ident", [P, P])
        causal = sb("causal", [P, P])
        pick = sb("pick", [A_HEADS, A_HEADS, P])
        ones = sb("ones", [P, 1])
        minus_half = sb("minus_half", [P, 8])
        cols = sb("cols", [P, 92])
        gqk = sb("gqk", [P, 2])
        negmask = sb("negmask", [P, off(TT)])
        score = sb("score", [P, off(TT)])
        tabs = sb("tabs", [P, 2, TT, 2 * P])
        sig = sb("sig", [P, 2, S])
        arena = sb("arena", [P, 9216])
        maxrow = sig[0:A_HEADS, 1, :]
        small = sb("small", [P, 192])

        x_in = yF[:, :].rearrange("p (t n) -> p t n", t=TT)
        mem_in = merged[:, 0:MT * D].rearrange("p (t n) -> p t n", t=MT)
        g_row = arena[:, 0:D]
        memg_row = arena[:, D:2 * D]
        x_sc = arena[:, 2 * D:4 * D].rearrange("p (b n) -> p b n", b=2)
        junk = arena[:, 4 * D:5 * D]
        vec_rows = arena[0:92, 5 * D:5 * D + P]
        gain_rows = arena[:, 5 * D + P:5 * D + 3 * P]
        memT_hi = y_hi
        memT_lo = y_lo
        Y0 = 0
        qiT = yF[:, 0:4 * 384].rearrange("p (h n) -> p h n", h=4)
        kiT = yF[:, 1536:2048]
        relu = yF[:, 2048:3072].rearrange("p (b n) -> p b n", b=2)
        cos32 = yF[:, 3072:3328].rearrange("p (t n) -> p t n", t=TT)
        sin32 = yF[:, 3328:3584].rearrange("p (t n) -> p t n", t=TT)
        ki_rot = yF[:, 3584:4096].rearrange("p (t n) -> p t n", t=TT)
        ang = arena[:, 6 * D:6 * D + 256]
        turns = arena[:, 6 * D + 256:6 * D + 512]
        cosd = arena[:, 6 * D + 512:6 * D + 768].rearrange("p (t n) -> p t n", t=TT)
        sind = arena[:, 6 * D + 768:7 * D].rearrange("p (t n) -> p t n", t=TT)
        invf = arena[:, 7 * D:7 * D + 64]
        pos_i = small[:, 0:4].bitcast(I32)
        pos_f = small[:, 4:8]
        qi_rot = arena[:, 4 * D:4 * D + 1536].rearrange("p (t n) -> p t n", t=3)
        qi_b = arena[:, 8 * D:8 * D + 512]
        km_raw = merged[:, 2048:4096]
        km_sq = arena[:, 4096:6144]
        rows = merged[0:A_HEADS, 0:2048].rearrange("p (r n) -> p r n", r=4)
        kmT = arena[:, 0:2048].rearrange("p (h n) -> p h n", h=M_HEADS)
        vm = arena[:, 2048:4096].rearrange("p (m n) -> p m n", m=MT)
        m_qT = arena[:, 4096:5120].rearrange("p (e n) -> p e n", e=2)
        m_sq = arena[:, 5120:6144].rearrange("p (e n) -> p e n", e=2)
        m_p = m_sq[:, :, :].rearrange("p e n -> p (e n)").rearrange("p (t n) -> p t n", t=TT)
        m_pT = arena[:, 6144:7168].rearrange("p (t n) -> p t n", t=TT)
        m_on = arena[:, 7168:8192].rearrange("p (t n) -> p t n", t=TT)
        m_zs = arena[:, 8192:9216].rearrange("p (e n) -> p e n", e=2)
        b_raw = arena[:, 0:1536].rearrange("p (t n) -> p t n", t=TT)
        b_rc = arena[:, 4096:5120]
        b_rs = arena[:, 2048:3072]
        b_qT = arena[:, 3072:3584]
        b_kT = arena[:, 3584:4096]
        b_pT = arena[:, 5120:6400]
        b_on = arena[:, 6400:6912].rearrange("p (t n) -> p t n", t=TT)
        b_zs = arena[:, 8192:8704]
        b_sq = arena[:, 7168:8192]
        a_qT = tabs[:, 0, :, :].rearrange("p t n -> p (t n)").rearrange("p (e n) -> p e n", e=2)
        a_kT = tabs[:, 1, :, :].rearrange("p t n -> p (t n)").rearrange("p (e n) -> p e n", e=2)
        a_conv = negmask[:, 0:1024].rearrange("p (b n) -> p b n", b=2)
        a_v = arena[:, 0:TT * (A_HD + 1)].rearrange("p (t n) -> p t n", t=TT)
        a_w = arena[:, 1028:2308]
        a_at = arena[:, 2308:3588]
        a_md = arena[:, 3588:4100].rearrange("p (t n) -> p t n", t=TT)
        a_hn = arena[:, 4100:5124].rearrange("p (t n) -> p t n", t=TT)
        a_o = arena[:, 5124:6148].rearrange("p (e n) -> p e n", e=2)
        a_oz = arena[:, 6148:7172].rearrange("p (e n) -> p e n", e=2)
        a_junk = arena[:, 7172:7428]
        xss, xrs = small[:, 8:14], small[:, 14:20]
        kss, krs = small[:, 20:28], small[:, 28:36]
        wi8 = small[:, 36:68].rearrange("p (t n) -> p t n", t=TT)
        ifr = small[:, 68:100].rearrange("p (t n) -> p t n", t=TT)
        top8 = small[:, 100:108]
        gcols = small[:, 108:140].rearrange("p (k h t) -> p k h t", k=2, h=A_HEADS)
        m_var, m_rs, m_ps, m_ns = (small[:, 140 + 4 * j:144 + 4 * j] for j in range(4))
        mx, nb, rsum, rinv = (small[:, 156 + 4 * j:160 + 4 * j] for j in range(4))
        b_var, b_rstd = small[:, 172:180], small[:, 180:188]
        gate_b = small[0:A_HEADS, 188:190]
        small2 = sb("small2", [P, 52])
        hcw = small2[:, 0:20].rearrange("p (j b) -> p j b", j=5)
        hcol = small2[:, 20:28].rearrange("p (k t) -> p k t", k=2)
        hg = small2[:, 28:30]
        a_den, a_ri, a_ss, a_s = (small2[:, 30 + 4 * j:34 + 4 * j] for j in range(4))
        scratch = small2[0:1, 48:52]

        banks = [ctx.enter_context(nc.psum_tensor(f"proj{b}", [P, S], F32)) for b in range(4)]
        att = [ctx.enter_context(nc.psum_tensor(f"att{b}", [P, S], F32)) for b in range(4)]

        x_landed = [sem(f"x_landed{t}") for t in range(TT)]
        mem_landed = sem("mem_landed")
        g_landed = sem("g_landed")
        small_landed, vec_landed = sem("small_landed"), sem("vec_landed")
        w_landed = [sem("w_landed0"), sem("w_landed1")]
        w_hi_done, w_lo_done, w_used = sem("w_hi_done"), sem("w_lo_done"), sem("w_used")
        proj_done = [sem(f"proj_done{b}") for b in range(4)]
        bank_empty = [sem(f"bank_empty{b}") for b in range(4)]
        dve_step, act_step, pool_step = sem("dve_step"), sem("act_step"), sem("pool_step")
        consts = sem("consts")
        x_ssq, x_var, x_rstd, x_scaled = sem("x_ssq"), sem("x_var"), sem("x_rstd"), sem("x_scaled")
        x_turned, xT_hi, xT_lo = sem("x_turned"), sem("xT_hi"), sem("xT_lo")
        vec_turned, vec_copied = sem("vec_turned"), sem("vec_copied")
        ang_ready, sincos = sem("ang_ready"), sem("sincos")
        qi_rotated, gates_copied = sem("qi_rotated"), sem("gates_copied")
        gates_turned, gates_read = sem("gates_turned"), sem("gates_read")
        gate_abs, gate_ln, gate_rows, gate_cols = sem("gate_abs"), sem("gate_ln"), sem("gate_rows"), sem("gate_cols")
        gate_back, em_done = sem("gate_back"), sem("em_done")
        idx_turned, idx_copied, ki_copied = sem("idx_turned"), sem("idx_copied"), sem("ki_copied")
        logits, relued, summed = sem("logits"), sem("relued"), sem("summed")
        km_squared, km_var, km_rstd, km_normed = (sem("km_squared"), sem("km_var"),
                                                             sem("km_rstd"), sem("km_normed"))
        km_turned, km_ready = sem("km_turned"), sem("km_ready")
        m_added = sem("m_added")
        m_ssq, m_varred, m_rstd = sem("m_ssq"), sem("m_varred"), sem("m_rstd")
        m_scores, m_bias, m_exp = sem("m_scores"), sem("m_bias"), sem("m_exp")
        m_pturned, m_pcopied, m_out, m_scaled, m_oturned, m_y = (sem("m_pturned"), sem("m_pcopied"), sem("m_out"),
                                                                 sem("m_scaled"), sem("m_oturned"), sem("m_y"))
        b_squared, b_varred, b_rstded, b_rotated = (sem("b_squared"), sem("b_varred"),
                                                             sem("b_rstded"), sem("b_rotated"))
        b_turned, b_qcopied, b_kcopied, b_scores = sem("b_turned"), sem("b_qcopied"), sem("b_kcopied"), sem("b_scores")
        b_masked, b_bias, b_exp, b_pturned, b_pcopied = (sem("b_masked"), sem("b_bias"), sem("b_exp"),
                                                         sem("b_pturned"), sem("b_pcopied"))
        b_out, b_scaled, b_oturned, b_y = sem("b_out"), sem("b_scaled"), sem("b_oturned"), sem("b_y")
        a_qk, a_spread, a_md_done, a_wdone = (sem("a_qk"), sem("a_spread"),
                                                       sem("a_md_done"), sem("a_wdone"))
        a_st, a_atd, a_params = sem("a_st"), sem("a_atd"), sem("a_params")
        a_num, a_rinv, a_ssq, a_var, a_rstd = sem("a_num"), sem("a_rinv"), sem("a_ssq"), sem("a_var"), sem("a_rstd")
        a_scale, a_hnd, a_turned, a_y, a_ozd = (sem("a_scale"), sem("a_hnd"), sem("a_turned"), sem("a_y"),
                                                sem("a_ozd"))
        g_merged, ones_set = sem("g_merged"), sem("ones_set")
        ys_hi, ys_lo = sem("ys_hi"), sem("ys_lo")
        x_again, out_sent = sem("x_again"), sem("out_sent")

        block = ctx.enter_context(nc.Block())

        def w_cols(w, k0, c0, n):
            return w[k0 * P:(k0 + KH) * P, bass.ds(c0, n)].rearrange("(k p) n -> p k n", p=P)

        wi, wkv, wo = w_in[0], w_mem_kv[0], w_out[0]
        wb = [w_branch[0, j] for j in range(3)]

        def turns_of(eng, steps, n, per, body):
            body(0, True, False)
            with eng.Fori(1, n - 1) as i:
                if steps is not None:
                    steps.enter(i, 1, per)
                body(i, False, False)
                if steps is not None:
                    steps.leave(n - 2)
            body(n - 1, False, True)

        @block.sync
        def _(sp):
            for t in FIRST_TILES:
                sp.dma_start(x_in[:, t], x[0, t * P:(t + 1) * P, :]).then_inc(x_landed[t], 16)

            def load(p, parts):
                for kh in range(2):
                    if not (isinstance(p, int) and p == 0):
                        sp.wait_ge(w_lo_done, p * 2 + (kh - 1))
                    at = 0
                    for w, c0, n in parts:
                        sp.dma_start(w_raw[:, kh, :, at:at + n], w_cols(w, kh * KH, c0, n)).then_inc(w_landed[kh], 16)
                        at += n

            load(IDX1[0], [(wi, C_QI, 512)])
            with nc.allow_non_contiguous_dma(reason="a few columns of vectors"):
                sp.dma_start(mem_in, mem[0].rearrange("(t p) n -> p t n", p=P)).then_inc(mem_landed, 16)
                sp.dma_start(memg_row, mem_norm_g.partition_broadcast(P)).then_inc(small_landed, 16)
                sp.dma_start(pos_i, positions[0].rearrange("(t p) -> p t", p=P)).then_inc(small_landed, 16)
                sp.dma_start(vec_rows[0:64, :], conv_w[0].rearrange("j (b n) -> (j b) n", n=P)).then_inc(vec_landed, 16)
                sp.dma_start(vec_rows[64:80, :], conv_b[0].rearrange("(b n) -> b n", n=P)).then_inc(vec_landed, 16)
                sp.dma_start(vec_rows[80:88, :], mlstm_norm_g[0].rearrange("h (b n) -> (h b) n", n=P)).then_inc(vec_landed, 16)
                sp.dma_start(vec_rows[88:90, :], mem_q_norm_g[0].rearrange("(b n) -> b n", n=P)).then_inc(vec_landed, 16)
                sp.dma_start(vec_rows[90:92, :], mem_k_norm_g[0].rearrange("(b n) -> b n", n=P)).then_inc(vec_landed, 16)
                sp.dma_start(gain_rows[:, 0:P], dsa_q_norm_g.partition_broadcast(P)).then_inc(small_landed, 16)
                sp.dma_start(gain_rows[:, P:2 * P], dsa_k_norm_g.partition_broadcast(P)).then_inc(small_landed, 16)
                sp.dma_start(invf, inv_freq.partition_broadcast(P)).then_inc(small_landed, 16)
                sp.dma_start(gate_b, mlstm_gate_b[0].rearrange("k h -> h k")).then_inc(small_landed, 16)
            load(IDX2[0], [(wi, C_KI, I_HD + I_HEADS), (wi, C_IF, 2 * A_HEADS)])
            with sp.Fori(0, 4) as i:
                load(i + KV[0], [(wkv, i * 512, 512)])
            with sp.Fori(0, M_HEADS) as h:
                load(h + MS[0], [(wi, h * M_HD + C_QM, M_HD), (wi, h * M_HD + C_ZM, M_HD)])
            with sp.Fori(0, B_HEADS) as h:
                load(h * 2 + BS[0], [(wi, h * P + (C_QB + c * D), P) for c in range(3)])
                load(h * 2 + (BS[0] + 1), [(wi, h * P + C_ZB, P), (wi, h * P + (C_GATE + 2 * D), P), (wb[2], h * P, P)])
            with sp.Fori(0, A_HEADS) as h:
                load(h * 3 + AS[0], [(wi, h * A_HD + C_QA, A_HD), (wi, h * A_HD + C_KA, A_HD)])
                load(h * 3 + (AS[0] + 1), [(wi, h * A_HD + C_OA, A_HD), (wi, h * A_HD + C_ZA, A_HD)])
                load(h * 3 + (AS[0] + 2), [(wi, h * A_HD + C_VA, A_HD)])
            with sp.Fori(0, 4) as j:
                load(j + GB[0], [(wi, j * 256 + (C_GATE + D), 256), (wb[1], j * 256, 256)])
            with sp.Fori(0, 4) as j:
                load(j + GA[0], [(wi, j * 256 + C_GATE, 256), (wb[0], j * 256, 256)])
            sp.wait_ge(ys_lo, 3 * KT)
            for t in range(TT):
                sp.dma_start(x_in[:, t], x[0, t * P:(t + 1) * P, :]).then_inc(x_again, 16)
            with sp.Fori(0, 2) as c:
                load(c + OUT[0], [(wo, c * 512, 512)])
            for c in range(2):
                for t in range(TT):
                    sp.wait_ge(bank_empty[t], OUT[2][t] + c + 1)
                    sp.dma_start(out[0, t * P:(t + 1) * P, c * 512:(c + 1) * 512],
                                 x_in[:, t, c * 512:(c + 1) * 512]).then_inc(out_sent, 16)
            sp.wait_ge(out_sent, 16 * 2 * TT)

        @block.tensor
        def _(pe):
            mm, turn = nc.tensor.matmul, nc.tensor.transpose

            def products(ps, lhs, rhs, k0, first, last):
                for k in range(KH):
                    for j, (a, b) in enumerate(((0, 0), (0, 1), (1, 0))):
                        ins = mm(ps, lhs[a](k, k0), rhs[b](k, k0), start=(first and k == 0 and j == 0),
                                 stop=(last and k == KH - 1 and j == 2))
                return ins

            def panel(p, blocks, hooks=None):
                hooks = hooks or {}
                slot = 0
                for kh in range(2):
                    pe.wait_ge(w_lo_done, p * 2 + (kh + 1))
                    for n, (b, used, lhs, rhs, width, before) in enumerate(blocks):
                        for hook in hooks.get(slot, ()):
                            hook()
                        slot += 1
                        if kh == 0 and not (isinstance(used, int) and used == 0):
                            pe.wait_ge(bank_empty[b], used)
                        if before is not None and before[kh] is not None:
                            pe.wait_ge(*before[kh])
                        ins = products(banks[b][:, 0:width], lhs(kh), rhs(kh), kh * KH, kh == 0, kh == 1)
                        if kh == 1:
                            ins.then_inc(proj_done[b], 1)
                        elif n == len(blocks) - 1:
                            ins.then_inc(w_used, 1)

            def w_as_lhs(c0):
                return lambda kh: [lambda k, k0, w=w: w[:, kh, k, c0:c0 + P] for w in (w_hi, w_lo)]

            def w_as_rhs(n):
                return lambda kh: [lambda k, k0, w=w: w[:, kh, k, 0:n] for w in (w_hi, w_lo)]

            def tokens(pair, t):
                return lambda kh: [lambda k, k0, w=w: w[:, k0 + k, t * P:(t + 1) * P] for w in pair]

            def all_tokens(pair):
                return lambda kh: [lambda k, k0, w=w: w[:, k0 + k, :] for w in pair]

            hT, yT = (hT_hi, hT_lo), (y_hi, y_lo)

            def y_split(times):
                return [(ys_lo, (times - 1) * KT + (kh + 1) * KH) for kh in range(2)]

            def x_transposes(i):
                pe.wait_ge(x_scaled, i + 1)
                for half in range(2):
                    n = 2 * i + half
                    if n >= 4:
                        pe.wait_ge(xT_lo, n - 3)
                    for k in range(4):
                        ins = turn(att[n % 4][:, k * P:(k + 1) * P],
                                   x_sc[:, i % 2, (half * 4 + k) * P:(half * 4 + k + 1) * P], ident[:, :])
                    ins.then_inc(x_turned, 1)

            def vector_transposes():
                pe.wait_ge(vec_landed, 16 * 5)
                pe.wait_ge(xT_lo, 2 * TT + 1)
                turn(att[0][:, 0:92], vec_rows, ident[0:92, 0:92]).then_inc(vec_turned, 1)

            pe.wait_ge(consts, 4)
            for i in range(TT - 1):
                x_transposes(i)

            panel(IDX1[0], [(t, 0, tokens(hT, t), w_as_rhs(512), 512, [(xT_lo, 2 * FIRST_TILES.index(t) + 2), None])
                            for t in range(1, TT)],
                  {1: [lambda: x_transposes(TT - 1)], 3: [lambda: x_transposes(TT)],
                   4: [lambda: x_transposes(TT + 1)], 5: [vector_transposes]})
            panel(IDX2[0], [(t, IDX2[2][t], tokens(hT, t), w_as_rhs(80), 80,
                             [(xT_lo, 2 * TT), None] if t == 0 else None) for t in range(TT)])

            def gates_to_rows():
                pe.wait_ge(gates_copied, TT)
                pe.wait_ge(vec_copied, 1)
                pe.wait_ge(xT_lo, 2 * (TT + MT))
                for kind in range(2):
                    for t in range(TT):
                        ins = turn(att[kind][0:A_HEADS, t * P:(t + 1) * P],
                                   ifr[:, t, kind * A_HEADS:(kind + 1) * A_HEADS], ident[:, :])
                ins.then_inc(gates_turned, 1)

            def idx_transposes():
                pe.wait_ge(qi_rotated, 3)
                pe.wait_ge(bank_empty[3], IDX2[2][3] + 1)
                pe.wait_ge(gates_read, 1)
                for t in range(3):
                    for j in range(4):
                        ins = turn(att[t][:, j * P:(j + 1) * P], qi_rot[:, t, j * P:(j + 1) * P], ident[:, :])
                    ins.then_inc(idx_turned, 1)
                for t in range(TT):
                    ins = turn(att[3][:, t * P:(t + 1) * P], ki_rot[:, t, :], ident[:, :])
                ins.then_inc(idx_turned, 1)

            def logit(u):
                t, h = u // 8 + 1, u % 8
                if u == 0:
                    pe.wait_ge(idx_copied, 3)
                    pe.wait_ge(ki_copied, 1)
                if u >= 4:
                    pe.wait_ge(relued, u - 3)
                lo = I_HD * (h % 2)
                mm(att[u % 4][:, 0:(t + 1) * P], qiT[lo:lo + I_HD, h // 2, (t - 1) * P:t * P],
                   kiT[lo:lo + I_HD, 0:(t + 1) * P], start=True, stop=True).then_inc(logits, 1)

            def kv_hooks(i):
                if i == 0:
                    return {0: [gates_to_rows], 2: [idx_transposes]}
                return {s: [lambda u=(i - 1) * 8 + 2 * s + e: logit(u) for e in range(2)] for s in range(4)}

            memT = (memT_hi, memT_lo)
            pe.wait_ge(xT_lo, 2 * (TT + MT))
            for i in range(4):
                panel(KV[0] + i, [(2 * (i % 2) + m, KV[2][2 * (i % 2) + m] + i // 2, tokens(memT, m),
                                   w_as_rhs(512), 512, None) for m in range(MT)], kv_hooks(i))

            def gates_to_columns():
                pe.wait_ge(gate_rows, 1)
                pe.wait_ge(summed, 24)
                for kind in range(2):
                    for t in range(TT):
                        c = (kind * TT + t) * A_HEADS
                        ins = turn(att[0][:, c:c + A_HEADS], rows[:, kind, t * P:(t + 1) * P],
                                   ident[0:A_HEADS, 0:A_HEADS])
                ins.then_inc(gate_back, 1)

            def km_transposes():
                pe.wait_ge(km_normed, 1)
                pe.wait_ge(gate_cols, 1)
                for h in range(M_HEADS):
                    for e in range(2):
                        for m in range(MT):
                            ins = turn(att[h][:, (e * MT + m) * P:(e * MT + m + 1) * P],
                                       km_raw[:, m * D + h * M_HD + e * P:m * D + h * M_HD + (e + 1) * P],
                                       ident[:, :])
                    ins.then_inc(km_turned, 1)

            def m_norm_scores(h):
                pe.wait_ge(m_added, h + 1)
                if isinstance(h, int) and h == 0:
                    pe.wait_ge(km_ready, M_HEADS)
                    pe.wait_ge(bank_empty[3], KV[2][3] + 2)
                else:
                    pe.wait_ge(m_y, h * 2)
                for t in range(TT):
                    ins = mm(att[0][:, t:t + 1], m_sq[:, 0, t * P:(t + 1) * P], ones[:, :], start=True, stop=True)
                ins.then_inc(m_ssq, 1)
                kh_ = kmT.rearrange("p h n -> p (h n)")
                for t in range(TT):
                    for e in range(2):
                        ins = mm(att[1 + t // 2][:, (t % 2) * MEM:(t % 2 + 1) * MEM], m_qT[:, e, t * P:(t + 1) * P],
                                 kh_[:, bass.ds(h * 512 + e * MEM, MEM)], start=(e == 0), stop=(e == 1))
                    if t % 2:
                        ins.then_inc(m_scores, 1)

            def m_turn_p(h):
                for g in range(2):
                    pe.wait_ge(m_exp, h * 4 + (2 * g + 2))
                    for t in (2 * g, 2 * g + 1):
                        for m in range(MT):
                            c = ((t % 2) * MT + m) * P
                            ins = turn(att[3 - 3 * g][:, c:c + P], m_p[:, t, m * P:(m + 1) * P], ident[:, :])
                    ins.then_inc(m_pturned, 1)

            def m_values(h):
                vflat = vm.rearrange("p m n -> p (m n)")
                for g in range(2):
                    pe.wait_ge(m_pcopied, h * 2 + (g + 1))
                    for t in (2 * g, 2 * g + 1):
                        for m in range(MT):
                            ins = mm(att[1 + g][:, (t % 2) * M_HD:(t % 2 + 1) * M_HD],
                                     m_pT[:, t, m * P:(m + 1) * P], vflat[:, bass.ds(h * M_HD + m * D, M_HD)],
                                     start=(m == 0), stop=(m == MT - 1))
                    ins.then_inc(m_out, 1)

            def m_turn_out(h):
                pe.wait_ge(m_scaled, h * 2 + 2)
                for e in range(2):
                    for t in range(TT):
                        ins = turn(att[3 - 3 * e][:, t * P:(t + 1) * P], m_on[:, t, e * P:(e + 1) * P], ident[:, :])
                    ins.then_inc(m_oturned, 1)

            def m_hooks(h, first):
                if first:
                    return {0: [gates_to_columns], 3: [km_transposes]}
                g = h - 1
                return {1: [lambda: m_norm_scores(g)], 4: [lambda: m_turn_p(g)],
                        5: [lambda: m_values(g)], 7: [lambda: m_turn_out(g)]}

            def m_body(h, first, last):
                panel(h + MS[0], [(b, h + MS[2][b], w_as_lhs(b * P), all_tokens(hT), S, None) for b in range(4)],
                      m_hooks(h, first))

            turns_of(pe, None, M_HEADS, 0, m_body)

            def b_turn_qk(h):
                pe.wait_ge(b_rotated, h + 1)
                if not (isinstance(h, int) and h == 0):
                    pe.wait_ge(b_pcopied, h * 4)
                else:
                    pe.wait_ge(m_y, 2 * M_HEADS)
                for c in range(2):
                    for t in range(TT):
                        ins = turn(att[c][:, t * P:(t + 1) * P],
                                   b_rc[:, (2 * t + c) * P:(2 * t + c + 1) * P], ident[:, :])
                    ins.then_inc(b_turned, 1)

            def b_score(h):
                if not (isinstance(h, int) and h == 0):
                    pe.wait_ge(b_y, h)
                pe.wait_ge(b_qcopied, h + 1)
                pe.wait_ge(b_kcopied, h + 1)
                for t in range(TT):
                    mm(att[(t + 2) % 4][:, 0:(t + 1) * P], b_qT[:, t * P:(t + 1) * P], b_kT[:, 0:(t + 1) * P],
                       start=True, stop=True).then_inc(b_scores, 1)

            def b_turn_p(h):
                for t in range(TT):
                    pe.wait_ge(b_exp, h * 4 + (t + 1))
                    for s in range(t + 1):
                        ins = turn(att[(t + 2) % 4][:, s * P:(s + 1) * P],
                                   score[:, off(t) + s * P:off(t) + (s + 1) * P], ident[:, :])
                    ins.then_inc(b_pturned, 1)

            def b_values(h):
                pe.wait_ge(b_pcopied, h * 4 + 4)
                for t in range(TT):
                    for s in range(t + 1):
                        ins = mm(att[2][:, t * P:(t + 1) * P], b_pT[:, off(t) + s * P:off(t) + (s + 1) * P],
                                 b_raw[:, s, 2 * P:3 * P], start=(s == 0), stop=(s == t))
                ins.then_inc(b_out, 1)

            def b_turn_out(h):
                pe.wait_ge(b_scaled, h + 1)
                for t in range(TT):
                    ins = turn(att[3][:, t * P:(t + 1) * P], b_on[:, t, :], ident[:, :])
                ins.then_inc(b_oturned, 1)

            def b_body(h, first, last):
                g = h - 1
                if first:
                    g = M_HEADS - 1
                    hooks_t = {1: [lambda: m_norm_scores(g)], 4: [lambda: m_turn_p(g)],
                               5: [lambda: m_values(g)], 7: [lambda: m_turn_out(g)]}
                    hooks_f = {}
                else:
                    hooks_t = {1: [lambda: b_score(g)], 5: [lambda: b_turn_p(g)], 7: [lambda: b_values(g)]}
                    hooks_f = {0: [lambda: b_turn_out(g)]}
                hooks_f[5] = [lambda: b_turn_qk(h)]
                step = (2, 2, 2, 1)
                panel(h * 2 + BS[0], [(t, h * step[t] + BS[2][t], tokens(hT, t), w_as_rhs(384), 384, None)
                                      for t in range(TT)], hooks_t)
                panel(h * 2 + (BS[0] + 1),
                      [(b, h * 2 + (BS[2][b] + 1), w_as_lhs(b * P), all_tokens(yT if b == 2 else hT), S,
                        y_split(1) if b == 2 and first else None) for b in range(3)], hooks_f)

            turns_of(pe, None, B_HEADS, 0, b_body)

            def a_spread_max(h):
                if isinstance(h, int) and h == 0:
                    pe.wait_ge(b_y, B_HEADS)
                else:
                    pe.wait_ge(a_y, h * 2)
                mm(att[0][:, :], pick[:, 0, :], maxrow, start=True, stop=True).then_inc(a_spread, 1)

            def a_scores(h):
                pe.wait_ge(a_qk, h * 4 + 4)
                for s in range(TT):
                    bank, c = ((1, 0), (2, 0), (3, 0), (3, 2 * P))[s]
                    n = S - s * P
                    for e in range(2):
                        ins = mm(att[bank][:, c:c + n], a_kT[:, e, s * P:(s + 1) * P], a_qT[:, e, s * P:S],
                                 start=(e == 0), stop=(e == 1))
                    ins.then_inc(a_st, 1)

            def a_numerators(h):
                pe.wait_ge(a_atd, h * 4 + 4)
                if isinstance(h, int) and h == 0:
                    pe.wait_ge(ones_set, 1)
                pe.wait_ge(bank_empty[3], h * 3 + (AS[2][3] + 3))
                for t in range(TT):
                    for s in range(t + 1):
                        c = st_off(s) + (t - s) * P
                        ins = mm(att[t][:, 0:A_HD + 1], a_at[:, c:c + P], a_v[:, s, :], start=(s == 0), stop=(s == t))
                    ins.then_inc(a_num, 1)

            def a_turn_h(h):
                pe.wait_ge(a_hnd, h * 4 + 4)
                for e in range(2):
                    for t in range(TT):
                        ins = turn(att[e][:, t * P:(t + 1) * P], a_hn[:, t, e * P:(e + 1) * P], ident[:, :])
                    ins.then_inc(a_turned, 1)

            def a_body(h, first, last):
                g = h - 1
                if first:
                    g = B_HEADS - 1
                    qk_hooks = {1: [lambda: b_score(g)], 3: [lambda: b_turn_p(g)], 5: [lambda: b_values(g)],
                                7: [lambda: b_turn_out(g)]}
                else:
                    qk_hooks = {1: [lambda: a_numerators(g)], 5: [lambda: a_turn_h(g)]}
                u = lambda b, j: h * 3 + (AS[2][b] + j)
                panel(h * 3 + AS[0], [(b, u(b, 0), w_as_lhs(b * P), all_tokens(hT), S, None) for b in range(4)],
                      qk_hooks)
                panel(h * 3 + (AS[0] + 1), [(b, u(b, 1), w_as_lhs(b * P), all_tokens(hT), S, None)
                                            for b in range(4)], {2: [lambda: a_spread_max_of(h)],
                                                                 5: [lambda: a_scores(h)]})
                panel(h * 3 + (AS[0] + 2), [(t, u(t, 2), tokens(hT, t), w_as_rhs(A_HD), A_HD, None)
                                            for t in range(TT)])

            def a_spread_max_of(h):
                pe.wait_ge(a_params, h + 1)
                a_spread_max(h)

            turns_of(pe, None, A_HEADS, 0, a_body)

            def gated(sec, j, n, before, hooks=None):
                panel(j + sec[0], [(b, j + sec[2][b], w_as_lhs(b * P), all_tokens(hT if b < 2 else yT), S,
                                    before if b == 2 else None) for b in (2, 3, 0, 1)], hooks)

            g = A_HEADS - 1
            gated(GB, 0, 0, y_split(2), {1: [lambda: a_numerators(g)], 5: [lambda: a_turn_h(g)]})
            with pe.Fori(1, 4) as j:
                gated(GB, j, 0, None)
            gated(GA, 0, 0, y_split(3))
            with pe.Fori(1, 4) as j:
                gated(GA, j, 0, None)
            for c in range(2):
                panel(OUT[0] + c, [(t, OUT[2][t] + c, tokens(yT, t), w_as_rhs(512), 512,
                                    y_split(4) if c == 0 and t == 0 else None) for t in range(TT)])

        @block.scalar
        def _(act):
            A_ = nc.scalar.activation
            steps = Steps(act, act_step)

            def split_hi(p, kh, loads, n, before=None):
                act.wait_ge(w_landed[kh], loads * 16)
                if kh == 1 and before is not None:
                    act.wait_ge(proj_done[before[0]], before[1])
                elif kh == 0 and not (isinstance(p, int) and p == 0):
                    act.wait_ge(w_used, p)
                A_(w_hi[:, kh, :, 0:n], w_raw[:, kh, :, 0:n], ACT.Copy).then_inc(w_hi_done, 1)

            def split_y(src, tiles=range(KT)):
                for k in tiles:
                    A_(y_hi[:, k, :], src[:, k * S:(k + 1) * S], ACT.Copy).then_inc(ys_hi, 1)

            act.dma_start(g_row, norm_g.partition_broadcast(P)).then_inc(g_landed, 16)

            def square(i):
                act.wait_ge(x_landed[FIRST_TILES[i]] if i < TT else mem_landed, 16)
                if i:
                    act.wait_ge(x_ssq, i)
                src = x_in[:, FIRST_TILES[i]] if i < TT else mem_in[:, i - TT]
                A_(junk, src, ACT.Square, accum_out=xss[:, i:i + 1]).then_inc(x_ssq, 1)

            def x_high(n):
                act.wait_ge(x_turned, n + 1)
                i, half = n // 2, n % 2
                dst, c = (hT_hi, FIRST_TILES[i]) if i < TT else (memT_hi, i - TT)
                A_(dst[:, half * 4:half * 4 + 4, c * P:(c + 1) * P],
                   att[n % 4][:, :].rearrange("p (k n) -> p k n", k=4), ACT.Copy).then_inc(xT_hi, 1)

            for i in range(TT):
                square(i)
            for n in range(4):
                x_high(n)
            split_hi(0, 0, 1, 512)
            for n in range(4, 2 * TT):
                x_high(n)
            split_hi(0, 1, 1, 512)
            for i in range(TT, TT + MT):
                square(i)
            for n in range(2 * TT, 2 * (TT + MT)):
                x_high(n)
            act.wait_ge(ang_ready, 1)
            A_(sind.rearrange("p t n -> p (t n)"), ang, ACT.Sin).then_inc(sincos, 1)
            A_(cosd.rearrange("p t n -> p (t n)"), turns, ACT.Sin).then_inc(sincos, 1)

            split_hi(1, 0, 3, 80)
            split_hi(1, 1, 3, 80, (3, 1))
            split_hi(2, 0, KV[1] + 1, 512)
            for t in range(TT):
                act.wait_ge(proj_done[t], IDX2[2][t] + 1)
                A_(wi8[:, t], banks[t][:, I_HD:I_HD + I_HEADS], ACT.Copy, scale=float(np.float32(I_HEADS ** -0.5)))
                ins = A_(ifr[:, t], banks[t][:, I_HD + I_HEADS:I_HD + 2 * I_HEADS], ACT.Copy)
                ins.then_inc(gates_copied, 1)

            def idx_copies():
                for t in range(3):
                    act.wait_ge(idx_turned, t + 1)
                    A_(qiT[:, :, t * P:(t + 1) * P], att[t][:, :].rearrange("p (j n) -> p j n", j=4),
                       ACT.Copy).then_inc(idx_copied, 1)

            def relus(i, part):
                for u in range(8 * i + 4 * part, 8 * i + 4 * part + 4):
                    t = u // 8 + 1
                    act.wait_ge(logits, u + 1)
                    if u >= 2:
                        act.wait_ge(summed, u - 1)
                    A_(relu[:, u % 2, 0:(t + 1) * P], att[u % 4][:, 0:(t + 1) * P], ACT.Relu,
                       scale=I_HD ** -0.5).then_inc(relued, 1)

            for i in range(4):
                p = KV[0] + i
                last = 3 if i == 0 else 2 * ((i - 1) % 2) + 1
                split_hi(p, 1, KV[1] + i + 1, 512, (last, KV[2][last] + (i + 1) // 2))
                if i == 1:
                    act.wait_ge(gate_abs, 1)
                    steps.then(A_(rows[:, 3], rows[:, 2], ACT.Exp, scale=-1.0))
                    A_(rows[:, 3], rows[:, 3], ACT.Ln, bias=1.0).then_inc(gate_ln, 1)
                if i == 0:
                    idx_copies()
                else:
                    relus(i - 1, 0)
                split_hi(p + 1, 0, KV[1] + i + 2 if i < 3 else MS[1] + 2, 512)
                if i:
                    relus(i - 1, 1)
                for m in range(MT):
                    b = 2 * (i % 2) + m
                    act.wait_ge(proj_done[b], KV[2][b] + i // 2 + 1)
                    if i < 2:
                        if i == 0 and m == 0:
                            act.wait_ge(x_scaled, TT + MT)
                        A_(km_raw[:, m * D + i * 512:m * D + (i + 1) * 512], banks[b][:, :], ACT.Copy)\
                            .then_inc(bank_empty[b], 1)
                    else:
                        A_(vm[:, m, (i - 2) * 512:(i - 1) * 512], banks[b][:, :], ACT.Copy)\
                            .then_inc(bank_empty[b], 1)

            def m_exps(h):
                for t in range(TT):
                    if t == 0:
                        act.wait_ge(m_bias, h + 1)
                    A_(m_p[:, t, :], att[1 + t // 2][:, (t % 2) * MEM:(t % 2 + 1) * MEM], ACT.Exp,
                       bias=nb[:, t:t + 1], scale=m_ps[:, t:t + 1], accum_out=rsum[:, t:t + 1]).then_inc(m_exp, 1)

            def m_evac(h, first):
                for e in range(2):
                    act.wait_ge(proj_done[e], h + (MS[2][e] + 1))
                    if first and e == 0:
                        act.wait_ge(vec_copied, 2)
                        act.wait_ge(km_var, 1)
                    A_(m_qT[:, e, :], banks[e][:, :], ACT.Copy, scale=gqk[:, e:e + 1])
                    ins = A_(m_sq[:, e, :], banks[e][:, :], ACT.Square)
                    ins.then_inc(bank_empty[e], 1)
                for e in range(2):
                    b = 2 + e
                    act.wait_ge(proj_done[b], h + (MS[2][b] + 1))
                    if not first and e == 0:
                        act.wait_ge(m_y, h * 2)
                    A_(m_zs[:, e, :], banks[b][:, :], ACT.Silu).then_inc(bank_empty[b], 1)


            def m_body(h, first, last):
                p = h + MS[0]
                split_hi(p, 1, h * 2 + (MS[1] + 2), 512, (3, h + MS[2][3]))
                if first:
                    act.wait_ge(gate_cols, 1)
                    A_(gcols[:, 1].rearrange("p h t -> p (h t)"), gcols[:, 1].rearrange("p h t -> p (h t)"), ACT.Exp,
                       scale=-1.0).then_inc(em_done, 1)
                    for g in range(M_HEADS):
                        act.wait_ge(km_turned, g + 1)
                        A_(kmT[:, g, :], att[g][:, :], ACT.Copy).then_inc(km_ready, 1)
                else:
                    m_exps(h - 1)
                if last:
                    split_hi(p + 1, 0, BS[1] + 3, 384)
                else:
                    split_hi(p + 1, 0, h * 2 + (MS[1] + 4), 512)
                m_evac(h, first)

            turns_of(act, steps, M_HEADS, 0, m_body)

            def b_exps(h):
                for t in range(TT):
                    if t == 0:
                        act.wait_ge(b_bias, h + 1)
                    s_t = score[:, off(t):off(t + 1)]
                    A_(s_t, s_t, ACT.Exp, bias=nb[:, t:t + 1], scale=m_ps[:, t:t + 1],
                       accum_out=rsum[:, t:t + 1]).then_inc(b_exp, 1)

            def b_raw_copies(h, first):
                for t in range(TT):
                    act.wait_ge(proj_done[t], h * (2, 2, 2, 1)[t] + (BS[2][t] + 1))
                    if t == 0:
                        if first:
                            act.wait_ge(m_out, 2 * M_HEADS)
                        else:
                            act.wait_ge(b_out, h)
                    A_(b_raw[:, t, :], banks[t][:, 0:384], ACT.Copy).then_inc(bank_empty[t], 1)

            def b_body(h, first, last):
                p = h * 2 + BS[0]
                split_hi(p, 1, h * 6 + (BS[1] + 3), 384, (3, BS[2][3]) if first else (2, h * 2 + BS[2][2]))
                if first:
                    m_exps(M_HEADS - 1)
                else:
                    b_exps(h - 1)
                split_hi(p + 1, 0, h * 6 + (BS[1] + 6), 384)
                b_raw_copies(h, first)
                split_hi(p + 1, 1, h * 6 + (BS[1] + 6), 384, (3, h + (BS[2][3] + 1)))
                if first:
                    act.wait_ge(m_y, 2 * M_HEADS)
                    act.wait_ge(xT_lo, 2 * (TT + MT))
                    split_y(yF)
                if last:
                    split_hi(p + 2, 0, AS[1] + 2, 512)
                else:
                    split_hi(p + 2, 0, h * 6 + (BS[1] + 9), 384)
                act.wait_ge(proj_done[0], h * 2 + (BS[2][0] + 2))
                if not first:
                    act.wait_ge(b_y, h)
                A_(b_zs, banks[0][:, :], ACT.Silu).then_inc(bank_empty[0], 1)
                act.wait_ge(proj_done[1], h * 2 + (BS[2][1] + 2))
                if not first:
                    act.wait_ge(bank_empty[2], h * 2 + BS[2][2])
                A_(sig[:, 0], banks[1][:, :], ACT.Sigmoid).then_inc(bank_empty[1], 1)
                act.wait_ge(b_turned, h * 2 + 1)
                A_(b_qT, att[0][:, :], ACT.Copy).then_inc(b_qcopied, 1)

            turns_of(act, steps, B_HEADS, 0, b_body)

            def a_norm(h):
                act.wait_ge(a_rinv, h + 1)
                for t in range(TT):
                    ins = A_(a_hn[:, t, :], att[t][:, 0:A_HD], ACT.Square, scale=a_ri[:, t:t + 1],
                             accum_out=a_ss[:, t:t + 1])
                ins.then_inc(a_ssq, 1)
                act.wait_ge(a_scale, h + 1)
                for t in range(TT):
                    A_(a_hn[:, t, :], att[t][:, 0:A_HD], ACT.Copy, scale=a_s[:, t:t + 1]).then_inc(a_hnd, 1)

            def a_weights(h):
                act.wait_ge(a_md_done, h + 1)
                for s in range(TT):
                    ins = A_(a_w[:, st_off(s):st_off(s) + P], a_md[:, s, :], ACT.Exp, bias=hcol[:, 0, s:s + 1])
                    if s < TT - 1:
                        A_(a_w[:, st_off(s) + P:st_off(s + 1)], att[0][:, (s + 1) * P:S], ACT.Exp,
                           bias=hcol[:, 0, s:s + 1])
                ins.then_inc(a_wdone, 1)

            def a_body(h, first, last):
                p = h * 3 + AS[0]
                loads = h * 5 + AS[1]
                split_hi(p, 1, loads + 2, 512, (2, AS[2][2]) if first else (3, h * 3 + AS[2][3]))
                if first:
                    b_exps(B_HEADS - 1)
                else:
                    a_norm(h - 1)
                split_hi(p + 1, 0, loads + 4, 512)
                for b in range(4):
                    act.wait_ge(bank_empty[b], h * 3 + (AS[2][b] + 1))
                    dst = (a_qT if b < 2 else a_kT)[:, b % 2, :]
                    A_(dst, a_conv[:, b % 2, :], ACT.Silu).then_inc(a_qk, 1)
                    if b == 1:
                        split_hi(p + 1, 1, loads + 4, 512, (3, h * 3 + (AS[2][3] + 1)))
                a_weights(h)
                split_hi(p + 2, 0, loads + 5, A_HD)
                for e in range(2):
                    act.wait_ge(proj_done[e], h * 3 + (AS[2][e] + 2))
                    A_(a_o[:, e, :], banks[e][:, :], ACT.Sigmoid).then_inc(bank_empty[e], 1)
                for e in range(2):
                    act.wait_ge(proj_done[2 + e], h * 3 + (AS[2][2 + e] + 2))
                    A_(a_oz[:, e, :], banks[2 + e][:, :], ACT.Silu).then_inc(bank_empty[2 + e], 1)
                split_hi(p + 2, 1, loads + 5, A_HD, (3, h * 3 + (AS[2][3] + 2)))
                if first:
                    act.wait_ge(b_y, B_HEADS)
                    split_y(yF)
                split_hi(p + 3, 0, loads + 7, 512)
                for t in range(TT):
                    act.wait_ge(proj_done[t], h * 3 + (AS[2][t] + 3))
                    A_(a_v[:, t, 0:A_HD], banks[t][:, 0:A_HD], ACT.Copy).then_inc(bank_empty[t], 1)

            turns_of(act, steps, A_HEADS, 0, a_body)

            def gates(sec, j, n):
                for b in range(2):
                    act.wait_ge(proj_done[b], j + (sec[2][b] + 1))
                    if not (isinstance(n, int) and n == 0):
                        act.wait_ge(g_merged, n * 2 + (b - 1))
                    A_(sig[:, b], banks[b][:, :], ACT.Sigmoid).then_inc(bank_empty[b], 1)

            def gb_body(sec, j, n, next_loads, before=1, between=None):
                p = j + sec[0]
                split_hi(p, 1, j * 2 + (sec[1] + 2), 512, (before, j + sec[2][before]))
                if n is None:
                    a_norm(A_HEADS - 1)
                    n = 0
                    act.wait_ge(bank_empty[2], AS[2][2])
                split_hi(p + 1, 0, next_loads, 512)
                if between:
                    between()
                gates(sec, j, n)

            gb_body(GB, 0, None, GB[1] + 4, 3)
            with act.Fori(1, 3) as j:
                gb_body(GB, j, j, j * 2 + (GB[1] + 4))

            def split_branch_a():
                act.wait_ge(a_y, 2 * A_HEADS)
                act.wait_ge(proj_done[3], GA[2][3])
                split_y(yF)

            def split_merged():
                act.wait_ge(g_merged, 14)
                act.wait_ge(proj_done[3], OUT[2][3])
                split_y(merged, range(KT - 2))

            gb_body(GB, 3, 3, GA[1] + 2, between=split_branch_a)
            with act.Fori(0, 3) as j:
                gb_body(GA, j, j + 4, j * 2 + (GA[1] + 4))
            gb_body(GA, 3, 7, OUT[1] + 1, between=split_merged)
            act.wait_ge(g_merged, 16)
            split_y(merged, range(KT - 2, KT))
            split_hi(OUT[0], 1, OUT[1] + 1, 512, (1, OUT[2][1]))
            split_hi(OUT[0] + 1, 0, OUT[1] + 2, 512)
            split_hi(OUT[0] + 1, 1, OUT[1] + 2, 512, (3, OUT[2][3] + 1))

        @block.vector
        def _(dve):
            V = nc.vector
            steps = Steps(dve, dve_step)
            then = steps.then

            def split_lo(p, kh, n):
                dve.wait_ge(w_hi_done, p * 2 + (kh + 1))
                V.tensor_tensor(w_lo[:, kh, :, 0:n], w_raw[:, kh, :, 0:n], w_hi[:, kh, :, 0:n].bitcast(F32),
                                ALU.subtract).then_inc(w_lo_done, 1)

            def split_y(src, times, tiles=range(KT)):
                for k in tiles:
                    dve.wait_ge(ys_hi, (times - 1) * KT + k + 1)
                    V.tensor_tensor(y_lo[:, k, :], src[:, k * S:(k + 1) * S], y_hi[:, k, :].bitcast(F32),
                                    ALU.subtract).then_inc(ys_lo, 1)

            V.memset(ones[:, :], 1.0)
            V.memset(minus_half[:, :], -0.5).then_inc(consts, 1)
            def x_variance(i):
                dve.wait_ge(x_ssq, i + 1)
                V.tensor_scalar(xss[:, i:i + 1], xss[:, i:i + 1], 1.0 / D, EPS, ALU.mult, ALU.add).then_inc(x_var, 1)

            def x_scale(i):
                dve.wait_ge(x_rstd, i + 1)
                if i == 0:
                    dve.wait_ge(g_landed, 16)
                if i == TT:
                    dve.wait_ge(small_landed, 16 * 6)
                if i >= 2:
                    dve.wait_ge(x_turned, 2 * (i - 1))
                src, g = (x_in[:, FIRST_TILES[i]], g_row) if i < TT else (mem_in[:, i - TT], memg_row)
                V.scalar_tensor_tensor(x_sc[:, i % 2, :], src, xrs[:, i:i + 1], g,
                                       ALU.mult, ALU.mult).then_inc(x_scaled, 1)

            def x_low(n):
                dve.wait_ge(xT_hi, n + 1)
                i, half = n // 2, n % 2
                hi, lo, c = (hT_hi, hT_lo, FIRST_TILES[i]) if i < TT else (memT_hi, memT_lo, i - TT)
                at = (slice(None), slice(half * 4, half * 4 + 4), slice(c * P, (c + 1) * P))
                V.tensor_tensor(lo[at], att[n % 4][:, :].rearrange("p (k n) -> p k n", k=4),
                                hi[at].bitcast(F32), ALU.subtract).then_inc(xT_lo, 1)

            x_variance(0)
            x_variance(1)
            x_scale(0)
            x_variance(2)
            x_scale(1)
            x_variance(3)
            x_scale(2)
            x_low(0)
            x_low(1)
            x_scale(3)
            split_lo(0, 0, 512)
            for n in range(2, 2 * TT):
                x_low(n)
            split_lo(0, 1, 512)
            for i in range(TT, TT + MT):
                x_variance(i)
                x_scale(i)
            for n in range(2 * TT, 2 * (TT + MT)):
                x_low(n)
            then(V.tensor_copy(pos_f, pos_i))
            for t in range(TT):
                ins = V.tensor_scalar(ang[:, t * 64:(t + 1) * 64], invf, pos_f[:, t:t + 1], None, ALU.mult)
            then(ins)
            then(V.tensor_scalar(turns, ang, INV_2PI, ROUNDER, ALU.mult, ALU.add))
            then(V.tensor_scalar(turns, turns, -ROUNDER, None, ALU.add))
            for part in (TWO_PI_HI, TWO_PI_MID, TWO_PI_LO):
                then(V.scalar_tensor_tensor(ang, turns, -part, ang, ALU.mult, ALU.add))
            then(V.tensor_scalar(turns, ang, float(np.pi / 2), float(-2 * np.pi), ALU.is_gt, ALU.mult))
            then(V.scalar_tensor_tensor(turns, ang, float(np.pi / 2), turns, ALU.add, ALU.add))
            then(V.tensor_scalar(turns, turns, PI_IN, -PI_IN, ALU.min, ALU.max))
            V.tensor_scalar(ang, ang, PI_IN, -PI_IN, ALU.min, ALU.max).then_inc(ang_ready, 1)

            dve.wait_ge(vec_turned, 1)
            V.tensor_copy(cols[:, :], att[0][:, 0:92]).then_inc(vec_copied, 1)
            dve.wait_ge(vec_copied, 1)
            V.tensor_tensor(gqk[:, :], cols[:, 88:90], cols[:, 90:92], ALU.mult).then_inc(vec_copied, 1)

            split_lo(1, 0, 80)
            dve.wait_ge(sincos, 2)
            for tab, src, src32 in ((0, cosd, cos32), (1, sind, sin32)):
                for half in range(2):
                    V.tensor_copy(src32[:, :, half * 32:(half + 1) * 32],
                                  src.rearrange("p t (i two) -> p t i two", two=2)[:, :, :, 0])
                for c in range(2):
                    for half in range(2):
                        g = gain_rows[:, c * P + half * 64:c * P + half * 64 + 64]
                        ins = V.tensor_tensor(tabs[:, tab, :, c * P + half * 64:c * P + half * 64 + 64], src,
                                              g.unsqueeze(1).to_broadcast([P, TT, 64]), ALU.mult)
            then(ins)

            def rotate(dst, a, b, src, cos, sin, heads):
                cb = cos.unsqueeze(1).to_broadcast([P, heads, I_HD])
                sb_ = sin.unsqueeze(1).to_broadcast([P, heads, I_HD])
                s3 = src.rearrange("p (h d) -> p h d", h=heads)
                V.tensor_tensor(a.rearrange("p (h d) -> p h d", h=heads), s3, cb, ALU.mult)
                return V.tensor_tensor(b.rearrange("p (h d) -> p h d", h=heads), s3, sb_, ALU.mult)

            def join(a, b, heads, half):
                a4 = a.rearrange("p (h two d) -> p h two d", h=heads, two=2)
                b4 = b.rearrange("p (h two d) -> p h two d", h=heads, two=2)
                V.tensor_tensor(a4[:, :, 0], a4[:, :, 0], b4[:, :, 1], ALU.subtract)
                return V.tensor_tensor(a4[:, :, 1], a4[:, :, 1], b4[:, :, 0], ALU.add)

            for t in range(1, TT):
                dve.wait_ge(proj_done[t], 1)
                if t > 1:
                    dve.wait_ge(qi_rotated, t - 1)
                a = qi_rot[:, t - 1, :]
                ins = rotate(None, a, qi_b, banks[t][:, :], cos32[:, t], sin32[:, t], I_HEADS)
                ins.then_inc(bank_empty[t], 1)
                dve.wait_ge(bank_empty[t], 1)
                join(a, qi_b, I_HEADS, 32).then_inc(qi_rotated, 1)
                if t == 1:
                    split_lo(1, 1, 80)
            split_lo(2, 0, 512)
            dve.wait_ge(qi_rotated, 3)
            for t in range(TT):
                dve.wait_ge(proj_done[t], IDX2[2][t] + 1)
                dve.wait_ge(gates_copied, t + 1)
                a, b = ki_rot[:, t, 0:I_HD], qi_b[:, 0:I_HD]
                then(rotate(None, a, b, banks[t][:, 0:I_HD], cos32[:, t], sin32[:, t], 1))
                then(join(a, b, 1, 32))
                V.tensor_copy(ki_rot[:, t, I_HD:2 * I_HD], a).then_inc(bank_empty[t], 1)

            def gate_in():
                dve.wait_ge(gates_turned, 1)
                then(V.tensor_scalar(rows[:, 0], att[0][0:A_HEADS, :], gate_b[:, 0:1], None, ALU.add))
                V.tensor_scalar(rows[:, 1], att[1][0:A_HEADS, :], gate_b[:, 1:2], None, ALU.add).then_inc(gates_read, 1)
                dve.wait_ge(gates_read, 1)
                V.scalar_tensor_tensor(rows[:, 2], rows[:, 1], -1.0, rows[:, 1], ALU.mult, ALU.max).then_inc(gate_abs, 1)

            def gate_scans():
                dve.wait_ge(gate_ln, 1)
                then(V.scalar_tensor_tensor(rows[:, 1], rows[:, 1], 0.0, rows[:, 3], ALU.min, ALU.subtract))
                then(V.memset(rows[:, 2], 1.0))
                then(V.tensor_tensor_scan(rows[:, 3], rows[:, 2], rows[:, 1], 0.0, ALU.mult, ALU.add))
                then(V.tensor_tensor(rows[:, 0], rows[:, 0], rows[:, 3], ALU.subtract))
                then(V.tensor_tensor_scan(maxrow, rows[:, 0], rows[:, 0], 0.0, ALU.max, ALU.max))
                V.tensor_tensor(rows[:, 1], rows[:, 3], maxrow, ALU.add).then_inc(gate_rows, 1)

            def sums(i, part):
                for u in range(8 * i + 4 * part, 8 * i + 4 * part + 4):
                    t, h = u // 8 + 1, u % 8
                    acc = score[:, off(t):off(t + 1)]
                    dve.wait_ge(relued, u + 1)
                    r = relu[:, u % 2, 0:(t + 1) * P]
                    if h == 0:
                        V.tensor_scalar(acc, r, wi8[:, t, 0:1], None, ALU.mult).then_inc(summed, 1)
                    else:
                        V.scalar_tensor_tensor(acc, r, wi8[:, t, h:h + 1], acc, ALU.mult, ALU.add).then_inc(summed, 1)
                    dve.wait_ge(summed, u + 1)
                if part == 1:
                    then(V.memset(score[0:64, off(t) + t * P + 64:off(t + 1)], NEG))

            for i in range(4):
                p = KV[0] + i
                split_lo(p, 1, 512)
                if i == 0:
                    gate_in()
                    dve.wait_ge(idx_turned, 4)
                    V.tensor_copy(kiT, att[3][:, :]).then_inc(ki_copied, 1)
                else:
                    sums(i - 1, 0)
                split_lo(p + 1, 0, 512)
                if i:
                    sums(i - 1, 1)
                if i == 1:
                    gate_scans()
                if i == 2:
                    dve.wait_ge(km_squared, 1)
                    then(V.tensor_reduce(kss, km_sq.rearrange("p (g n) -> p g n", n=M_HD), AX, ALU.add))
                    V.tensor_scalar(kss, kss, 1.0 / M_HD, EPS, ALU.mult, ALU.add).then_inc(km_var, 1)

            def held(cell=0):
                if steps.turn is not None:
                    V.memset(scratch[:, cell:cell + 1], 0.0)

            def top_round(t):
                row = score[:, off(t):off(t + 1)]
                held()
                then(V.max(top8, row))
                held()
                then(V.match_replace(row, top8, row, TAKEN))

            def make_mask(t):
                V.tensor_scalar(negmask[:, off(t):off(t + 1)], score[:, off(t):off(t + 1)], 0.5 * TAKEN, NEG,
                                ALU.is_gt, ALU.mult)

            def m_norms(h):
                dve.wait_ge(m_ssq, h + 1)
                V.tensor_scalar(m_var, att[0][:, 0:TT], 1.0 / M_HD, EPS, ALU.mult, ALU.add).then_inc(m_varred, 1)
                dve.wait_ge(m_scores, h * 2 + 1)
                V.reduce_max(mx[:, 0:2], att[1][:, :].rearrange("p (t n) -> p t n", t=2), AX)
                dve.wait_ge(m_scores, h * 2 + 2)
                V.reduce_max(mx[:, 2:4], att[2][:, :].rearrange("p (t n) -> p t n", t=2), AX)
                dve.wait_ge(m_rstd, h + 1)
                V.tensor_scalar(m_ps, m_rs, M_HD ** -0.5, None, ALU.mult)
                then(V.tensor_scalar(m_ns, m_rs, -(M_HD ** -0.5), None, ALU.mult))
                V.tensor_tensor(nb, mx, m_ns, ALU.mult).then_inc(m_bias, 1)

            def m_probs(h):
                for g in range(2):
                    dve.wait_ge(m_pturned, h * 2 + (g + 1))
                    V.tensor_copy(m_pT[:, 2 * g:2 * g + 2, :].rearrange("p t n -> p (t n)"), att[3 - 3 * g][:, :])\
                        .then_inc(m_pcopied, 1)

            def m_rest(h):
                dve.wait_ge(m_exp, h * 4 + 4)
                then(V.reciprocal(rinv, rsum))
                for g in range(2):
                    dve.wait_ge(m_out, h * 2 + (g + 1))
                    V.tensor_tensor(m_on[:, 2 * g:2 * g + 2, :], att[1 + g][:, :].rearrange("p (t n) -> p t n", t=2),
                                    rinv[:, 2 * g:2 * g + 2].unsqueeze(2).to_broadcast([P, 2, M_HD]),
                                    ALU.mult).then_inc(m_scaled, 1)
                dve.wait_ge(bank_empty[3], h + (MS[2][3] + 1))
                for e in range(2):
                    dve.wait_ge(m_oturned, h * 2 + (e + 1))
                    V.tensor_tensor(yF[:, bass.ds(h * (2 * S) + e * S, S)], att[3 - 3 * e][:, :], m_zs[:, e, :],
                                    ALU.mult).then_inc(m_y, 1)

            def m_body(h, first, last):
                p = h + MS[0]
                split_lo(p, 1, 512)
                if first:
                    dve.wait_ge(gate_back, 1)
                    V.tensor_copy(gcols, att[0][:, 0:2 * TT * A_HEADS]
                                  .rearrange("p (k t h) -> p k h t", k=2, t=TT)).then_inc(gate_cols, 1)
                    dve.wait_ge(km_rstd, 1)
                    km3 = km_raw.rearrange("p (g n) -> p g n", n=M_HD)
                    V.tensor_tensor(km3, km3, krs.unsqueeze(2).to_broadcast([P, MT * M_HEADS, M_HD]),
                                    ALU.mult).then_inc(km_normed, 1)
                else:
                    m_norms(h - 1)
                tile = 1 if first else 2 if last else 3
                rounds = 16 if first or last else 8
                for r in range(rounds // 2):
                    top_round(tile)
                if not first:
                    m_probs(h - 1)
                split_lo(p + 1, 0, 384 if last else 512)
                if not first:
                    m_rest(h - 1)
                for r in range(rounds // 2):
                    top_round(tile)

            turns_of(dve, steps, M_HEADS, M_PER, m_body)
            then(V.memset(negmask[:, 0:P], 0.0))
            for t in range(1, TT):
                make_mask(t)
            then(V.memset(negmask[0:64, 64:P], NEG))

            def b_maxes(h):
                for t in range(TT):
                    dve.wait_ge(b_scores, h * 4 + (t + 1))
                    held(t)
                    V.tensor_tensor_reduce(out=score[:, off(t):off(t + 1)], in0=att[(t + 2) % 4][:, 0:(t + 1) * P],
                                           in1=negmask[:, off(t):off(t + 1)], scale=1.0, scalar=LOWEST,
                                           op0=ALU.add, op1=ALU.max, accum_out=mx[:, t:t + 1]).then_inc(b_masked, 1)
                dve.wait_ge(b_masked, h * 4 + 4)
                V.tensor_tensor(nb, mx, m_ns, ALU.mult).then_inc(b_bias, 1)

            def b_probs(h):
                for t in range(TT):
                    dve.wait_ge(b_pturned, h * 4 + (t + 1))
                    V.tensor_copy(b_pT[:, off(t):off(t + 1)], att[(t + 2) % 4][:, 0:(t + 1) * P]).then_inc(b_pcopied, 1)
                dve.wait_ge(b_exp, h * 4 + 4)
                then(V.reciprocal(rinv, rsum))

            def b_outs(h):
                dve.wait_ge(b_out, h + 1)
                V.tensor_tensor(b_on, att[2][:, :].rearrange("p (t n) -> p t n", t=TT),
                                rinv.unsqueeze(2).to_broadcast([P, TT, P]), ALU.mult).then_inc(b_scaled, 1)

            def b_finish(h):
                dve.wait_ge(b_oturned, h + 1)
                dve.wait_ge(bank_empty[0], h * 2 + (BS[2][0] + 2))
                V.tensor_tensor(yF[:, bass.ds(h * S, S)], att[3][:, :], b_zs, ALU.mult).then_inc(b_y, 1)

            def b_rotary(h):
                dve.wait_ge(b_squared, h + 1)
                then(V.tensor_reduce(b_var, b_sq.rearrange("p (g n) -> p g n", n=P), AX, ALU.add))
                V.tensor_scalar(b_var, b_var, 1.0 / B_HD, EPS, ALU.mult, ALU.add).then_inc(b_varred, 1)
                for tab, dst in ((0, b_rc), (1, b_rs)):
                    ins = V.tensor_tensor(dst.rearrange("p (t n) -> p t n", t=TT), b_raw[:, :, 0:2 * P],
                                          tabs[:, tab], ALU.mult)
                then(ins)
                then(join(b_rc, b_rs, 2 * TT, 64))
                dve.wait_ge(b_rstded, h + 1)
                r2 = b_rstd.rearrange("p (t c) -> p t c", c=2)
                keys = b_rc.rearrange("p (t c n) -> p t c n", t=TT, c=2)[:, :, 1]
                V.tensor_tensor(keys, keys, r2[:, :, 1:2].to_broadcast([P, TT, P]), ALU.mult).then_inc(b_rotated, 1)
                V.tensor_scalar(m_ps, r2[:, :, 0], B_HD ** -0.5, None, ALU.mult)
                then(V.tensor_scalar(m_ns, r2[:, :, 0], -(B_HD ** -0.5), None, ALU.mult))

            def b_body(h, first, last):
                p = h * 2 + BS[0]
                split_lo(p, 1, 384)
                if first:
                    m_norms(M_HEADS - 1)
                else:
                    b_maxes(h - 1)
                if first:
                    m_probs(M_HEADS - 1)
                split_lo(p + 1, 0, 384)
                if first:
                    m_rest(M_HEADS - 1)
                else:
                    b_probs(h - 1)
                    b_outs(h - 1)
                split_lo(p + 1, 1, 384)
                if first:
                    split_y(yF, 1)
                else:
                    b_finish(h - 1)
                b_rotary(h)
                split_lo(p + 2, 0, 512 if last else 384)
                dve.wait_ge(b_turned, h * 2 + 2)
                V.tensor_copy(b_kT, att[1][:, :]).then_inc(b_kcopied, 1)
                dve.wait_ge(bank_empty[1], h * 2 + (BS[2][1] + 2))
                dve.wait_ge(proj_done[2], h * 2 + (BS[2][2] + 2))
                V.tensor_tensor(merged[:, bass.ds(h * S, S)], banks[2][:, :], sig[:, 0], ALU.mult)\
                    .then_inc(bank_empty[2], 1)

            turns_of(dve, steps, B_HEADS, B_PER, b_body)

            def a_conv_all(h):
                for b in range(4):
                    dve.wait_ge(proj_done[b], h * 3 + (AS[2][b] + 1))
                    if b >= 2:
                        dve.wait_ge(a_qk, h * 4 + (b - 1))
                    u, acc = banks[b], a_conv[:, b % 2, :]
                    then(V.tensor_scalar(acc, u[:, :], hcw[:, 3, b:b + 1], hcw[:, 4, b:b + 1], ALU.mult, ALU.add))
                    for lag in range(1, CONV):
                        ins = V.scalar_tensor_tensor(acc[:, lag:], u[:, 0:S - lag],
                                                     hcw[:, CONV - 1 - lag, b:b + 1], acc[:, lag:],
                                                     ALU.mult, ALU.add)
                        if lag < CONV - 1:
                            then(ins)
                    ins.then_inc(bank_empty[b], 1)

            def a_load_params(h, first):
                if not first:
                    dve.wait_ge(a_y, h * 2)
                cw = cols[:, 0:80].rearrange("p (j c e) -> p j c e", j=5, c=2)
                V.tensor_copy(hcw.rearrange("p j (c e) -> p j c e", c=2), cw[:, :, :, bass.ds(h * 2, 2)])
                V.tensor_copy(hcol, gcols.rearrange("p k h t -> p k (h t)")[:, :, bass.ds(h * TT, TT)])
                V.tensor_copy(pick[:, 0, :], pick.rearrange("p h n -> p (h n)")[:, bass.ds(h * P, P)])
                V.tensor_copy(hg, cols[:, bass.ds(h * 2 + 80, 2)]).then_inc(a_params, 1)
                dve.wait_ge(a_params, h + 1)

            def a_denominators(h):
                dve.wait_ge(a_num, h * 4 + 4)
                for t in range(TT):
                    ins = V.tensor_scalar(a_den[:, t:t + 1], att[t][:, A_HD:A_HD + 1], -1.0, hcol[:, 1, t:t + 1],
                                          ALU.mult, ALU.max)
                then(ins)
                for t in range(TT):
                    ins = V.tensor_tensor(a_den[:, t:t + 1], att[t][:, A_HD:A_HD + 1], a_den[:, t:t + 1], ALU.max)
                then(ins)
                V.reciprocal(a_ri, a_den).then_inc(a_rinv, 1)
                dve.wait_ge(a_ssq, h + 1)
                V.tensor_scalar(a_ss, a_ss, 1.0 / A_HD, EPS, ALU.mult, ALU.add).then_inc(a_var, 1)
                dve.wait_ge(a_rstd, h + 1)
                V.tensor_tensor(a_s, a_ri, a_den, ALU.mult).then_inc(a_scale, 1)

            def a_finish(h):
                dve.wait_ge(a_ozd, h + 1)
                for e in range(2):
                    dve.wait_ge(a_turned, h * 2 + (e + 1))
                    V.scalar_tensor_tensor(yF[:, bass.ds(h * (2 * S) + e * S, S)], att[e][:, :], hg[:, e:e + 1],
                                           a_oz[:, e, :], ALU.mult, ALU.mult).then_inc(a_y, 1)

            def a_body(h, first, last):
                p = h * 3 + AS[0]
                split_lo(p, 1, 512)
                if first:
                    b_maxes(B_HEADS - 1)
                    b_probs(B_HEADS - 1)
                    split_lo(p + 1, 0, 512)
                    b_outs(B_HEADS - 1)
                    b_finish(B_HEADS - 1)
                    dve.wait_ge(em_done, 1)
                else:
                    a_denominators(h - 1)
                    split_lo(p + 1, 0, 512)
                    a_finish(h - 1)
                a_load_params(h, first)
                a_conv_all(h)
                split_lo(p + 1, 1, 512)
                dve.wait_ge(a_spread, h + 1)
                V.tensor_tensor(a_md, att[0][:, :].rearrange("p (t n) -> p t n", t=TT),
                                causal[:, :].unsqueeze(1).to_broadcast([P, TT, P]), ALU.add).then_inc(a_md_done, 1)
                split_lo(p + 2, 0, A_HD)
                dve.wait_ge(a_wdone, h + 1)
                for s in range(TT):
                    dve.wait_ge(a_st, h * 4 + min(s + 1 + s // 2, 4))
                    bank, c = ((1, 0), (2, 0), (3, 0), (3, 2 * P))[s]
                    n = S - s * P
                    V.scalar_tensor_tensor(a_at[:, st_off(s):st_off(s) + n], att[bank][:, c:c + n], A_HD ** -0.5,
                                           a_w[:, st_off(s):st_off(s) + n], ALU.mult, ALU.mult).then_inc(a_atd, 1)
                split_lo(p + 2, 1, A_HD)
                if first:
                    split_y(yF, 2)
                    V.memset(a_v[:, :, A_HD:A_HD + 1], 1.0).then_inc(ones_set, 1)
                split_lo(p + 3, 0, 512)

            turns_of(dve, steps, A_HEADS, A_PER, a_body)

            def gb_merge(sec, j, n):
                for b in range(2):
                    dve.wait_ge(bank_empty[b], j + (sec[2][b] + 1))
                    dve.wait_ge(proj_done[2 + b], j + (sec[2][2 + b] + 1))
                    V.tensor_tensor(sig[:, b], banks[2 + b][:, :], sig[:, b], ALU.mult).then_inc(bank_empty[2 + b], 1)
                    dve.wait_ge(bank_empty[2 + b], j + (sec[2][2 + b] + 1))
                    m = merged[:, bass.ds(j * (2 * S) + b * S, S)]
                    V.tensor_tensor(m, m, sig[:, b], ALU.add).then_inc(g_merged, 1)

            split_lo(GB[0], 1, 512)
            a_denominators(A_HEADS - 1)
            split_lo(GB[0] + 1, 0, 512)
            a_finish(A_HEADS - 1)
            gb_merge(GB, 0, 0)

            def gb_body(sec, j, n, between=None):
                split_lo(j + sec[0], 1, 512)
                split_lo(j + (sec[0] + 1), 0, 512)
                if between:
                    between()
                gb_merge(sec, j, n)

            with dve.Fori(1, 3) as j:
                gb_body(GB, j, j)
            gb_body(GB, 3, 3, lambda: split_y(yF, 3))
            with dve.Fori(0, 3) as j:
                gb_body(GA, j, j + 4)
            gb_body(GA, 3, 7, lambda: split_y(merged, 4, range(KT - 2)))
            split_y(merged, 4, range(KT - 2, KT))
            split_lo(OUT[0], 1, 512)
            split_lo(OUT[0] + 1, 0, 512)
            dve.wait_ge(x_again, 16 * TT)
            for c in range(2):
                for t in range(TT):
                    dve.wait_ge(proj_done[t], OUT[2][t] + c + 1)
                    o = x_in[:, t, c * 512:(c + 1) * 512]
                    V.tensor_tensor(o, banks[t][:, :], o, ALU.add).then_inc(bank_empty[t], 1)
                if c == 0:
                    split_lo(OUT[0] + 1, 1, 512)

        @block.gpsimd
        def _(pool):
            G = nc.gpsimd
            steps = Steps(pool, pool_step)
            G.memset(ident[:, :], 0.0)
            G.memset(causal[:, :], 0.0)
            steps.then(G.memset(pick[:, :, :], 0.0))
            G.affine_select(out=ident[:, :], in_=ident[:, :], compare_op=ALU.not_equal, fill=1.0, base=0,
                            pattern=[[-1, P]], channel_multiplier=1).then_inc(consts, 1)
            G.affine_select(out=causal[:, :], in_=causal[:, :], compare_op=ALU.is_ge, fill=NEG, base=0,
                            pattern=[[1, P]], channel_multiplier=-1).then_inc(consts, 1)
            G.affine_select(out=pick[:, :, :], in_=pick[:, :, :], compare_op=ALU.not_equal, fill=-1.0, base=0,
                            pattern=[[-1, A_HEADS], [0, P]], channel_multiplier=1).then_inc(consts, 1)
            pool.wait_ge(consts, 4)
            for t in range(TT + MT):
                pool.wait_ge(x_var, t + 1)
                G.tensor_tensor(xrs[:, t:t + 1], xss[:, t:t + 1], minus_half[:, 0:1], ALU.pow).then_inc(x_rstd, 1)
            for b in range(4):
                pool.wait_ge(bank_empty[b], KV[2][b] + 1)
            pool.wait_ge(idx_turned, 4)
            G.tensor_tensor(km_sq, km_raw, km_raw, ALU.mult).then_inc(km_squared, 1)
            pool.wait_ge(km_var, 1)
            G.tensor_tensor(krs, kss, minus_half[:, 0:8], ALU.pow).then_inc(km_rstd, 1)
            with pool.Fori(0, M_HEADS) as h:
                pool.wait_ge(bank_empty[1], h + (MS[2][1] + 1))
                G.tensor_tensor(m_sq[:, 0, :], m_sq[:, 0, :], m_sq[:, 1, :], ALU.add).then_inc(m_added, 1)
                pool.wait_ge(m_varred, h + 1)
                G.tensor_tensor(m_rs, m_var, minus_half[:, 0:TT], ALU.pow).then_inc(m_rstd, 1)
            with pool.Fori(0, B_HEADS) as h:
                pool.wait_ge(bank_empty[3], h + (BS[2][3] + 1))
                qk = b_raw[:, :, 0:2 * P]
                G.tensor_tensor(b_sq.rearrange("p (t n) -> p t n", t=TT), qk, qk, ALU.mult).then_inc(b_squared, 1)
                pool.wait_ge(b_varred, h + 1)
                G.tensor_tensor(b_rstd, b_var, minus_half[:, 0:8], ALU.pow).then_inc(b_rstded, 1)

            def a_powers(h):
                pool.wait_ge(a_var, h + 1)
                G.tensor_tensor(a_den, a_ss, minus_half[:, 0:TT], ALU.pow).then_inc(a_rstd, 1)

            def a_gate(h):
                pool.wait_ge(bank_empty[3], h * 3 + (AS[2][3] + 2))
                G.tensor_tensor(a_oz, a_o, a_oz, ALU.mult).then_inc(a_ozd, 1)

            a_gate(0)
            with pool.Fori(1, A_HEADS) as h:
                a_powers(h - 1)
                a_gate(h)
            a_powers(A_HEADS - 1)


M_PER, B_PER, A_PER = 18, 5, 14

_INS = ['x', 'mem', 'positions', 'norm_g', 'mem_norm_g', 'w_in', 'conv_w', 'conv_b', 'mlstm_gate_b',
        'mlstm_norm_g', 'dsa_q_norm_g', 'dsa_k_norm_g', 'mem_q_norm_g', 'mem_k_norm_g', 'w_mem_kv',
        'w_branch', 'w_out']


def kernel(**inputs):
    import concourse.bacc as bacc
    from concourse.bass_utils import run_bass_kernel_spmd as run

    nc = bacc.Bacc("TRN2", target_bir_lowering=False, num_devices=1)
    arrays, args = {}, []
    for name in _INS:
        arrays[name] = np.ascontiguousarray(inputs[name])
    half = B_HD // 2
    arrays['inv_freq'] = (ROPE_THETA ** (-np.arange(half) / half)).astype(np.float32)[None, :]
    for name, a in arrays.items():
        args.append(nc.dram_tensor(name + "_in", a.shape, mybir.dt.from_np(a.dtype), kind="ExternalInput").ap())
    out = nc.dram_tensor("out", (1, S, D), F32, kind="ExternalOutput").ap()
    hybrid_block(nc, *args, out)
    r = run(nc, [{name + "_in": a for name, a in arrays.items()}], core_ids=[0])
    return r.results[0]["out"]
```

```python
from contextlib import ExitStack

import numpy as np

import concourse.bass as bass
from concourse import mybir

F32 = mybir.dt.float32
F32R = mybir.dt.float32r
I32 = mybir.dt.int32
ALU = mybir.AluOpType
ACT = mybir.ActivationFunctionType
AX = mybir.AxisListType.X

P = 128
S = 512
D = 1024
TT = S // P
KT = D // P
KH = KT // 2
MEM = 256
MT = MEM // P
CONV = 4
FIRST_TILES = (1, 2, 3, 0)
A_HEADS, A_HD = 4, 256
B_HEADS, B_HD = 8, 128
I_HEADS, I_HD = 8, 64
M_HEADS, M_HD = 4, 256
TOPK = 128
EPS = 1e-6
ROPE_THETA = 10000.0

C_QA = 0
C_KA = C_QA + D
C_VA = C_KA + D
C_IF = C_VA + D
C_OA = C_IF + 2 * A_HEADS
C_ZA = C_OA + D
C_QB = C_ZA + D
C_ZB = C_QB + 3 * D
C_QI = C_ZB + D
C_KI = C_QI + I_HEADS * I_HD
C_QM = C_KI + I_HD + I_HEADS
I_COLS = I_HD + I_HEADS + 2 * A_HEADS
C_ZM = C_QM + D
C_GATE = C_ZM + D

NEG = -1.0e30
TAKEN = -3.0e38
LOWEST = -3.0e38
INV_2PI = float(np.float32(1.0 / (2.0 * np.pi)))
ROUNDER = 1.5 * 2.0 ** 23
TWO_PI_HI = 6.28125
TWO_PI_MID = float(np.float32(np.floor((2 * np.pi - TWO_PI_HI) * 2 ** 20) / 2 ** 20))
TWO_PI_LO = float(np.float32(2 * np.pi - TWO_PI_HI - TWO_PI_MID))
PI_IN = 3.1415925


def off(t):
    return P * t * (t + 1) // 2


def st_off(s):
    return sum(S - P * r for r in range(s))


class Panels:

    def __init__(self):
        self.panel, self.loads, self.uses = 0, 0, [0, 0, 0, 0]

    def take(self, panels, loads, banks):
        start = (self.panel, self.loads, tuple(self.uses))
        self.panel += panels
        self.loads += loads
        self.uses = [u + b for u, b in zip(self.uses, banks)]
        return start


_plan = Panels()
IDX1 = _plan.take(1, 1, (0, 1, 1, 1))
IDX2 = _plan.take(1, 0, (1, 0, 0, 0))
KV = _plan.take(4, 4, (2, 2, 2, 2))
MS = _plan.take(M_HEADS, 2 * M_HEADS, (M_HEADS,) * 4)
BS = _plan.take(2 * B_HEADS, 6 * B_HEADS, (2 * B_HEADS, 2 * B_HEADS, 2 * B_HEADS, B_HEADS))
AS = _plan.take(3 * A_HEADS, 5 * A_HEADS, (3 * A_HEADS,) * 4)
GB = _plan.take(4, 8, (4,) * 4)
GA = _plan.take(4, 8, (4,) * 4)
OUT = _plan.take(2, 2, (2,) * 4)


class Steps:

    def __init__(self, eng, sem):
        self.eng, self.sem, self.n, self.turn, self.base, self.per = eng, sem, 0, None, 0, 0

    def value(self):
        if self.turn is None:
            return self.n
        return self.turn * self.per + (self.base + self.n)

    def then(self, instruction):
        instruction.then_inc(self.sem, 1)
        self.n += 1
        self.eng.wait_ge(self.sem, self.value())

    def enter(self, turn, first, per):
        self.turn, self.per, self.base, self.entered = turn, per, self.n - first * per, self.n
        self.n = 0

    def leave(self, turns):
        assert self.n == self.per, (self.n, self.per)
        self.n = self.entered + turns * self.per
        self.turn = None


def hybrid_block(nc, x, mem, positions, norm_g, mem_norm_g, w_in, conv_w, conv_b, mlstm_gate_b,
                 mlstm_norm_g, dsa_q_norm_g, dsa_k_norm_g, mem_q_norm_g, mem_k_norm_g,
                 w_mem_kv, w_branch, w_out, inv_freq, out):
    ctx = ExitStack()
    with ctx:
        def sb(name, shape, dt=F32):
            return ctx.enter_context(nc.sbuf_tensor(name, shape, dt))

        def sem(name):
            return ctx.enter_context(nc.semaphore(name))

        hT_hi = sb("hT_hi", [P, KT, S], F32R)
        hT_lo = sb("hT_lo", [P, KT, S], F32R)
        w_raw = sb("w_raw", [P, 2, KH, S])
        w_hi = sb("w_hi", [P, 2, KH, S], F32R)
        w_lo = sb("w_lo", [P, 2, KH, S], F32R)
        y_hi = sb("y_hi", [P, KT, S], F32R)
        y_lo = sb("y_lo", [P, KT, S], F32R)
        yF = sb("yF", [P, KT * S])
        merged = sb("merged", [P, KT * S])
        ident = sb("ident", [P, P])
        causal = sb("causal", [P, P])
        pick = sb("pick", [A_HEADS, A_HEADS, P])
        ones = sb("ones", [P, 1])
        minus_half = sb("minus_half", [P, 8])
        cols = sb("cols", [P, 92])
        gqk = sb("gqk", [P, 2])
        negmask = sb("negmask", [P, off(TT)])
        score = sb("score", [P, off(TT)])
        tabs = sb("tabs", [P, 2, TT, 2 * P])
        sig = sb("sig", [P, 2, S])
        arena = sb("arena", [P, 9216])
        maxrow = sig[0:A_HEADS, 1, :]
        small = sb("small", [P, 192])

        x_in = yF[:, :].rearrange("p (t n) -> p t n", t=TT)
        mem_in = merged[:, 0:MT * D].rearrange("p (t n) -> p t n", t=MT)
        g_row = arena[:, 0:D]
        memg_row = arena[:, D:2 * D]
        x_sc = arena[:, 2 * D:4 * D].rearrange("p (b n) -> p b n", b=2)
        junk = arena[:, 4 * D:5 * D]
        idx2_raw = arena[:, 8 * D - 2 * KH * I_COLS:8 * D].rearrange("p (h k n) -> p h k n", h=2, k=KH)
        vec_rows = arena[0:92, 5 * D:5 * D + P]
        gain_rows = arena[:, 7 * D + P:7 * D + 3 * P]
        memT_hi = y_hi
        memT_lo = y_lo
        kiT = [y[:, 0:2, MEM:] for y in (y_hi, y_lo)]
        qiT = [[y[:, 2 * t:2 * t + 2, MEM:] for t in range(1, TT)] for y in (y_hi, y_lo)]
        relu = yF[:, 2048:3072].rearrange("p (b n) -> p b n", b=2)
        cos32 = yF[:, 3072:3328].rearrange("p (t n) -> p t n", t=TT)
        sin32 = yF[:, 3328:3584].rearrange("p (t n) -> p t n", t=TT)
        ki_rot = yF[:, 3584:4096].rearrange("p (t n) -> p t n", t=TT)
        ang = arena[:, 6 * D:6 * D + 256]
        turns = arena[:, 6 * D + 256:6 * D + 512]
        cosd = arena[:, 6 * D + 512:6 * D + 768].rearrange("p (t n) -> p t n", t=TT)
        sind = arena[:, 6 * D + 768:7 * D].rearrange("p (t n) -> p t n", t=TT)
        invf = arena[:, 7 * D:7 * D + 64]
        pos_i = small[:, 0:4].bitcast(I32)
        pos_f = small[:, 4:8]
        qi_rot = arena[:, 4 * D:4 * D + 1536].rearrange("p (t n) -> p t n", t=3)
        qi_b = arena[:, 8 * D:8 * D + 512]
        kiF = arena[0:I_COLS, 8 * D + 512:9 * D]
        km_raw = merged[:, 2048:4096]
        km_sq = arena[:, 4096:6144]
        rows = merged[0:A_HEADS, 0:2048].rearrange("p (r n) -> p r n", r=4)
        kmT = arena[:, 0:2048].rearrange("p (h n) -> p h n", h=M_HEADS)
        vm = arena[:, 2048:4096].rearrange("p (m n) -> p m n", m=MT)
        m_qT = arena[:, 4096:5120].rearrange("p (e n) -> p e n", e=2)
        m_sq = arena[:, 5120:6144].rearrange("p (e n) -> p e n", e=2)
        m_p = m_sq[:, :, :].rearrange("p e n -> p (e n)").rearrange("p (t n) -> p t n", t=TT)
        m_pT = arena[:, 6144:7168].rearrange("p (m n) -> p m n", m=MT)
        m_vh = arena[:, 7168:7680].rearrange("p (m n) -> p m n", m=MT)
        m_zs = arena[:, 8192:9216].rearrange("p (e n) -> p e n", e=2)
        b_raw = arena[:, 0:1536].rearrange("p (t n) -> p t n", t=TT)
        b_rc = arena[:, 4096:5120]
        b_rs = arena[:, 2048:3072]
        b_qT = arena[:, 3072:3584]
        b_kT = arena[:, 3584:4096]
        b_pT = arena[:, 5120:7168].rearrange("p (s n) -> p s n", s=TT)
        b_zs = arena[:, 8192:8704]
        b_sq = arena[:, 7168:8192]
        a_qT = tabs[:, 0, :, :].rearrange("p t n -> p (t n)").rearrange("p (e n) -> p e n", e=2)
        a_kT = tabs[:, 1, :, :].rearrange("p t n -> p (t n)").rearrange("p (e n) -> p e n", e=2)
        a_conv = negmask[:, 0:1024].rearrange("p (b n) -> p b n", b=2)
        a_v = arena[:, 0:TT * (A_HD + 1)].rearrange("p (t n) -> p t n", t=TT)
        a_w = arena[:, 1028:2308]
        a_at = arena[:, 2308:3588]
        a_md = arena[:, 3588:4100].rearrange("p (t n) -> p t n", t=TT)
        a_hn = arena[:, 4100:5124].rearrange("p (t n) -> p t n", t=TT)
        a_o = arena[:, 5124:6148].rearrange("p (e n) -> p e n", e=2)
        a_oz = arena[:, 6148:7172].rearrange("p (e n) -> p e n", e=2)
        xss, xrs = small[:, 8:14], small[:, 14:20]
        kss, krs = small[:, 20:28], small[:, 28:36]
        wi8 = small[:, 36:68].rearrange("p (t n) -> p t n", t=TT)
        ifr = small[:, 68:100].rearrange("p (t n) -> p t n", t=TT)
        top8 = small[:, 100:108]
        gcols = small[:, 108:140].rearrange("p (k h t) -> p k h t", k=2, h=A_HEADS)
        m_var, m_rs, m_ps, m_ns = (small[:, 140 + 4 * j:144 + 4 * j] for j in range(4))
        mx, nb, rsum, rinv = (small[:, 156 + 4 * j:160 + 4 * j] for j in range(4))
        b_var, b_rstd = small[:, 172:180], small[:, 180:188]
        gate_b = small[0:A_HEADS, 188:190]
        small2 = sb("small2", [P, 52])
        hcw = small2[:, 0:20].rearrange("p (j b) -> p j b", j=5)
        hcol = small2[:, 20:28].rearrange("p (k t) -> p k t", k=2)
        hg = small2[:, 28:30]
        a_den, a_ri, a_ss, a_s = (small2[:, 30 + 4 * j:34 + 4 * j] for j in range(4))
        scratch = small2[0:1, 48:52]

        banks = [ctx.enter_context(nc.psum_tensor(f"proj{b}", [P, S], F32)) for b in range(4)]
        att = [ctx.enter_context(nc.psum_tensor(f"att{b}", [P, S], F32)) for b in range(4)]

        x_landed = [sem(f"x_landed{t}") for t in range(TT)]
        mem_landed = sem("mem_landed")
        g_landed = sem("g_landed")
        small_landed, vec_landed, ang_landed = sem("small_landed"), sem("vec_landed"), sem("ang_landed")
        w_landed, idx2_landed = [sem("w_landed0"), sem("w_landed1")], sem("idx2_landed")
        w_hi_done, w_lo_done, w_used = sem("w_hi_done"), sem("w_lo_done"), sem("w_used")
        proj_done = [sem(f"proj_done{b}") for b in range(4)]
        bank_empty = [sem(f"bank_empty{b}") for b in range(4)]
        dve_step, act_step, pool_step = sem("dve_step"), sem("act_step"), sem("pool_step")
        consts = sem("consts")
        x_ssq, x_var, x_rstd, x_scaled = sem("x_ssq"), sem("x_var"), sem("x_rstd"), sem("x_scaled")
        x_turned, xT_hi, xT_lo = sem("x_turned"), sem("xT_hi"), sem("xT_lo")
        vec_turned, vec_copied = sem("vec_turned"), sem("vec_copied")
        ang_ready, sincos, tabs32, tabs_ready = sem("ang_ready"), sem("sincos"), sem("tabs32"), sem("tabs_ready")
        qi_rotated, gates_copied = sem("qi_rotated"), sem("gates_copied")
        gates_turned, gates_read = sem("gates_turned"), sem("gates_read")
        gate_abs, gate_ln, gate_rows, gate_cols = sem("gate_abs"), sem("gate_ln"), sem("gate_rows"), sem("gate_cols")
        gate_back, em_done = sem("gate_back"), sem("em_done")
        idx_turned, idx_copied, ki_copied = sem("idx_turned"), sem("idx_copied"), sem("ki_copied")
        ki_turned, ki_rotated, q_split = sem("ki_turned"), sem("ki_rotated"), sem("q_split")
        logits, relued, summed = sem("logits"), sem("relued"), sem("summed")
        km_squared, km_var, km_rstd, km_normed = (sem("km_squared"), sem("km_var"),
                                                             sem("km_rstd"), sem("km_normed"))
        km_turned, km_ready = sem("km_turned"), sem("km_ready")
        m_added = sem("m_added")
        m_ssq, m_varred, m_rstd = sem("m_ssq"), sem("m_varred"), sem("m_rstd")
        m_scores, m_bias, m_exp = sem("m_scores"), sem("m_bias"), sem("m_exp")
        m_scaled, m_pturned, m_pcopied, m_vcopied, m_out, m_y = (sem("m_scaled"), sem("m_pturned"), sem("m_pcopied"),
                                                                 sem("m_vcopied"), sem("m_out"), sem("m_y"))
        b_squared, b_varred, b_rstded, b_rotated = (sem("b_squared"), sem("b_varred"),
                                                             sem("b_rstded"), sem("b_rotated"))
        b_turned, b_qcopied, b_kcopied, b_scores = sem("b_turned"), sem("b_qcopied"), sem("b_kcopied"), sem("b_scores")
        b_masked, b_bias, b_exp, b_pturned, b_pcopied = (sem("b_masked"), sem("b_bias"), sem("b_exp"),
                                                         sem("b_pturned"), sem("b_pcopied"))
        b_scaled, b_out, b_y = sem("b_scaled"), sem("b_out"), sem("b_y")
        a_qk, a_spread, a_md_done, a_wdone = (sem("a_qk"), sem("a_spread"),
                                                       sem("a_md_done"), sem("a_wdone"))
        a_st, a_atd, a_params = sem("a_st"), sem("a_atd"), sem("a_params")
        a_num, a_rinv, a_ssq, a_var, a_rstd = sem("a_num"), sem("a_rinv"), sem("a_ssq"), sem("a_var"), sem("a_rstd")
        a_scale, a_hnd, a_turned, a_y, a_ozd = (sem("a_scale"), sem("a_hnd"), sem("a_turned"), sem("a_y"),
                                                sem("a_ozd"))
        g_merged, ones_set = sem("g_merged"), sem("ones_set")
        ys_hi, ys_lo = sem("ys_hi"), sem("ys_lo")
        x_again, out_sent = sem("x_again"), sem("out_sent")

        block = ctx.enter_context(nc.Block())

        def w_cols(w, k0, c0, n):
            return w[k0 * P:(k0 + KH) * P, bass.ds(c0, n)].rearrange("(k p) n -> p k n", p=P)

        wi, wkv, wo = w_in[0], w_mem_kv[0], w_out[0]
        wb = [w_branch[0, j] for j in range(3)]

        def turns_of(eng, steps, n, per, body):
            body(0, True, False)
            with eng.Fori(1, n - 1) as i:
                if steps is not None:
                    steps.enter(i, 1, per)
                body(i, False, False)
                if steps is not None:
                    steps.leave(n - 2)
            body(n - 1, False, True)

        @block.sync
        def _(sp):
            def load(p, parts):
                for kh in range(2):
                    narrow = isinstance(p, int) and p == IDX2[0] + 1
                    sp.wait_ge(w_lo_done, IDX2[0] * 2 + (kh - 1) if narrow else p * 2 + (kh - 1))
                    at = 0
                    for w, c0, n in parts:
                        sp.dma_start(w_raw[:, kh, :, at:at + n], w_cols(w, kh * KH, c0, n)).then_inc(w_landed[kh], 16)
                        at += n

            def load_x(tiles):
                for t in tiles:
                    sp.dma_start(x_in[:, t], x[0, t * P:(t + 1) * P, :]).then_inc(x_landed[t], 16)

            load_x(FIRST_TILES[:2])
            sp.dma_start(w_raw[:, 0], w_cols(wi, 0, C_QI, 512)).then_inc(w_landed[0], 16)
            load_x(FIRST_TILES[2:])
            sp.dma_start(w_raw[:, 1], w_cols(wi, KH, C_QI, 512)).then_inc(w_landed[1], 16)
            with nc.allow_non_contiguous_dma(reason="a few columns of vectors"):
                sp.dma_start(mem_in, mem[0].rearrange("(t p) n -> p t n", p=P)).then_inc(mem_landed, 16)
                sp.dma_start(memg_row, mem_norm_g.partition_broadcast(P)).then_inc(small_landed, 16)
                sp.dma_start(vec_rows[0:64, :], conv_w[0].rearrange("j (b n) -> (j b) n", n=P)).then_inc(vec_landed, 16)
                sp.dma_start(vec_rows[64:80, :], conv_b[0].rearrange("(b n) -> b n", n=P)).then_inc(vec_landed, 16)
                sp.dma_start(vec_rows[80:88, :], mlstm_norm_g[0].rearrange("h (b n) -> (h b) n", n=P)).then_inc(vec_landed, 16)
                sp.dma_start(vec_rows[88:90, :], mem_q_norm_g[0].rearrange("(b n) -> b n", n=P)).then_inc(vec_landed, 16)
                sp.dma_start(vec_rows[90:92, :], mem_k_norm_g[0].rearrange("(b n) -> b n", n=P)).then_inc(vec_landed, 16)
                sp.dma_start(gain_rows[:, 0:P], dsa_q_norm_g.partition_broadcast(P)).then_inc(small_landed, 16)
                sp.dma_start(gain_rows[:, P:2 * P], dsa_k_norm_g.partition_broadcast(P)).then_inc(small_landed, 16)
                sp.dma_start(gate_b, mlstm_gate_b[0].rearrange("k h -> h k")).then_inc(small_landed, 16)
            for kh in range(2):
                sp.dma_start(idx2_raw[:, kh, :, 0:I_HD + I_HEADS], w_cols(wi, kh * KH, C_KI, I_HD + I_HEADS))\
                    .then_inc(idx2_landed, 16)
                sp.dma_start(idx2_raw[:, kh, :, I_HD + I_HEADS:], w_cols(wi, kh * KH, C_IF, 2 * A_HEADS))\
                    .then_inc(idx2_landed, 16)
            load(KV[0], [(wkv, 0, 512)])
            with sp.Fori(1, 4) as i:
                load(i + KV[0], [(wkv, i * 512, 512)])
            with sp.Fori(0, M_HEADS) as h:
                load(h + MS[0], [(wi, h * M_HD + C_QM, M_HD), (wi, h * M_HD + C_ZM, M_HD)])
            with sp.Fori(0, B_HEADS) as h:
                load(h * 2 + BS[0], [(wi, h * P + (C_QB + c * D), P) for c in range(3)])
                load(h * 2 + (BS[0] + 1), [(wi, h * P + C_ZB, P), (wi, h * P + (C_GATE + 2 * D), P), (wb[2], h * P, P)])
            with sp.Fori(0, A_HEADS) as h:
                load(h * 3 + AS[0], [(wi, h * A_HD + C_QA, A_HD), (wi, h * A_HD + C_KA, A_HD)])
                load(h * 3 + (AS[0] + 1), [(wi, h * A_HD + C_OA, A_HD), (wi, h * A_HD + C_ZA, A_HD)])
                load(h * 3 + (AS[0] + 2), [(wi, h * A_HD + C_VA, A_HD)])
            with sp.Fori(0, 4) as j:
                load(j + GB[0], [(wi, j * 256 + (C_GATE + D), 256), (wb[1], j * 256, 256)])
            with sp.Fori(0, 4) as j:
                load(j + GA[0], [(wi, j * 256 + C_GATE, 256), (wb[0], j * 256, 256)])
            sp.wait_ge(ys_lo, 3 * KT)
            for t in range(TT):
                sp.dma_start(x_in[:, t], x[0, t * P:(t + 1) * P, :]).then_inc(x_again, 16)
            with sp.Fori(0, 2) as c:
                load(c + OUT[0], [(wo, c * 512, 512)])
            for c in range(2):
                for t in range(TT):
                    sp.wait_ge(bank_empty[t], OUT[2][t] + c + 1)
                    sp.dma_start(out[0, t * P:(t + 1) * P, c * 512:(c + 1) * 512],
                                 x_in[:, t, c * 512:(c + 1) * 512]).then_inc(out_sent, 16)
            sp.wait_ge(out_sent, 16 * 2 * TT)

        @block.tensor
        def _(pe):
            mm, turn = nc.tensor.matmul, nc.tensor.transpose

            def products(ps, lhs, rhs, k0, first, last):
                for k in range(KH):
                    for j, (a, b) in enumerate(((0, 0), (0, 1), (1, 0))):
                        ins = mm(ps, lhs[a](k, k0), rhs[b](k, k0), start=(first and k == 0 and j == 0),
                                 stop=(last and k == KH - 1 and j == 2))
                return ins

            def panel(p, blocks, hooks=None):
                hooks = hooks or {}
                slot = 0
                for kh in range(2):
                    pe.wait_ge(w_lo_done, p * 2 + (kh + 1))
                    for n, (b, used, lhs, rhs, width, before) in enumerate(blocks):
                        for hook in hooks.get(slot, ()):
                            hook()
                        slot += 1
                        if kh == 0 and not (isinstance(used, int) and used == 0):
                            pe.wait_ge(bank_empty[b], used)
                        if before is not None and before[kh] is not None:
                            pe.wait_ge(*before[kh])
                        ins = products(banks[b][:, 0:width], lhs(kh), rhs(kh), kh * KH, kh == 0, kh == 1)
                        if kh == 1:
                            ins.then_inc(proj_done[b], 1)
                        elif n == len(blocks) - 1:
                            ins.then_inc(w_used, 1)

            def w_as_lhs(c0):
                return lambda kh: [lambda k, k0, w=w: w[:, kh, k, c0:c0 + P] for w in (w_hi, w_lo)]

            def w_as_rhs(n):
                return lambda kh: [lambda k, k0, w=w: w[:, kh, k, 0:n] for w in (w_hi, w_lo)]

            def tokens(pair, t):
                return lambda kh: [lambda k, k0, w=w: w[:, k0 + k, t * P:(t + 1) * P] for w in pair]

            def all_tokens(pair):
                return lambda kh: [lambda k, k0, w=w: w[:, k0 + k, :] for w in pair]

            hT, yT = (hT_hi, hT_lo), (y_hi, y_lo)

            def y_split(times):
                return [(ys_lo, (times - 1) * KT + (kh + 1) * KH) for kh in range(2)]

            def x_transposes(i):
                pe.wait_ge(x_scaled, i + 1)
                for half in range(2):
                    n = 2 * i + half
                    if n >= 4:
                        pe.wait_ge(xT_lo, n - 3)
                    for k in range(4):
                        ins = turn(att[n % 4][:, k * P:(k + 1) * P],
                                   x_sc[:, i % 2, (half * 4 + k) * P:(half * 4 + k + 1) * P], ident[:, :])
                    ins.then_inc(x_turned, 1)

            def vector_transposes():
                pe.wait_ge(vec_landed, 16 * 5)
                pe.wait_ge(xT_lo, 2 * TT + 1)
                turn(att[0][:, 0:92], vec_rows, ident[0:92, 0:92]).then_inc(vec_turned, 1)

            pe.wait_ge(consts, 4)
            for i in range(2):
                x_transposes(i)

            panel(IDX1[0], [(t, 0, tokens(hT, t), w_as_rhs(512), 512, [(xT_lo, 2 * FIRST_TILES.index(t) + 2), None])
                            for t in range(1, TT)],
                  {1: [lambda: x_transposes(TT - 2)], 2: [lambda: x_transposes(TT - 1)], 4: [lambda: x_transposes(TT)],
                   5: [lambda: x_transposes(TT + 1), vector_transposes]})
            pe.wait_ge(xT_lo, 2 * TT)
            for kh in range(2):
                pe.wait_ge(w_lo_done, IDX2[0] * 2 + kh + 1)
                ins = products(banks[0][0:I_COLS, :], [lambda k, k0, w=w: w[:, kh, k, 0:I_COLS] for w in (w_hi, w_lo)],
                               all_tokens(hT)(kh), kh * KH, kh == 0, kh == 1)
                ins.then_inc(proj_done[0] if kh else w_used, 1)

            def ki_transposes():
                pe.wait_ge(bank_empty[0], 1)
                pe.wait_ge(xT_lo, 2 * (TT + MT))
                for t in range(TT):
                    ins = turn(att[3][:, t * I_COLS:(t + 1) * I_COLS], kiF[:, t * P:(t + 1) * P],
                               ident[0:I_COLS, 0:I_COLS])
                ins.then_inc(ki_turned, 1)

            def gates_to_rows():
                pe.wait_ge(gates_copied, 1)
                pe.wait_ge(vec_copied, 1)
                pe.wait_ge(xT_lo, 2 * (TT + MT))
                for kind in range(2):
                    for t in range(TT):
                        ins = turn(att[kind][0:A_HEADS, t * P:(t + 1) * P],
                                   ifr[:, t, kind * A_HEADS:(kind + 1) * A_HEADS], ident[:, :])
                ins.then_inc(gates_turned, 1)

            def idx_transposes():
                pe.wait_ge(qi_rotated, 3)
                pe.wait_ge(ki_rotated, 1)
                pe.wait_ge(gates_read, 1)
                for t in range(3):
                    for j in range(4):
                        ins = turn(att[t][:, j * P:(j + 1) * P], qi_rot[:, t, j * P:(j + 1) * P], ident[:, :])
                    ins.then_inc(idx_turned, 1)
                for t in range(TT):
                    ins = turn(att[3][:, t * P:(t + 1) * P], ki_rot[:, t, :], ident[:, :])
                ins.then_inc(idx_turned, 1)

            def logit(u):
                t, h = u // 8 + 1, u % 8
                if u == 0:
                    pe.wait_ge(q_split, 3)
                    pe.wait_ge(ki_copied, 1)
                if u >= 4:
                    pe.wait_ge(relued, u - 3)
                lo = I_HD * (h % 2)
                q = [qiT[a][t - 1][lo:lo + I_HD, h // 4, (h // 2 % 2) * P:(h // 2 % 2 + 1) * P] for a in range(2)]
                for half in range(2 if (t + 1) * P > MEM else 1):
                    w = min(MEM, (t + 1) * P - half * MEM)
                    for j, (a, b) in enumerate(((0, 0), (0, 1), (1, 0))):
                        ins = mm(att[u % 4][:, half * MEM:half * MEM + w], q[a], kiT[b][lo:lo + I_HD, half, 0:w],
                                 start=(j == 0), stop=(j == 2))
                ins.then_inc(logits, 1)

            def kv_hooks(i):
                if i == 0:
                    return {1: [ki_transposes], 2: [gates_to_rows], 3: [idx_transposes]}
                return {s: [lambda u=(i - 1) * 8 + 2 * s + e: logit(u) for e in range(2)] for s in range(4)}

            memT = (memT_hi, memT_lo)
            pe.wait_ge(xT_lo, 2 * (TT + MT))
            for i in range(4):
                panel(KV[0] + i, [(2 * (i % 2) + m, KV[2][2 * (i % 2) + m] + i // 2, tokens(memT, m),
                                   w_as_rhs(512), 512, None) for m in range(MT)], kv_hooks(i))

            def gates_to_columns():
                pe.wait_ge(gate_rows, 1)
                pe.wait_ge(summed, 24)
                for kind in range(2):
                    for t in range(TT):
                        c = (kind * TT + t) * A_HEADS
                        ins = turn(att[0][:, c:c + A_HEADS], rows[:, kind, t * P:(t + 1) * P],
                                   ident[0:A_HEADS, 0:A_HEADS])
                ins.then_inc(gate_back, 1)

            def km_transposes():
                pe.wait_ge(km_normed, 1)
                pe.wait_ge(gate_cols, 1)
                for h in range(M_HEADS):
                    for e in range(2):
                        for m in range(MT):
                            ins = turn(att[h][:, (e * MT + m) * P:(e * MT + m + 1) * P],
                                       km_raw[:, m * D + h * M_HD + e * P:m * D + h * M_HD + (e + 1) * P],
                                       ident[:, :])
                    ins.then_inc(km_turned, 1)

            def m_norm_scores(h):
                pe.wait_ge(m_added, h + 1)
                if isinstance(h, int) and h == 0:
                    pe.wait_ge(km_ready, M_HEADS)
                    pe.wait_ge(bank_empty[3], KV[2][3] + 2)
                else:
                    pe.wait_ge(m_y, h * 2)
                for t in range(TT):
                    ins = mm(att[0][:, t:t + 1], m_sq[:, 0, t * P:(t + 1) * P], ones[:, :], start=True, stop=True)
                ins.then_inc(m_ssq, 1)
                kh_ = kmT.rearrange("p h n -> p (h n)")
                for t in range(TT):
                    for e in range(2):
                        ins = mm(att[1 + t // 2][:, (t % 2) * MEM:(t % 2 + 1) * MEM], m_qT[:, e, t * P:(t + 1) * P],
                                 kh_[:, bass.ds(h * 512 + e * MEM, MEM)], start=(e == 0), stop=(e == 1))
                    if t % 2:
                        ins.then_inc(m_scores, 1)

            def m_turn_p(h):
                pe.wait_ge(m_scaled, h + 1)
                for g in range(2):
                    for t in (2 * g, 2 * g + 1):
                        for m in range(MT):
                            c = (m * 2 + t % 2) * P
                            ins = turn(att[3 - 3 * g][:, c:c + P], m_p[:, t, m * P:(m + 1) * P], ident[:, :])
                    ins.then_inc(m_pturned, 1)

            def m_values(h):
                pe.wait_ge(m_pcopied, h * 2 + 2)
                pe.wait_ge(m_vcopied, h + 1)
                for e in range(2):
                    for m in range(MT):
                        ins = mm(att[1 + e][:, :], m_vh[:, m, e * P:(e + 1) * P], m_pT[:, m, :],
                                 start=(m == 0), stop=(m == MT - 1))
                    ins.then_inc(m_out, 1)

            def m_hooks(h, first):
                if first:
                    return {0: [gates_to_columns], 3: [km_transposes]}
                g = h - 1
                return {1: [lambda: m_norm_scores(g)], 4: [lambda: m_turn_p(g)],
                        6: [lambda: m_values(g)]}

            def m_body(h, first, last):
                panel(h + MS[0], [(b, h + MS[2][b], w_as_lhs(b * P), all_tokens(hT), S, None) for b in range(4)],
                      m_hooks(h, first))

            turns_of(pe, None, M_HEADS, 0, m_body)

            def b_turn_qk(h):
                pe.wait_ge(b_rotated, h + 1)
                if not (isinstance(h, int) and h == 0):
                    pe.wait_ge(b_pcopied, h * 4)
                else:
                    pe.wait_ge(m_y, 2 * M_HEADS)
                for c in range(2):
                    for t in range(TT):
                        ins = turn(att[c][:, t * P:(t + 1) * P],
                                   b_rc[:, (2 * t + c) * P:(2 * t + c + 1) * P], ident[:, :])
                    ins.then_inc(b_turned, 1)

            def b_score(h):
                if not (isinstance(h, int) and h == 0):
                    pe.wait_ge(b_y, h)
                pe.wait_ge(b_qcopied, h + 1)
                pe.wait_ge(b_kcopied, h + 1)
                for t in range(TT):
                    mm(att[(t + 2) % 4][:, 0:(t + 1) * P], b_qT[:, t * P:(t + 1) * P], b_kT[:, 0:(t + 1) * P],
                       start=True, stop=True).then_inc(b_scores, 1)

            def b_turn_p(h):
                for t in range(TT):
                    pe.wait_ge(b_scaled, h * 4 + (t + 1))
                    for s in range(t + 1):
                        ins = turn(att[(t + 2) % 4][:, s * P:(s + 1) * P],
                                   score[:, off(t) + s * P:off(t) + (s + 1) * P], ident[:, :])
                    ins.then_inc(b_pturned, 1)

            def b_values(h):
                pe.wait_ge(b_pcopied, h * 4 + 4)
                for s in range(TT):
                    ins = mm(att[2][:, s * P:S], b_raw[:, s, 2 * P:3 * P], b_pT[:, s, s * P:S],
                             start=(s == 0), stop=(s == TT - 1))
                ins.then_inc(b_out, 1)

            def b_body(h, first, last):
                g = h - 1
                if first:
                    g = M_HEADS - 1
                    hooks_t = {1: [lambda: m_norm_scores(g)], 4: [lambda: m_turn_p(g)],
                               6: [lambda: m_values(g)]}
                    hooks_f = {}
                else:
                    hooks_t = {1: [lambda: b_score(g)], 5: [lambda: b_turn_p(g)], 7: [lambda: b_values(g)]}
                    hooks_f = {}
                hooks_f[5] = [lambda: b_turn_qk(h)]
                step = (2, 2, 2, 1)
                panel(h * 2 + BS[0], [(t, h * step[t] + BS[2][t], tokens(hT, t), w_as_rhs(384), 384, None)
                                      for t in range(TT)], hooks_t)
                panel(h * 2 + (BS[0] + 1),
                      [(b, h * 2 + (BS[2][b] + 1), w_as_lhs(b * P), all_tokens(yT if b == 2 else hT), S,
                        y_split(1) if b == 2 and first else None) for b in range(3)], hooks_f)

            turns_of(pe, None, B_HEADS, 0, b_body)

            def a_spread_max(h):
                if isinstance(h, int) and h == 0:
                    pe.wait_ge(b_y, B_HEADS)
                else:
                    pe.wait_ge(a_y, h * 2)
                mm(att[0][:, :], pick[:, 0, :], maxrow, start=True, stop=True).then_inc(a_spread, 1)

            def a_scores(h):
                pe.wait_ge(a_qk, h * 4 + 4)
                for s in range(TT):
                    bank, c = ((1, 0), (2, 0), (3, 0), (3, 2 * P))[s]
                    n = S - s * P
                    for e in range(2):
                        ins = mm(att[bank][:, c:c + n], a_kT[:, e, s * P:(s + 1) * P], a_qT[:, e, s * P:S],
                                 start=(e == 0), stop=(e == 1))
                    ins.then_inc(a_st, 1)

            def a_numerators(h):
                pe.wait_ge(a_atd, h * 4 + 4)
                if isinstance(h, int) and h == 0:
                    pe.wait_ge(ones_set, 1)
                pe.wait_ge(bank_empty[3], h * 3 + (AS[2][3] + 3))
                for t in range(TT):
                    for s in range(t + 1):
                        c = st_off(s) + (t - s) * P
                        ins = mm(att[t][:, 0:A_HD + 1], a_at[:, c:c + P], a_v[:, s, :], start=(s == 0), stop=(s == t))
                    ins.then_inc(a_num, 1)

            def a_turn_h(h):
                pe.wait_ge(a_hnd, h * 4 + 4)
                for e in range(2):
                    for t in range(TT):
                        ins = turn(att[e][:, t * P:(t + 1) * P], a_hn[:, t, e * P:(e + 1) * P], ident[:, :])
                    ins.then_inc(a_turned, 1)

            def a_body(h, first, last):
                g = h - 1
                if first:
                    g = B_HEADS - 1
                    qk_hooks = {1: [lambda: b_score(g)], 3: [lambda: b_turn_p(g)], 5: [lambda: b_values(g)]}
                else:
                    qk_hooks = {1: [lambda: a_numerators(g)], 5: [lambda: a_turn_h(g)]}
                u = lambda b, j: h * 3 + (AS[2][b] + j)
                panel(h * 3 + AS[0], [(b, u(b, 0), w_as_lhs(b * P), all_tokens(hT), S, None) for b in range(4)],
                      qk_hooks)
                panel(h * 3 + (AS[0] + 1), [(b, u(b, 1), w_as_lhs(b * P), all_tokens(hT), S, None)
                                            for b in range(4)], {2: [lambda: a_spread_max_of(h)],
                                                                 5: [lambda: a_scores(h)]})
                panel(h * 3 + (AS[0] + 2), [(t, u(t, 2), tokens(hT, t), w_as_rhs(A_HD), A_HD, None)
                                            for t in range(TT)])

            def a_spread_max_of(h):
                pe.wait_ge(a_params, h + 1)
                a_spread_max(h)

            turns_of(pe, None, A_HEADS, 0, a_body)

            def gated(sec, j, n, before, hooks=None):
                panel(j + sec[0], [(b, j + sec[2][b], w_as_lhs(b * P), all_tokens(hT if b < 2 else yT), S,
                                    before if b == 2 else None) for b in (2, 3, 0, 1)], hooks)

            g = A_HEADS - 1
            gated(GB, 0, 0, y_split(2), {1: [lambda: a_numerators(g)], 5: [lambda: a_turn_h(g)]})
            with pe.Fori(1, 4) as j:
                gated(GB, j, 0, None)
            gated(GA, 0, 0, y_split(3))
            with pe.Fori(1, 4) as j:
                gated(GA, j, 0, None)
            for c in range(2):
                panel(OUT[0] + c, [(t, OUT[2][t] + c, tokens(yT, t), w_as_rhs(512), 512,
                                    y_split(4) if c == 0 and t == 0 else None) for t in range(TT)])

        @block.scalar
        def _(act):
            A_ = nc.scalar.activation
            steps = Steps(act, act_step)

            def split_hi(p, kh, loads, n, before=None, raw=w_raw):
                act.wait_ge(*((w_landed[kh], loads * 16) if raw is w_raw else (idx2_landed, 16 * 4)))
                if kh == 1 and before is not None:
                    act.wait_ge(proj_done[before[0]], before[1])
                elif kh == 0 and not (isinstance(p, int) and p == 0):
                    act.wait_ge(w_used, p)
                A_(w_hi[:, kh, :, 0:n], raw[:, kh, :, 0:n], ACT.Copy).then_inc(w_hi_done, 1)

            def split_y(src, tiles=range(KT)):
                for k in tiles:
                    A_(y_hi[:, k, :], src[:, k * S:(k + 1) * S], ACT.Copy).then_inc(ys_hi, 1)

            act.dma_start(g_row, norm_g.partition_broadcast(P)).then_inc(g_landed, 16)
            with nc.allow_non_contiguous_dma(reason="one position a partition"):
                act.dma_start(pos_i, positions[0].rearrange("(t p) -> p t", p=P)).then_inc(ang_landed, 16)
                act.dma_start(invf, inv_freq.partition_broadcast(P)).then_inc(ang_landed, 16)

            def square(i):
                act.wait_ge(x_landed[FIRST_TILES[i]] if i < TT else mem_landed, 16)
                if i:
                    act.wait_ge(x_ssq, i)
                src = x_in[:, FIRST_TILES[i]] if i < TT else mem_in[:, i - TT]
                A_(junk, src, ACT.Square, accum_out=xss[:, i:i + 1]).then_inc(x_ssq, 1)

            def x_high(n):
                act.wait_ge(x_turned, n + 1)
                i, half = n // 2, n % 2
                dst, c = (hT_hi, FIRST_TILES[i]) if i < TT else (memT_hi, i - TT)
                A_(dst[:, half * 4:half * 4 + 4, c * P:(c + 1) * P],
                   att[n % 4][:, :].rearrange("p (k n) -> p k n", k=4), ACT.Copy).then_inc(xT_hi, 1)

            square(0)
            square(1)
            x_high(0)
            x_high(1)
            split_hi(0, 0, 1, 512)
            x_high(2)
            x_high(3)
            square(2)
            square(3)
            x_high(4)
            x_high(5)
            split_hi(0, 1, 1, 512)
            for i in range(TT, TT + MT):
                square(i)
            x_high(6)
            x_high(7)
            act.wait_ge(ang_ready, 1)
            A_(sind.rearrange("p t n -> p (t n)"), ang, ACT.Sin).then_inc(sincos, 1)
            A_(cosd.rearrange("p t n -> p (t n)"), turns, ACT.Sin).then_inc(sincos, 1)
            for n in range(2 * TT, 2 * (TT + MT)):
                x_high(n)

            split_hi(1, 0, 0, I_COLS, raw=idx2_raw)
            split_hi(1, 1, 0, I_COLS, (3, 1), idx2_raw)
            split_hi(2, 0, KV[1] + 1, 512)
            act.wait_ge(proj_done[0], IDX2[2][0] + 1)
            A_(kiF, banks[0][0:I_COLS, :], ACT.Copy).then_inc(bank_empty[0], 1)

            def gate_copies():
                act.wait_ge(ki_turned, 1)
                k4 = att[3][:, 0:TT * I_COLS].rearrange("p (t n) -> p t n", t=TT)
                A_(wi8, k4[:, :, I_HD:I_HD + I_HEADS], ACT.Copy, scale=float(np.float32(I_HEADS ** -0.5)))
                A_(ifr, k4[:, :, I_HD + I_HEADS:I_COLS], ACT.Copy).then_inc(gates_copied, 1)

            def idx_copies():
                for t in range(3):
                    act.wait_ge(idx_turned, t + 1)
                    A_(qiT[0][t], att[t][:, :].rearrange("p (k n) -> p k n", k=2), ACT.Copy).then_inc(idx_copied, 1)
                act.wait_ge(idx_turned, 4)
                A_(kiT[0], att[3][:, :].rearrange("p (k n) -> p k n", k=2), ACT.Copy).then_inc(idx_copied, 1)

            def relus(i, part):
                for u in range(8 * i + 4 * part, 8 * i + 4 * part + 4):
                    t = u // 8 + 1
                    act.wait_ge(logits, u + 1)
                    if u >= 2:
                        act.wait_ge(summed, u - 1)
                    A_(relu[:, u % 2, 0:(t + 1) * P], att[u % 4][:, 0:(t + 1) * P], ACT.Relu,
                       scale=I_HD ** -0.5).then_inc(relued, 1)

            for i in range(4):
                p = KV[0] + i
                last = 0 if i == 0 else 2 * ((i - 1) % 2) + 1
                split_hi(p, 1, KV[1] + i + 1, 512, (last, KV[2][last] + (i + 1) // 2))
                if i == 1:
                    act.wait_ge(gate_abs, 1)
                    steps.then(A_(rows[:, 3], rows[:, 2], ACT.Exp, scale=-1.0))
                    A_(rows[:, 3], rows[:, 3], ACT.Ln, bias=1.0).then_inc(gate_ln, 1)
                if i == 0:
                    gate_copies()
                else:
                    relus(i - 1, 0)
                split_hi(p + 1, 0, KV[1] + i + 2 if i < 3 else MS[1] + 2, 512)
                if i:
                    relus(i - 1, 1)
                else:
                    idx_copies()
                for m in range(MT):
                    b = 2 * (i % 2) + m
                    act.wait_ge(proj_done[b], KV[2][b] + i // 2 + 1)
                    if i < 2:
                        if i == 0 and m == 0:
                            act.wait_ge(x_scaled, TT + MT)
                        A_(km_raw[:, m * D + i * 512:m * D + (i + 1) * 512], banks[b][:, :], ACT.Copy)\
                            .then_inc(bank_empty[b], 1)
                    else:
                        A_(vm[:, m, (i - 2) * 512:(i - 1) * 512], banks[b][:, :], ACT.Copy)\
                            .then_inc(bank_empty[b], 1)

            def m_exps(h):
                for t in range(TT):
                    if t == 0:
                        act.wait_ge(m_bias, h + 1)
                    A_(m_p[:, t, :], att[1 + t // 2][:, (t % 2) * MEM:(t % 2 + 1) * MEM], ACT.Exp,
                       bias=nb[:, t:t + 1], scale=m_ps[:, t:t + 1], accum_out=rsum[:, t:t + 1]).then_inc(m_exp, 1)

            def m_evac(h, first):
                for e in range(2):
                    act.wait_ge(proj_done[e], h + (MS[2][e] + 1))
                    if first and e == 0:
                        act.wait_ge(vec_copied, 2)
                        act.wait_ge(km_var, 1)
                    A_(m_qT[:, e, :], banks[e][:, :], ACT.Copy, scale=gqk[:, e:e + 1])
                    ins = A_(m_sq[:, e, :], banks[e][:, :], ACT.Square)
                    ins.then_inc(bank_empty[e], 1)
                for e in range(2):
                    b = 2 + e
                    act.wait_ge(proj_done[b], h + (MS[2][b] + 1))
                    if not first and e == 0:
                        act.wait_ge(m_y, h * 2)
                    A_(m_zs[:, e, :], banks[b][:, :], ACT.Silu).then_inc(bank_empty[b], 1)

            def m_body(h, first, last):
                p = h + MS[0]
                split_hi(p, 1, h * 2 + (MS[1] + 2), 512, (3, h + MS[2][3]))
                if first:
                    act.wait_ge(gate_cols, 1)
                    A_(gcols[:, 1].rearrange("p h t -> p (h t)"), gcols[:, 1].rearrange("p h t -> p (h t)"), ACT.Exp,
                       scale=-1.0).then_inc(em_done, 1)
                    for g in range(M_HEADS):
                        act.wait_ge(km_turned, g + 1)
                        A_(kmT[:, g, :], att[g][:, :], ACT.Copy).then_inc(km_ready, 1)
                else:
                    m_exps(h - 1)
                if last:
                    split_hi(p + 1, 0, BS[1] + 3, 384)
                else:
                    split_hi(p + 1, 0, h * 2 + (MS[1] + 4), 512)
                m_evac(h, first)

            turns_of(act, steps, M_HEADS, 0, m_body)

            def b_exps(h):
                for t in range(TT):
                    if t == 0:
                        act.wait_ge(b_bias, h + 1)
                    s_t = score[:, off(t):off(t + 1)]
                    A_(s_t, s_t, ACT.Exp, bias=nb[:, t:t + 1], scale=m_ps[:, t:t + 1],
                       accum_out=rsum[:, t:t + 1]).then_inc(b_exp, 1)

            def b_raw_copies(h, first):
                for t in range(TT):
                    act.wait_ge(proj_done[t], h * (2, 2, 2, 1)[t] + (BS[2][t] + 1))
                    if t == 0:
                        if first:
                            act.wait_ge(m_out, 2 * M_HEADS)
                        else:
                            act.wait_ge(b_out, h)
                    A_(b_raw[:, t, :], banks[t][:, 0:384], ACT.Copy).then_inc(bank_empty[t], 1)

            def b_body(h, first, last):
                p = h * 2 + BS[0]
                split_hi(p, 1, h * 6 + (BS[1] + 3), 384, (3, BS[2][3]) if first else (2, h * 2 + BS[2][2]))
                if first:
                    m_exps(M_HEADS - 1)
                else:
                    b_exps(h - 1)
                split_hi(p + 1, 0, h * 6 + (BS[1] + 6), 384)
                b_raw_copies(h, first)
                split_hi(p + 1, 1, h * 6 + (BS[1] + 6), 384, (3, h + (BS[2][3] + 1)))
                if first:
                    act.wait_ge(m_y, 2 * M_HEADS)
                    act.wait_ge(xT_lo, 2 * (TT + MT))
                    split_y(yF)
                if last:
                    split_hi(p + 2, 0, AS[1] + 2, 512)
                else:
                    split_hi(p + 2, 0, h * 6 + (BS[1] + 9), 384)
                act.wait_ge(proj_done[0], h * 2 + (BS[2][0] + 2))
                if not first:
                    act.wait_ge(b_y, h)
                A_(b_zs, banks[0][:, :], ACT.Silu).then_inc(bank_empty[0], 1)
                act.wait_ge(proj_done[1], h * 2 + (BS[2][1] + 2))
                if not first:
                    act.wait_ge(bank_empty[2], h * 2 + BS[2][2])
                A_(sig[:, 0], banks[1][:, :], ACT.Sigmoid).then_inc(bank_empty[1], 1)
                act.wait_ge(b_turned, h * 2 + 1)
                A_(b_qT, att[0][:, :], ACT.Copy).then_inc(b_qcopied, 1)

            turns_of(act, steps, B_HEADS, 0, b_body)

            def a_norm(h):
                act.wait_ge(a_rinv, h + 1)
                for t in range(TT):
                    ins = A_(a_hn[:, t, :], att[t][:, 0:A_HD], ACT.Square, scale=a_ri[:, t:t + 1],
                             accum_out=a_ss[:, t:t + 1])
                ins.then_inc(a_ssq, 1)
                act.wait_ge(a_scale, h + 1)
                for t in range(TT):
                    A_(a_hn[:, t, :], att[t][:, 0:A_HD], ACT.Copy, scale=a_s[:, t:t + 1]).then_inc(a_hnd, 1)

            def a_weights(h):
                act.wait_ge(a_md_done, h + 1)
                for s in range(TT):
                    ins = A_(a_w[:, st_off(s):st_off(s) + P], a_md[:, s, :], ACT.Exp, bias=hcol[:, 0, s:s + 1])
                    if s < TT - 1:
                        A_(a_w[:, st_off(s) + P:st_off(s + 1)], att[0][:, (s + 1) * P:S], ACT.Exp,
                           bias=hcol[:, 0, s:s + 1])
                ins.then_inc(a_wdone, 1)

            def a_body(h, first, last):
                p = h * 3 + AS[0]
                loads = h * 5 + AS[1]
                split_hi(p, 1, loads + 2, 512, (2, AS[2][2]) if first else (3, h * 3 + AS[2][3]))
                if first:
                    b_exps(B_HEADS - 1)
                else:
                    a_norm(h - 1)
                split_hi(p + 1, 0, loads + 4, 512)
                for b in range(4):
                    act.wait_ge(bank_empty[b], h * 3 + (AS[2][b] + 1))
                    dst = (a_qT if b < 2 else a_kT)[:, b % 2, :]
                    A_(dst, a_conv[:, b % 2, :], ACT.Silu).then_inc(a_qk, 1)
                    if b == 1:
                        split_hi(p + 1, 1, loads + 4, 512, (3, h * 3 + (AS[2][3] + 1)))
                a_weights(h)
                split_hi(p + 2, 0, loads + 5, A_HD)
                for e in range(2):
                    act.wait_ge(proj_done[e], h * 3 + (AS[2][e] + 2))
                    A_(a_o[:, e, :], banks[e][:, :], ACT.Sigmoid).then_inc(bank_empty[e], 1)
                for e in range(2):
                    act.wait_ge(proj_done[2 + e], h * 3 + (AS[2][2 + e] + 2))
                    A_(a_oz[:, e, :], banks[2 + e][:, :], ACT.Silu).then_inc(bank_empty[2 + e], 1)
                split_hi(p + 2, 1, loads + 5, A_HD, (3, h * 3 + (AS[2][3] + 2)))
                if first:
                    act.wait_ge(b_y, B_HEADS)
                    split_y(yF)
                split_hi(p + 3, 0, loads + 7, 512)
                for t in range(TT):
                    act.wait_ge(proj_done[t], h * 3 + (AS[2][t] + 3))
                    A_(a_v[:, t, 0:A_HD], banks[t][:, 0:A_HD], ACT.Copy).then_inc(bank_empty[t], 1)

            turns_of(act, steps, A_HEADS, 0, a_body)

            def gates(sec, j, n):
                for b in range(2):
                    act.wait_ge(proj_done[b], j + (sec[2][b] + 1))
                    if not (isinstance(n, int) and n == 0):
                        act.wait_ge(g_merged, n * 2 + (b - 1))
                    A_(sig[:, b], banks[b][:, :], ACT.Sigmoid).then_inc(bank_empty[b], 1)

            def gb_body(sec, j, n, next_loads, before=1, between=None):
                p = j + sec[0]
                split_hi(p, 1, j * 2 + (sec[1] + 2), 512, (before, j + sec[2][before]))
                if n is None:
                    a_norm(A_HEADS - 1)
                    n = 0
                    act.wait_ge(bank_empty[2], AS[2][2])
                split_hi(p + 1, 0, next_loads, 512)
                if between:
                    between()
                gates(sec, j, n)

            gb_body(GB, 0, None, GB[1] + 4, 3)
            with act.Fori(1, 3) as j:
                gb_body(GB, j, j, j * 2 + (GB[1] + 4))

            def split_branch_a():
                act.wait_ge(a_y, 2 * A_HEADS)
                act.wait_ge(proj_done[3], GA[2][3])
                split_y(yF)

            def split_merged():
                act.wait_ge(g_merged, 14)
                act.wait_ge(proj_done[3], OUT[2][3])
                split_y(merged, range(KT - 2))

            gb_body(GB, 3, 3, GA[1] + 2, between=split_branch_a)
            with act.Fori(0, 3) as j:
                gb_body(GA, j, j + 4, j * 2 + (GA[1] + 4))
            gb_body(GA, 3, 7, OUT[1] + 1, between=split_merged)
            act.wait_ge(g_merged, 16)
            split_y(merged, range(KT - 2, KT))
            split_hi(OUT[0], 1, OUT[1] + 1, 512, (1, OUT[2][1]))
            split_hi(OUT[0] + 1, 0, OUT[1] + 2, 512)
            split_hi(OUT[0] + 1, 1, OUT[1] + 2, 512, (3, OUT[2][3] + 1))

        @block.vector
        def _(dve):
            V = nc.vector
            steps = Steps(dve, dve_step)
            then = steps.then

            def split_lo(p, kh, n, raw=w_raw):
                dve.wait_ge(w_hi_done, p * 2 + (kh + 1))
                V.tensor_tensor(w_lo[:, kh, :, 0:n], raw[:, kh, :, 0:n], w_hi[:, kh, :, 0:n].bitcast(F32),
                                ALU.subtract).then_inc(w_lo_done, 1)

            def split_y(src, times, tiles=range(KT)):
                for k in tiles:
                    dve.wait_ge(ys_hi, (times - 1) * KT + k + 1)
                    V.tensor_tensor(y_lo[:, k, :], src[:, k * S:(k + 1) * S], y_hi[:, k, :].bitcast(F32),
                                    ALU.subtract).then_inc(ys_lo, 1)

            V.memset(ones[:, :], 1.0)
            V.memset(minus_half[:, :], -0.5).then_inc(consts, 1)

            def x_variance(i):
                dve.wait_ge(x_ssq, i + 1)
                V.tensor_scalar(xss[:, i:i + 1], xss[:, i:i + 1], 1.0 / D, EPS, ALU.mult, ALU.add).then_inc(x_var, 1)

            def x_scale(i):
                dve.wait_ge(x_rstd, i + 1)
                if i == 0:
                    dve.wait_ge(g_landed, 16)
                if i >= 2:
                    dve.wait_ge(x_turned, 2 * (i - 1))
                V.scalar_tensor_tensor(x_sc[:, i % 2, :], x_in[:, FIRST_TILES[i]], xrs[:, i:i + 1], g_row,
                                       ALU.mult, ALU.mult).then_inc(x_scaled, 1)

            def x_low(n):
                dve.wait_ge(xT_hi, n + 1)
                i, half = n // 2, n % 2
                hi, lo, c = (hT_hi, hT_lo, FIRST_TILES[i]) if i < TT else (memT_hi, memT_lo, i - TT)
                at = (slice(None), slice(half * 4, half * 4 + 4), slice(c * P, (c + 1) * P))
                V.tensor_tensor(lo[at], att[n % 4][:, :].rearrange("p (k n) -> p k n", k=4),
                                hi[at].bitcast(F32), ALU.subtract).then_inc(xT_lo, 1)

            x_variance(0)
            x_scale(0)
            x_variance(1)
            x_scale(1)
            x_low(0)
            x_low(1)
            split_lo(0, 0, 512)
            x_variance(2)
            x_low(2)
            x_low(3)
            x_scale(2)
            x_variance(3)
            x_low(4)
            x_low(5)
            x_scale(3)
            split_lo(0, 1, 512)
            x_variance(TT)
            x_variance(TT + 1)
            dve.wait_ge(ang_landed, 16 * 2)
            then(V.tensor_copy(pos_f, pos_i))
            for t in range(TT):
                ins = V.tensor_scalar(ang[:, t * 64:(t + 1) * 64], invf, pos_f[:, t:t + 1], None, ALU.mult)
            then(ins)
            then(V.tensor_scalar(turns, ang, INV_2PI, ROUNDER, ALU.mult, ALU.add))
            then(V.tensor_scalar(turns, turns, -ROUNDER, None, ALU.add))
            for part in (TWO_PI_HI, TWO_PI_MID, TWO_PI_LO):
                then(V.scalar_tensor_tensor(ang, turns, -part, ang, ALU.mult, ALU.add))
            then(V.tensor_scalar(turns, ang, float(np.pi / 2), float(-2 * np.pi), ALU.is_gt, ALU.mult))
            then(V.scalar_tensor_tensor(turns, ang, float(np.pi / 2), turns, ALU.add, ALU.add))
            then(V.tensor_scalar(turns, turns, PI_IN, -PI_IN, ALU.min, ALU.max))
            V.tensor_scalar(ang, ang, PI_IN, -PI_IN, ALU.min, ALU.max).then_inc(ang_ready, 1)
            x_low(6)
            x_low(7)
            dve.wait_ge(sincos, 2)
            for src, src32 in ((cosd, cos32), (sind, sin32)):
                for half in range(2):
                    V.tensor_copy(src32[:, :, half * 32:(half + 1) * 32],
                                  src.rearrange("p t (i two) -> p t i two", two=2)[:, :, :, 0]).then_inc(tabs32, 1)
            for n in range(2 * TT, 2 * (TT + MT)):
                x_low(n)
            split_lo(1, 0, I_COLS, idx2_raw)
            dve.wait_ge(vec_turned, 1)
            V.tensor_copy(cols[:, :], att[0][:, 0:92]).then_inc(vec_copied, 1)
            dve.wait_ge(vec_copied, 1)
            V.tensor_tensor(gqk[:, :], cols[:, 88:90], cols[:, 90:92], ALU.mult).then_inc(vec_copied, 1)

            def rotate(a, b, src, cos, sin, heads):
                cb = cos.unsqueeze(1).to_broadcast([P, heads, I_HD])
                sb_ = sin.unsqueeze(1).to_broadcast([P, heads, I_HD])
                s3 = src.rearrange("p (h d) -> p h d", h=heads)
                V.tensor_tensor(a.rearrange("p (h d) -> p h d", h=heads), s3, cb, ALU.mult)
                return V.tensor_tensor(b.rearrange("p (h d) -> p h d", h=heads), s3, sb_, ALU.mult)

            def join(a, b, heads):
                a4 = a.rearrange("p (h two d) -> p h two d", h=heads, two=2)
                b4 = b.rearrange("p (h two d) -> p h two d", h=heads, two=2)
                V.tensor_tensor(a4[:, :, 0], a4[:, :, 0], b4[:, :, 1], ALU.subtract)
                return V.tensor_tensor(a4[:, :, 1], a4[:, :, 1], b4[:, :, 0], ALU.add)

            dve.wait_ge(tabs32, 4)
            for t in range(1, TT):
                dve.wait_ge(proj_done[t], 1)
                if t > 1:
                    dve.wait_ge(qi_rotated, t - 1)
                a = qi_rot[:, t - 1, :]
                ins = rotate(a, qi_b, banks[t][:, :], cos32[:, t], sin32[:, t], I_HEADS)
                ins.then_inc(bank_empty[t], 1)
                dve.wait_ge(bank_empty[t], 1)
                join(a, qi_b, I_HEADS).then_inc(qi_rotated, 1)
                if t == 1:
                    split_lo(1, 1, I_COLS, idx2_raw)
                if t == 2:
                    split_lo(2, 0, 512)

            def rotate_keys():
                dve.wait_ge(gates_copied, 1)
                dve.wait_ge(qi_rotated, 3)
                k4 = att[3][:, 0:TT * I_COLS].rearrange("p (t n) -> p t n", t=TT)[:, :, 0:I_HD]
                a, b = ki_rot[:, :, 0:I_HD], qi_b[:, 0:TT * I_HD].rearrange("p (t n) -> p t n", t=TT)
                V.tensor_tensor(a, k4, cos32, ALU.mult)
                then(V.tensor_tensor(b, k4, sin32, ALU.mult))
                h = I_HD // 2
                V.tensor_tensor(a[:, :, 0:h], a[:, :, 0:h], b[:, :, h:], ALU.subtract)
                then(V.tensor_tensor(a[:, :, h:], a[:, :, h:], b[:, :, 0:h], ALU.add))
                V.tensor_copy(ki_rot[:, :, I_HD:2 * I_HD], a).then_inc(ki_rotated, 1)

            def gate_in():
                dve.wait_ge(gates_turned, 1)
                then(V.tensor_scalar(rows[:, 0], att[0][0:A_HEADS, :], gate_b[:, 0:1], None, ALU.add))
                V.tensor_scalar(rows[:, 1], att[1][0:A_HEADS, :], gate_b[:, 1:2], None, ALU.add).then_inc(gates_read, 1)
                dve.wait_ge(gates_read, 1)
                V.scalar_tensor_tensor(rows[:, 2], rows[:, 1], -1.0, rows[:, 1], ALU.mult, ALU.max).then_inc(gate_abs, 1)

            def gate_scans():
                dve.wait_ge(gate_ln, 1)
                then(V.scalar_tensor_tensor(rows[:, 1], rows[:, 1], 0.0, rows[:, 3], ALU.min, ALU.subtract))
                then(V.memset(rows[:, 2], 1.0))
                then(V.tensor_tensor_scan(rows[:, 3], rows[:, 2], rows[:, 1], 0.0, ALU.mult, ALU.add))
                then(V.tensor_tensor(rows[:, 0], rows[:, 0], rows[:, 3], ALU.subtract))
                then(V.tensor_tensor_scan(maxrow, rows[:, 0], rows[:, 0], 0.0, ALU.max, ALU.max))
                V.tensor_tensor(rows[:, 1], rows[:, 3], maxrow, ALU.add).then_inc(gate_rows, 1)

            def sums(i, part):
                for u in range(8 * i + 4 * part, 8 * i + 4 * part + 4):
                    t, h = u // 8 + 1, u % 8
                    acc = score[:, off(t):off(t + 1)]
                    dve.wait_ge(relued, u + 1)
                    r = relu[:, u % 2, 0:(t + 1) * P]
                    if h == 0:
                        V.tensor_scalar(acc, r, wi8[:, t, 0:1], None, ALU.mult).then_inc(summed, 1)
                    else:
                        V.scalar_tensor_tensor(acc, r, wi8[:, t, h:h + 1], acc, ALU.mult, ALU.add).then_inc(summed, 1)
                    dve.wait_ge(summed, u + 1)
                if part == 1:
                    then(V.memset(score[0:64, off(t) + t * P + 64:off(t + 1)], NEG))

            def idx_lows():
                for n in range(4):
                    dve.wait_ge(idx_copied, n + 1)
                    hi, lo = (qiT[0][n], qiT[1][n]) if n < 3 else kiT
                    V.tensor_tensor(lo, att[n][:, :].rearrange("p (k n) -> p k n", k=2), hi.bitcast(F32),
                                    ALU.subtract).then_inc(q_split if n < 3 else ki_copied, 1)

            for i in range(4):
                p = KV[0] + i
                split_lo(p, 1, 512)
                if i == 0:
                    rotate_keys()
                    gate_in()
                else:
                    sums(i - 1, 0)
                split_lo(p + 1, 0, 512)
                if i:
                    sums(i - 1, 1)
                else:
                    idx_lows()
                if i == 1:
                    gate_scans()
                if i == 2:
                    dve.wait_ge(km_squared, 1)
                    then(V.tensor_reduce(kss, km_sq.rearrange("p (g n) -> p g n", n=M_HD), AX, ALU.add))
                    V.tensor_scalar(kss, kss, 1.0 / M_HD, EPS, ALU.mult, ALU.add).then_inc(km_var, 1)

            def held(cell=0):
                if steps.turn is not None:
                    V.memset(scratch[:, cell:cell + 1], 0.0)

            def top_round(t):
                row = score[:, off(t):off(t + 1)]
                held()
                then(V.max(top8, row))
                held()
                then(V.match_replace(row, top8, row, TAKEN))

            def make_mask(t):
                V.tensor_scalar(negmask[:, off(t):off(t + 1)], score[:, off(t):off(t + 1)], 0.5 * TAKEN, NEG,
                                ALU.is_gt, ALU.mult)

            def m_norms(h):
                dve.wait_ge(m_ssq, h + 1)
                V.tensor_scalar(m_var, att[0][:, 0:TT], 1.0 / M_HD, EPS, ALU.mult, ALU.add).then_inc(m_varred, 1)
                dve.wait_ge(m_scores, h * 2 + 1)
                V.reduce_max(mx[:, 0:2], att[1][:, :].rearrange("p (t n) -> p t n", t=2), AX)
                dve.wait_ge(m_scores, h * 2 + 2)
                V.reduce_max(mx[:, 2:4], att[2][:, :].rearrange("p (t n) -> p t n", t=2), AX)
                dve.wait_ge(m_rstd, h + 1)
                V.tensor_scalar(m_ps, m_rs, M_HD ** -0.5, None, ALU.mult)
                then(V.tensor_scalar(m_ns, m_rs, -(M_HD ** -0.5), None, ALU.mult))
                V.tensor_tensor(nb, mx, m_ns, ALU.mult).then_inc(m_bias, 1)

            def m_scale_p(h):
                dve.wait_ge(m_exp, h * 4 + 4)
                then(V.reciprocal(rinv, rsum))
                V.tensor_tensor(m_p, m_p, rinv.unsqueeze(2).to_broadcast([P, TT, MEM]), ALU.mult).then_inc(m_scaled, 1)

            def m_probs(h):
                for g in range(2):
                    dve.wait_ge(m_pturned, h * 2 + (g + 1))
                    V.tensor_copy(m_pT[:, :, g * 2 * P:(g + 1) * 2 * P],
                                  att[3 - 3 * g][:, :].rearrange("p (m n) -> p m n", m=MT)).then_inc(m_pcopied, 1)

            def m_rest(h):
                dve.wait_ge(bank_empty[3], h + (MS[2][3] + 1))
                for e in range(2):
                    dve.wait_ge(m_out, h * 2 + (e + 1))
                    V.tensor_tensor(yF[:, bass.ds(h * (2 * S) + e * S, S)], att[1 + e][:, :], m_zs[:, e, :],
                                    ALU.mult).then_inc(m_y, 1)

            def m_body(h, first, last):
                p = h + MS[0]
                split_lo(p, 1, 512)
                if first:
                    dve.wait_ge(gate_back, 1)
                    V.tensor_copy(gcols, att[0][:, 0:2 * TT * A_HEADS]
                                  .rearrange("p (k t h) -> p k h t", k=2, t=TT)).then_inc(gate_cols, 1)
                    dve.wait_ge(km_rstd, 1)
                    km3 = km_raw.rearrange("p (g n) -> p g n", n=M_HD)
                    V.tensor_tensor(km3, km3, krs.unsqueeze(2).to_broadcast([P, MT * M_HEADS, M_HD]),
                                    ALU.mult).then_inc(km_normed, 1)
                else:
                    m_norms(h - 1)
                tile = 1 if first else 2 if last else 3
                rounds = 16 if first else 10 if last else 8
                early = 8 if first else 2
                for r in range(early):
                    top_round(tile)
                if not first:
                    m_scale_p(h - 1)
                    m_probs(h - 1)
                split_lo(p + 1, 0, 384 if last else 512)
                if not first:
                    m_rest(h - 1)
                for r in range(rounds - early):
                    top_round(tile)

            turns_of(dve, steps, M_HEADS, M_PER, m_body)

            def make_masks():
                then(V.memset(negmask[:, 0:P], 0.0))
                for t in range(1, TT):
                    make_mask(t)
                then(V.memset(negmask[0:64, 64:P], NEG))

            def b_maxes(h):
                for t in range(TT):
                    dve.wait_ge(b_scores, h * 4 + (t + 1))
                    held(t)
                    V.tensor_tensor_reduce(out=score[:, off(t):off(t + 1)], in0=att[(t + 2) % 4][:, 0:(t + 1) * P],
                                           in1=negmask[:, off(t):off(t + 1)], scale=1.0, scalar=LOWEST,
                                           op0=ALU.add, op1=ALU.max, accum_out=mx[:, t:t + 1]).then_inc(b_masked, 1)
                dve.wait_ge(b_masked, h * 4 + 4)
                V.tensor_tensor(nb, mx, m_ns, ALU.mult).then_inc(b_bias, 1)

            def b_scale_p(h):
                dve.wait_ge(b_exp, h * 4 + 4)
                then(V.reciprocal(rinv, rsum))
                for t in range(TT):
                    s_t = score[:, off(t):off(t + 1)]
                    V.tensor_scalar(s_t, s_t, rinv[:, t:t + 1], None, ALU.mult).then_inc(b_scaled, 1)

            def b_probs(h):
                for t in range(TT):
                    dve.wait_ge(b_pturned, h * 4 + (t + 1))
                    V.tensor_copy(b_pT[:, 0:t + 1, t * P:(t + 1) * P],
                                  att[(t + 2) % 4][:, 0:(t + 1) * P].rearrange("p (s n) -> p s n", n=P))\
                        .then_inc(b_pcopied, 1)

            def b_finish(h):
                dve.wait_ge(b_out, h + 1)
                dve.wait_ge(bank_empty[0], h * 2 + (BS[2][0] + 2))
                V.tensor_tensor(yF[:, bass.ds(h * S, S)], att[2][:, :], b_zs, ALU.mult).then_inc(b_y, 1)

            def b_rotary(h):
                dve.wait_ge(b_squared, h + 1)
                then(V.tensor_reduce(b_var, b_sq.rearrange("p (g n) -> p g n", n=P), AX, ALU.add))
                V.tensor_scalar(b_var, b_var, 1.0 / B_HD, EPS, ALU.mult, ALU.add).then_inc(b_varred, 1)
                for tab, dst in ((0, b_rc), (1, b_rs)):
                    ins = V.tensor_tensor(dst.rearrange("p (t n) -> p t n", t=TT), b_raw[:, :, 0:2 * P],
                                          tabs[:, tab], ALU.mult)
                then(ins)
                then(join(b_rc, b_rs, 2 * TT))
                dve.wait_ge(b_rstded, h + 1)
                r2 = b_rstd.rearrange("p (t c) -> p t c", c=2)
                keys = b_rc.rearrange("p (t c n) -> p t c n", t=TT, c=2)[:, :, 1]
                V.tensor_tensor(keys, keys, r2[:, :, 1:2].to_broadcast([P, TT, P]), ALU.mult).then_inc(b_rotated, 1)
                V.tensor_scalar(m_ps, r2[:, :, 0], B_HD ** -0.5, None, ALU.mult)
                then(V.tensor_scalar(m_ns, r2[:, :, 0], -(B_HD ** -0.5), None, ALU.mult))

            def b_body(h, first, last):
                p = h * 2 + BS[0]
                split_lo(p, 1, 384)
                if first:
                    m_norms(M_HEADS - 1)
                else:
                    b_maxes(h - 1)
                    b_scale_p(h - 1)
                if first:
                    m_scale_p(M_HEADS - 1)
                    m_probs(M_HEADS - 1)
                split_lo(p + 1, 0, 384)
                if first:
                    m_rest(M_HEADS - 1)
                    for r in range(4):
                        top_round(2)
                else:
                    b_probs(h - 1)
                split_lo(p + 1, 1, 384)
                if first:
                    split_y(yF, 1)
                else:
                    b_finish(h - 1)
                if first:
                    dve.wait_ge(tabs_ready, 8)
                b_rotary(h)
                split_lo(p + 2, 0, 512 if last else 384)
                dve.wait_ge(b_turned, h * 2 + 2)
                V.tensor_copy(b_kT, att[1][:, :]).then_inc(b_kcopied, 1)
                dve.wait_ge(bank_empty[1], h * 2 + (BS[2][1] + 2))
                dve.wait_ge(proj_done[2], h * 2 + (BS[2][2] + 2))
                V.tensor_tensor(merged[:, bass.ds(h * S, S)], banks[2][:, :], sig[:, 0], ALU.mult)\
                    .then_inc(bank_empty[2], 1)
                if first:
                    for r in range(2):
                        top_round(2)
                    make_masks()

            turns_of(dve, steps, B_HEADS, B_PER, b_body)

            def a_conv_all(h):
                for b in range(4):
                    dve.wait_ge(proj_done[b], h * 3 + (AS[2][b] + 1))
                    if b >= 2:
                        dve.wait_ge(a_qk, h * 4 + (b - 1))
                    u, acc = banks[b], a_conv[:, b % 2, :]
                    then(V.tensor_scalar(acc, u[:, :], hcw[:, 3, b:b + 1], hcw[:, 4, b:b + 1], ALU.mult, ALU.add))
                    for lag in range(1, CONV):
                        ins = V.scalar_tensor_tensor(acc[:, lag:], u[:, 0:S - lag],
                                                     hcw[:, CONV - 1 - lag, b:b + 1], acc[:, lag:],
                                                     ALU.mult, ALU.add)
                        if lag < CONV - 1:
                            then(ins)
                    ins.then_inc(bank_empty[b], 1)

            def a_load_params(h, first):
                if not first:
                    dve.wait_ge(a_y, h * 2)
                cw = cols[:, 0:80].rearrange("p (j c e) -> p j c e", j=5, c=2)
                V.tensor_copy(hcw.rearrange("p j (c e) -> p j c e", c=2), cw[:, :, :, bass.ds(h * 2, 2)])
                V.tensor_copy(hcol, gcols.rearrange("p k h t -> p k (h t)")[:, :, bass.ds(h * TT, TT)])
                V.tensor_copy(pick[:, 0, :], pick.rearrange("p h n -> p (h n)")[:, bass.ds(h * P, P)])
                V.tensor_copy(hg, cols[:, bass.ds(h * 2 + 80, 2)]).then_inc(a_params, 1)
                dve.wait_ge(a_params, h + 1)

            def a_denominators(h):
                dve.wait_ge(a_num, h * 4 + 4)
                for t in range(TT):
                    ins = V.tensor_scalar(a_den[:, t:t + 1], att[t][:, A_HD:A_HD + 1], -1.0, hcol[:, 1, t:t + 1],
                                          ALU.mult, ALU.max)
                then(ins)
                for t in range(TT):
                    ins = V.tensor_tensor(a_den[:, t:t + 1], att[t][:, A_HD:A_HD + 1], a_den[:, t:t + 1], ALU.max)
                then(ins)
                V.reciprocal(a_ri, a_den).then_inc(a_rinv, 1)
                dve.wait_ge(a_ssq, h + 1)
                V.tensor_scalar(a_ss, a_ss, 1.0 / A_HD, EPS, ALU.mult, ALU.add).then_inc(a_var, 1)
                dve.wait_ge(a_rstd, h + 1)
                V.tensor_tensor(a_s, a_ri, a_den, ALU.mult).then_inc(a_scale, 1)

            def a_finish(h):
                dve.wait_ge(a_ozd, h + 1)
                for e in range(2):
                    dve.wait_ge(a_turned, h * 2 + (e + 1))
                    V.scalar_tensor_tensor(yF[:, bass.ds(h * (2 * S) + e * S, S)], att[e][:, :], hg[:, e:e + 1],
                                           a_oz[:, e, :], ALU.mult, ALU.mult).then_inc(a_y, 1)

            def a_body(h, first, last):
                p = h * 3 + AS[0]
                split_lo(p, 1, 512)
                if first:
                    b_maxes(B_HEADS - 1)
                    b_scale_p(B_HEADS - 1)
                    b_probs(B_HEADS - 1)
                    split_lo(p + 1, 0, 512)
                    b_finish(B_HEADS - 1)
                    dve.wait_ge(em_done, 1)
                else:
                    a_denominators(h - 1)
                    split_lo(p + 1, 0, 512)
                    a_finish(h - 1)
                a_load_params(h, first)
                a_conv_all(h)
                split_lo(p + 1, 1, 512)
                dve.wait_ge(a_spread, h + 1)
                V.tensor_tensor(a_md, att[0][:, :].rearrange("p (t n) -> p t n", t=TT),
                                causal[:, :].unsqueeze(1).to_broadcast([P, TT, P]), ALU.add).then_inc(a_md_done, 1)
                split_lo(p + 2, 0, A_HD)
                dve.wait_ge(a_wdone, h + 1)
                for s in range(TT):
                    dve.wait_ge(a_st, h * 4 + min(s + 1 + s // 2, 4))
                    bank, c = ((1, 0), (2, 0), (3, 0), (3, 2 * P))[s]
                    n = S - s * P
                    V.scalar_tensor_tensor(a_at[:, st_off(s):st_off(s) + n], att[bank][:, c:c + n], A_HD ** -0.5,
                                           a_w[:, st_off(s):st_off(s) + n], ALU.mult, ALU.mult).then_inc(a_atd, 1)
                split_lo(p + 2, 1, A_HD)
                if first:
                    split_y(yF, 2)
                    V.memset(a_v[:, :, A_HD:A_HD + 1], 1.0).then_inc(ones_set, 1)
                split_lo(p + 3, 0, 512)

            turns_of(dve, steps, A_HEADS, A_PER, a_body)

            def gb_merge(sec, j, n):
                for b in range(2):
                    dve.wait_ge(bank_empty[b], j + (sec[2][b] + 1))
                    dve.wait_ge(proj_done[2 + b], j + (sec[2][2 + b] + 1))
                    V.tensor_tensor(sig[:, b], banks[2 + b][:, :], sig[:, b], ALU.mult).then_inc(bank_empty[2 + b], 1)
                    dve.wait_ge(bank_empty[2 + b], j + (sec[2][2 + b] + 1))
                    m = merged[:, bass.ds(j * (2 * S) + b * S, S)]
                    V.tensor_tensor(m, m, sig[:, b], ALU.add).then_inc(g_merged, 1)

            split_lo(GB[0], 1, 512)
            a_denominators(A_HEADS - 1)
            split_lo(GB[0] + 1, 0, 512)
            a_finish(A_HEADS - 1)
            gb_merge(GB, 0, 0)

            def gb_body(sec, j, n, between=None):
                split_lo(j + sec[0], 1, 512)
                split_lo(j + (sec[0] + 1), 0, 512)
                if between:
                    between()
                gb_merge(sec, j, n)

            with dve.Fori(1, 3) as j:
                gb_body(GB, j, j)
            gb_body(GB, 3, 3, lambda: split_y(yF, 3))
            with dve.Fori(0, 3) as j:
                gb_body(GA, j, j + 4)
            gb_body(GA, 3, 7, lambda: split_y(merged, 4, range(KT - 2)))
            split_y(merged, 4, range(KT - 2, KT))
            split_lo(OUT[0], 1, 512)
            split_lo(OUT[0] + 1, 0, 512)
            dve.wait_ge(x_again, 16 * TT)
            for c in range(2):
                for t in range(TT):
                    dve.wait_ge(proj_done[t], OUT[2][t] + c + 1)
                    o = x_in[:, t, c * 512:(c + 1) * 512]
                    V.tensor_tensor(o, banks[t][:, :], o, ALU.add).then_inc(bank_empty[t], 1)
                if c == 0:
                    split_lo(OUT[0] + 1, 1, 512)

        @block.gpsimd
        def _(pool):
            G = nc.gpsimd
            steps = Steps(pool, pool_step)
            G.memset(ident[:, :], 0.0)
            G.memset(causal[:, :], 0.0)
            steps.then(G.memset(pick[:, :, :], 0.0))
            G.affine_select(out=ident[:, :], in_=ident[:, :], compare_op=ALU.not_equal, fill=1.0, base=0,
                            pattern=[[-1, P]], channel_multiplier=1).then_inc(consts, 1)
            G.affine_select(out=causal[:, :], in_=causal[:, :], compare_op=ALU.is_ge, fill=NEG, base=0,
                            pattern=[[1, P]], channel_multiplier=-1).then_inc(consts, 1)
            G.affine_select(out=pick[:, :, :], in_=pick[:, :, :], compare_op=ALU.not_equal, fill=-1.0, base=0,
                            pattern=[[-1, A_HEADS], [0, P]], channel_multiplier=1).then_inc(consts, 1)
            pool.wait_ge(consts, 4)

            def x_power(i):
                pool.wait_ge(x_var, i + 1)
                G.tensor_tensor(xrs[:, i:i + 1], xss[:, i:i + 1], minus_half[:, 0:1], ALU.pow).then_inc(x_rstd, 1)

            for i in range(TT + MT):
                x_power(i)
                if i >= TT:
                    if i == TT:
                        pool.wait_ge(small_landed, 16 * 4)
                    pool.wait_ge(x_turned, 2 * (i - 1))
                    pool.wait_ge(x_rstd, i + 1)
                    row = x_sc[:, i % 2, :]
                    steps.then(G.tensor_tensor(row, mem_in[:, i - TT], xrs[:, i:i + 1].to_broadcast([P, D]), ALU.mult))
                    G.tensor_tensor(row, row, memg_row, ALU.mult).then_inc(x_scaled, 1)
            pool.wait_ge(sincos, 2)
            pool.wait_ge(small_landed, 16 * 4)
            for tab, src in ((0, cosd), (1, sind)):
                for c in range(2):
                    for half in range(2):
                        g = gain_rows[:, c * P + half * 64:c * P + half * 64 + 64]
                        G.tensor_tensor(tabs[:, tab, :, c * P + half * 64:c * P + half * 64 + 64], src,
                                        g.unsqueeze(1).to_broadcast([P, TT, 64]), ALU.mult).then_inc(tabs_ready, 1)
            for b in range(4):
                pool.wait_ge(bank_empty[b], KV[2][b] + 1)
            pool.wait_ge(idx_turned, 4)
            G.tensor_tensor(km_sq, km_raw, km_raw, ALU.mult).then_inc(km_squared, 1)
            pool.wait_ge(km_var, 1)
            G.tensor_tensor(krs, kss, minus_half[:, 0:8], ALU.pow).then_inc(km_rstd, 1)
            with pool.Fori(0, M_HEADS) as h:
                pool.wait_ge(bank_empty[1], h + (MS[2][1] + 1))
                G.tensor_tensor(m_sq[:, 0, :], m_sq[:, 0, :], m_sq[:, 1, :], ALU.add).then_inc(m_added, 1)
                pool.wait_ge(m_varred, h + 1)
                G.tensor_tensor(m_rs, m_var, minus_half[:, 0:TT], ALU.pow).then_inc(m_rstd, 1)
                G.tensor_copy(m_vh, vm[:, :, bass.ds(h * M_HD, M_HD)]).then_inc(m_vcopied, 1)
            with pool.Fori(0, B_HEADS) as h:
                pool.wait_ge(bank_empty[3], h + (BS[2][3] + 1))
                qk = b_raw[:, :, 0:2 * P]
                G.tensor_tensor(b_sq.rearrange("p (t n) -> p t n", t=TT), qk, qk, ALU.mult).then_inc(b_squared, 1)
                pool.wait_ge(b_varred, h + 1)
                G.tensor_tensor(b_rstd, b_var, minus_half[:, 0:8], ALU.pow).then_inc(b_rstded, 1)

            def a_powers(h):
                pool.wait_ge(a_var, h + 1)
                G.tensor_tensor(a_den, a_ss, minus_half[:, 0:TT], ALU.pow).then_inc(a_rstd, 1)

            def a_gate(h):
                pool.wait_ge(bank_empty[3], h * 3 + (AS[2][3] + 2))
                G.tensor_tensor(a_oz, a_o, a_oz, ALU.mult).then_inc(a_ozd, 1)

            a_gate(0)
            with pool.Fori(1, A_HEADS) as h:
                a_powers(h - 1)
                a_gate(h)
            a_powers(A_HEADS - 1)


M_PER, B_PER, A_PER = 18, 5, 14

_INS = ['x', 'mem', 'positions', 'norm_g', 'mem_norm_g', 'w_in', 'conv_w', 'conv_b', 'mlstm_gate_b',
        'mlstm_norm_g', 'dsa_q_norm_g', 'dsa_k_norm_g', 'mem_q_norm_g', 'mem_k_norm_g', 'w_mem_kv',
        'w_branch', 'w_out']


def kernel(**inputs):
    import concourse.bacc as bacc
    from concourse.bass_utils import run_bass_kernel_spmd as run

    nc = bacc.Bacc("TRN2", target_bir_lowering=False, num_devices=1)
    arrays, args = {}, []
    for name in _INS:
        arrays[name] = np.ascontiguousarray(inputs[name])
    half = B_HD // 2
    arrays['inv_freq'] = (ROPE_THETA ** (-np.arange(half) / half)).astype(np.float32)[None, :]
    for name, a in arrays.items():
        args.append(nc.dram_tensor(name + "_in", a.shape, mybir.dt.from_np(a.dtype), kind="ExternalInput").ap())
    out = nc.dram_tensor("out", (1, S, D), F32, kind="ExternalOutput").ap()
    hybrid_block(nc, *args, out)
    r = run(nc, [{name + "_in": a for name, a in arrays.items()}], core_ids=[0])
    return r.results[0]["out"]
```
